# Optimizing a Trainium2 kernel written in Bass

```python
import math
import jax, jax.numpy as jnp
from jax import lax
import numpy as np

D_MODEL = 1024
BATCH = 1
SEQ = 512
DEPTH = 2

N_HEADS = 16
N_KV_HEADS = 4
HEAD_DIM = 64
GROUP = N_HEADS // N_KV_HEADS
ATTN_WIDTH = N_HEADS * HEAD_DIM
KV_WIDTH = N_KV_HEADS * HEAD_DIM
WINDOW = 128
BLOCK = 128
ATTN_IN = 2 * ATTN_WIDTH + 2 * KV_WIDTH
POOL_WIDTH = D_MODEL
POOL_WINDOWS = (2, 4, 8, 16)
N_POOL_GROUPS = len(POOL_WINDOWS)
POOL_GC = POOL_WIDTH // N_POOL_GROUPS
POOL_IN = 2 * POOL_WIDTH
N_MIXERS = 2
N_A = (DEPTH + 1) // 2
N_B = DEPTH // 2
EPS = 1e-6


def rmsnorm(x, g):
    xf = x.astype(jnp.float32)
    y = xf * lax.rsqrt(jnp.mean(xf * xf, axis=-1, keepdims=True) + EPS)
    return (y * g.astype(jnp.float32)).astype(x.dtype)

def swa_with_sinks(q, k, v, sinks):
    B, S = q.shape[0], q.shape[1]
    nb = S // BLOCK
    qb = q.reshape(B, nb, BLOCK, N_KV_HEADS, GROUP, HEAD_DIM)
    def band(t):
        tb = t.reshape(B, nb, BLOCK, N_KV_HEADS, HEAD_DIM)
        prev = jnp.pad(tb, ((0, 0), (1, 0), (0, 0), (0, 0), (0, 0)))[:, :-1]
        return jnp.concatenate([prev, tb], axis=2)
    kc, vc = band(k), band(v)
    s = jnp.einsum('bnqhgd,bnkhd->bnhgqk', qb, kc).astype(jnp.float32)
    s = s * (1.0 / math.sqrt(HEAD_DIM))
    qi = jnp.arange(BLOCK)[:, None]
    kj = jnp.arange(2 * BLOCK)[None, :]
    diff = qi + BLOCK - kj
    in_band = (diff >= 0) & (diff < WINDOW)
    not_pad = (jnp.arange(nb)[:, None, None] > 0) | (kj[None] >= BLOCK)
    valid = in_band[None] & not_pad
    s = jnp.where(valid[None, :, None, None], s, -jnp.inf)
    sink = sinks.astype(jnp.float32).reshape(N_KV_HEADS, GROUP)[:, :, None, None]
    m = jnp.maximum(jnp.max(s, axis=-1, keepdims=True), sink)
    p = jnp.exp(s - m)
    denom = jnp.sum(p, axis=-1, keepdims=True) + jnp.exp(sink - m)
    p = (p / denom).astype(v.dtype)
    o = jnp.einsum('bnhgqk,bnkhd->bnqhgd', p, vc)
    return o.reshape(B, S, ATTN_WIDTH)

def attn_layer(h, w_in, sinks, w_out):
    B, S, _ = h.shape
    proj = h @ w_in
    q, k, v, z = jnp.split(proj, [ATTN_WIDTH, ATTN_WIDTH + KV_WIDTH, ATTN_WIDTH + 2 * KV_WIDTH], axis=-1)
    q = q.reshape(B, S, N_KV_HEADS, GROUP, HEAD_DIM)
    k = k.reshape(B, S, N_KV_HEADS, HEAD_DIM)
    v = v.reshape(B, S, N_KV_HEADS, HEAD_DIM)
    o = swa_with_sinks(q, k, v, sinks)
    return (o * jax.nn.silu(z)) @ w_out

def multiscale_pool(u):
    B, S, _ = u.shape
    uf = u.astype(jnp.float32).reshape(B, S, N_POOL_GROUPS, POOL_GC)
    cs = jnp.pad(jnp.cumsum(uf, axis=1), ((0, 0), (1, 0), (0, 0), (0, 0)))
    outs = []
    for gi, w in enumerate(POOL_WINDOWS):
        c = cs[:, :, gi]
        lower = jnp.pad(c[:, :S + 1 - w], ((0, 0), (w - 1, 0), (0, 0)))
        count = jnp.minimum(jnp.arange(1, S + 1), w).astype(jnp.float32)[None, :, None]
        outs.append((c[:, 1:] - lower) / count - uf[:, :, gi])
    return jnp.stack(outs, axis=2).astype(u.dtype)

def pool_layer(h, w_in, w_mix, scale, w_out):
    B, S, _ = h.shape
    u, z = jnp.split(h @ w_in, [POOL_WIDTH], axis=-1)
    p = multiscale_pool(u)
    m = jnp.einsum('bsgc,gcd->bsgd', p, w_mix).reshape(B, S, POOL_WIDTH) * scale
    return (m * jax.nn.silu(z)) @ w_out

def first_inputs(seed: int = 0) -> dict:
    key = jax.random.key(seed)
    ks = jax.random.split(key, 12)
    out_scale = 1.0 / math.sqrt(2.0 * DEPTH)
    x = jax.random.normal(ks[0], (BATCH, SEQ, D_MODEL), jnp.float32)
    norm_g = 1.0 + 0.05 * jax.random.normal(ks[1], (DEPTH, D_MODEL), jnp.float32)
    attn_w_in = jax.random.normal(ks[2], (N_A, D_MODEL, ATTN_IN), jnp.float32) * D_MODEL ** -0.5
    attn_sinks = 0.5 * jax.random.normal(ks[3], (N_A, N_HEADS), jnp.float32)
    attn_w_out = jax.random.normal(ks[4], (N_A, ATTN_WIDTH, D_MODEL), jnp.float32) * ATTN_WIDTH ** -0.5 * out_scale
    pool_w_in = jax.random.normal(ks[5], (N_B, D_MODEL, POOL_IN), jnp.float32) * D_MODEL ** -0.5
    pool_w_mix = jax.random.normal(ks[6], (N_B, N_POOL_GROUPS, POOL_GC, POOL_GC), jnp.float32) * POOL_GC ** -0.5
    pool_scale = 1.0 + 0.1 * jax.random.normal(ks[7], (N_B, POOL_WIDTH), jnp.float32)
    pool_w_out = jax.random.normal(ks[8], (N_B, POOL_WIDTH, D_MODEL), jnp.float32) * POOL_WIDTH ** -0.5 * out_scale
    final_g = 1.0 + 0.05 * jax.random.normal(ks[9], (D_MODEL,), jnp.float32)
    return {"x": x, "norm_g": norm_g, "attn_w_in": attn_w_in, "attn_sinks": attn_sinks,
            "attn_w_out": attn_w_out, "pool_w_in": pool_w_in, "pool_w_mix": pool_w_mix,
            "pool_scale": pool_scale, "pool_w_out": pool_w_out, "final_g": final_g}

def first_block(x, norm_g, attn_w_in, attn_sinks, attn_w_out, pool_w_in, pool_w_mix,
              pool_scale, pool_w_out, final_g):
    for i in range(DEPTH):
        h = rmsnorm(x, norm_g[i])
        j = i // N_MIXERS
        if i % N_MIXERS == 0:
            y = attn_layer(h, attn_w_in[j], attn_sinks[j], attn_w_out[j])
        else:
            y = pool_layer(h, pool_w_in[j], pool_w_mix[j], pool_scale[j], pool_w_out[j])
        x = x + y.astype(x.dtype)
    return rmsnorm(x, final_g)


CHUNK = 64
Q_BLOCK = 128
ROPE_THETA = 10000.0

SB_HEAD_DIM = 64
SB_WIDTH = D_MODEL // 2
SB_HEADS = SB_WIDTH // SB_HEAD_DIM
DF_HEAD_DIM = 64
DF_WIDTH = D_MODEL - SB_WIDTH
DF_HEADS = DF_WIDTH // (2 * DF_HEAD_DIM)
MIX_WIDTH = SB_WIDTH + DF_WIDTH
PROJ_WIDTH = 3 * SB_WIDTH + 3 * DF_WIDTH
D_FF = 4 * D_MODEL


def rmsnorm_2(x, g):
    xf = x.astype(jnp.float32)
    y = xf * lax.rsqrt(jnp.mean(xf * xf, axis=-1, keepdims=True) + EPS) * g.astype(jnp.float32)
    return y.astype(x.dtype)

def rope(x, pos):
    d = x.shape[-1]
    inv = 1.0 / (ROPE_THETA ** (jnp.arange(0, d, 2, dtype=jnp.float32) / d))
    ang = pos.astype(jnp.float32)[:, None] * inv[None, :]
    ang = jnp.concatenate([ang, ang], axis=-1)
    shape = (1, x.shape[1]) + (1,) * (x.ndim - 3) + (d,)
    cos = jnp.cos(ang).reshape(shape)
    sin = jnp.sin(ang).reshape(shape)
    xf = x.astype(jnp.float32)
    x1, x2 = xf[..., : d // 2], xf[..., d // 2:]
    rot = jnp.concatenate([-x2, x1], axis=-1)
    return (xf * cos + rot * sin).astype(x.dtype)

def stick_breaking_attention(q, k, v):
    B, S, H, d = q.shape
    nb = S // Q_BLOCK
    scale = d ** -0.5
    kh = k.transpose(0, 2, 1, 3)
    vh = v.transpose(0, 2, 1, 3)
    qb = q.transpose(0, 2, 1, 3).reshape(B, H, nb, Q_BLOCK, d).transpose(2, 0, 1, 3, 4)
    kpos = jnp.arange(S)
    qpos = kpos.reshape(nb, Q_BLOCK)

    def block(args):
        qblk, qp = args
        z = jnp.einsum('bhqd,bhkd->bhqk', qblk, kh).astype(jnp.float32) * scale
        strict = kpos[None, :] < qp[:, None]
        log_beta = jax.nn.log_sigmoid(z)
        log_keep = jnp.where(strict, jax.nn.log_sigmoid(-z), 0.0)
        between = lax.cumsum(log_keep, axis=log_keep.ndim - 1, reverse=True) - log_keep
        w = jnp.where(strict, jnp.exp(log_beta + between), 0.0)
        return jnp.einsum('bhqk,bhkd->bhqd', w.astype(vh.dtype), vh)

    out = lax.map(block, (qb, qpos))
    return out.transpose(1, 0, 3, 2, 4).reshape(B, S, H * d)

def differential_attention(q, k, v, lam):
    B, S, H, _, d = q.shape
    dv = v.shape[-1]
    nb = S // Q_BLOCK
    scale = d ** -0.5
    kh = k.transpose(0, 2, 3, 1, 4)
    vh = v.transpose(0, 2, 1, 3)
    qb = q.transpose(0, 2, 3, 1, 4).reshape(B, H, 2, nb, Q_BLOCK, d).transpose(3, 0, 1, 2, 4, 5)
    kchunk = jnp.arange(S) // CHUNK
    qpos = jnp.arange(S).reshape(nb, Q_BLOCK)
    neg = jnp.finfo(jnp.float32).min

    def block(args):
        qblk, qp = args
        s = jnp.einsum('bhmqd,bhmkd->bhmqk', qblk, kh).astype(jnp.float32) * scale
        allowed = kchunk[None, :] <= (qp // CHUNK)[:, None]
        p = jax.nn.softmax(jnp.where(allowed, s, neg), axis=-1)
        attn = p[:, :, 0] - lam * p[:, :, 1]
        return jnp.einsum('bhqk,bhkd->bhqd', attn.astype(vh.dtype), vh)

    out = lax.map(block, (qb, qpos))
    return out.transpose(1, 0, 3, 2, 4).reshape(B, S, H, dv)

def second_inputs(seed: int = 0) -> dict:
    key = jax.random.key(seed)
    ks = jax.random.split(key, 14)
    f32 = jnp.float32
    out_scale = (2.0 * DEPTH) ** -0.5
    x = jax.random.normal(ks[0], (BATCH, SEQ, D_MODEL), f32)
    w_in = jax.random.normal(ks[1], (DEPTH, D_MODEL, PROJ_WIDTH), f32) * D_MODEL ** -0.5
    w_o = jax.random.normal(ks[2], (DEPTH, MIX_WIDTH, D_MODEL), f32) * (MIX_WIDTH ** -0.5) * out_scale
    attn_norm = 1.0 + 0.02 * jax.random.normal(ks[3], (DEPTH, D_MODEL), f32)
    subln_norm = 1.0 + 0.02 * jax.random.normal(ks[4], (DEPTH, 2 * DF_HEAD_DIM), f32)
    lam_q1 = 0.1 * jax.random.normal(ks[5], (DEPTH, DF_HEAD_DIM), f32)
    lam_k1 = 0.1 * jax.random.normal(ks[6], (DEPTH, DF_HEAD_DIM), f32)
    lam_q2 = 0.1 * jax.random.normal(ks[7], (DEPTH, DF_HEAD_DIM), f32)
    lam_k2 = 0.1 * jax.random.normal(ks[8], (DEPTH, DF_HEAD_DIM), f32)
    mlp_norm = 1.0 + 0.02 * jax.random.normal(ks[9], (DEPTH, D_MODEL), f32)
    w_ff1 = jax.random.normal(ks[10], (DEPTH, D_MODEL, D_FF), f32) * D_MODEL ** -0.5
    w_ff2 = jax.random.normal(ks[11], (DEPTH, D_FF, D_MODEL), f32) * (D_FF ** -0.5) * out_scale
    final_norm = 1.0 + 0.02 * jax.random.normal(ks[12], (D_MODEL,), f32)
    return {"x": x, "w_in": w_in, "w_o": w_o, "attn_norm": attn_norm,
            "subln_norm": subln_norm, "lam_q1": lam_q1, "lam_k1": lam_k1,
            "lam_q2": lam_q2, "lam_k2": lam_k2, "mlp_norm": mlp_norm,
            "w_ff1": w_ff1, "w_ff2": w_ff2, "final_norm": final_norm}

def second_block(x, w_in, w_o, attn_norm, subln_norm, lam_q1, lam_k1, lam_q2, lam_k2,
              mlp_norm, w_ff1, w_ff2, final_norm):
    B, S, _ = x.shape
    pos = jnp.arange(S)
    splits = np.cumsum([SB_WIDTH, SB_WIDTH, SB_WIDTH, DF_WIDTH, DF_WIDTH]).tolist()
    for l in range(DEPTH):
        h = rmsnorm_2(x, attn_norm[l])
        proj = jnp.einsum('bsd,de->bse', h, w_in[l])
        sb_q, sb_k, sb_v, df_q, df_k, df_v = jnp.split(proj, splits, axis=-1)

        sb_out = stick_breaking_attention(
            sb_q.reshape(B, S, SB_HEADS, SB_HEAD_DIM),
            sb_k.reshape(B, S, SB_HEADS, SB_HEAD_DIM),
            sb_v.reshape(B, S, SB_HEADS, SB_HEAD_DIM))

        lambda_init = 0.8 - 0.6 * math.exp(-0.3 * l)
        lam = (jnp.exp(jnp.sum(lam_q1[l].astype(jnp.float32) * lam_k1[l].astype(jnp.float32)))
               - jnp.exp(jnp.sum(lam_q2[l].astype(jnp.float32) * lam_k2[l].astype(jnp.float32)))
               + lambda_init)
        dq = rope(df_q.reshape(B, S, DF_HEADS, 2, DF_HEAD_DIM), pos)
        dk = rope(df_k.reshape(B, S, DF_HEADS, 2, DF_HEAD_DIM), pos)
        dvv = df_v.reshape(B, S, DF_HEADS, 2 * DF_HEAD_DIM)
        df_heads = differential_attention(dq, dk, dvv, lam)
        df_out = (rmsnorm_2(df_heads, subln_norm[l]) * (1.0 - lambda_init)).reshape(B, S, DF_WIDTH)

        mixed = jnp.concatenate([sb_out, df_out.astype(sb_out.dtype)], axis=-1)
        x = x + jnp.einsum('bse,ed->bsd', mixed, w_o[l])

        h = rmsnorm_2(x, mlp_norm[l])
        u = jnp.square(jax.nn.relu(jnp.einsum('bsd,df->bsf', h, w_ff1[l])))
        x = x + jnp.einsum('bsf,fd->bsd', u, w_ff2[l])
    return rmsnorm_2(x, final_norm)


def setup_inputs(seed=0):
    out = dict(first_inputs(seed))
    for name, value in second_inputs(seed + 1).items():
        if name != "x":
            out[name + "_2"] = value
    return out


def reference(
    x, norm_g, attn_w_in, attn_sinks, attn_w_out, pool_w_in, pool_w_mix, pool_scale, pool_w_out,
    final_g, w_in_2, w_o_2, attn_norm_2, subln_norm_2, lam_q1_2, lam_k1_2, lam_q2_2, lam_k2_2,
    mlp_norm_2, w_ff1_2, w_ff2_2, final_norm_2,
):
    x = first_block(
        x, norm_g, attn_w_in, attn_sinks, attn_w_out, pool_w_in, pool_w_mix, pool_scale,
        pool_w_out, final_g,
    )
    return second_block(
        x, w_in_2, w_o_2, attn_norm_2, subln_norm_2, lam_q1_2, lam_k1_2, lam_q2_2, lam_k2_2,
        mlp_norm_2, w_ff1_2, w_ff2_2, final_norm_2,
    )


_drawn_inputs = setup_inputs


def setup_inputs(seed=0):
    import zlib

    import numpy as np

    out = dict(_drawn_inputs(seed))
    spreads = {}
    factors = {'attn_sinks': 8.0,
     'attn_norm_2': 4.056,
     'subln_norm_2': 7.766,
     'lam_q2_2': 8.0,
     'mlp_norm_2': 3.682,
     'final_norm_2': 2.845}
    for name, (base, spread) in spreads.items():
        noise = np.random.default_rng([zlib.crc32(name.encode()), seed]).standard_normal(out[name].shape)
        drawn = base * np.exp(spread * noise) if base else spread * noise
        out[name] = __import__('jax').numpy.asarray(drawn.astype(out[name].dtype))
    for name, factor in factors.items():
        out[name] = (out[name] * factor).astype(out[name].dtype)
    return out
```

```python
import math
from contextlib import ExitStack

import concourse.bass as bass
from concourse import mybir

F32 = mybir.dt.float32
F32R = mybir.dt.float32r
BF16 = mybir.dt.bfloat16
ALU = mybir.AluOpType
ACT = mybir.ActivationFunctionType

P = 128
EPS = 1e-6
NEG = -1e30


class Tally:

    def __init__(self):
        self.n = {}

    def take(self, name, k=1):
        before = self.n.get(name, 0)
        self.n[name] = before + k
        return before


def make_plan(depth):
    tally = Tally()

    def slot(kind, j, results, **more):
        return dict(kind=kind, j=j, t=tally.take("t"), r=tally.take("r", results), n=results, steps=[], **more)

    def use(**step):
        k = step["op"]
        if k in ("swa_qk", "df_qk", "sb_qk", "stat"):
            step["z"] = tally.take("z")
            step["zd"] = tally.take("z_done", 3 if k == "sb_qk" else 1)
        if k in ("swa_t", "t", "df_f"):
            step["p0"] = tally.take("p0", 2 if k == "t" else 1)
        if k in ("swa_t", "t"):
            step["p1"] = tally.take("p1")
        if k == "swa_t" and step["h"] % 2 == 0 or k == "t" and (step["df"] or step["h"] % 2 == 0):
            step["o"] = tally.take("o")
        elif k in ("swa_t", "t"):
            step["o"] = tally.n["o"] - 1
        return step

    plan = {}
    tally.take("r", 8)
    attn = [slot("k", j, 1) for j in range(2)] + [slot("v", j, 2) for j in range(2)]
    attn += [slot("q", j, 1) for j in range(8)] + [slot("z", j, 1) for j in range(8)]
    attn += [slot("out", j, 1) for j in range(8)]
    plan["attn"] = attn
    attn[0]["steps"].append(use(op="stat"))
    for i in range(18):
        s = attn[6 + i // 2]
        if i < 16:
            s["steps"].append(use(op="swa_qk", h=i, half=i % 2))
        if i >= 2:
            s["steps"].append(use(op="swa_t", h=i - 2, half=i % 2))
    pool = [slot("pu", j, 1) for j in range(8)] + [slot("pz", j, 1) for j in range(8)]
    pool += [slot("mix", j, 4) for j in range(2)] + [slot("out", j, 1) for j in range(8)]
    plan["pool"] = pool
    pool[0]["steps"].append(use(op="stat"))
    plan["mid_stat"] = use(op="stat")
    for l in range(depth):
        s = []
        for name in ("df", "df", "sb", "sb"):
            half = len(s) // 6 % 2
            s += [slot(name + "k", 2 * half + j, 1) for j in range(2)]
            s += [slot(name + "q", 2 * half + j, 1) for j in range(2)]
            s += [slot(name + "v", 2 * half + j, 2) for j in range(2)]
        s += [slot("wo", j, 2, second=j >= 4) for j in range(8)]
        plan["layer", l] = s
        s[0]["steps"].append(use(op="stat"))
        todo = {}
        for d in range(4):
            at = 6 * (1 + d // 2) + 2 * (d % 2)
            for m in range(2):
                todo.setdefault(at + m, []).append(dict(op="df_qk", h=d, m=m))
            todo.setdefault(at + 2, []).append(dict(op="t", h=d, df=True))
            todo.setdefault(at + 3, []).append(dict(op="df_f", h=d))
        for h in range(8):
            todo.setdefault(18 + h, []).append(dict(op="sb_qk", h=h))
            todo.setdefault(19 + h, []).append(dict(op="t", h=h, df=False))
            if h % 2:
                todo.setdefault(20 + h, []).append(dict(op="sb_o", h=h))
        order = ["sb_qk", "df_qk", "df_f", "t", "sb_o"]
        for k in sorted(todo):
            for step in sorted(todo[k], key=lambda x: order.index(x["op"])):
                s[k]["steps"].append(use(**step))
        for step in [st for x in s for st in x["steps"] if st["op"] == "sb_o"]:
            step["o"] = [st["o"] for x in s for st in x["steps"] if st["op"] == "t" and not st["df"] and st["h"] == step["h"]][0]
        plan["ff_stat", l] = use(op="stat")
        plan["ff", l] = (tally.take("t", 64), tally.take("r", 64))
    plan["last_stat"] = use(op="stat")
    plan["last_r"] = tally.take("r", 8)
    plan["tiles"] = tally.n["t"]
    return plan


def build(nc, x, norm_g, attn_w_in, attn_sinks, attn_w_out, pool_w_in, pool_w_mix, pool_scale,
          pool_w_out, final_g, w_in_2, w_o_2, attn_norm_2, subln_norm_2, lam_q1_2, lam_k1_2,
          lam_q2_2, lam_k2_2, mlp_norm_2, w_ff1_2, w_ff2_2, final_norm_2, rope_table, out):
    S, D = x.shape[1], x.shape[2]
    KT = D // P
    NB = S // P
    DEPTH = w_in_2.shape[0]
    FF = w_ff1_2.shape[2]
    BLOCKS = FF // D
    plan = make_plan(DEPTH)
    LAST_T = plan["tiles"]
    NS = S + NB
    POOL_W = (2, 4, 8, 16)
    PAD = max(POOL_W)
    ZOFF = {3: 0, 2: 512, 0: 896, 1: 1024}
    CHUNKS = [(0, 512, [3]), (512, 512, [2, 0]), (1024, 256, [1])]
    G_NORM, G_FINAL, G_SCALE, G_ATTN, G_MLP, G_LAST, G_SUB = 0, 16, 24, 32, 48, 64, 72
    GROWS = G_SUB + DEPTH

    with ExitStack() as ctx:
        def sb(name, shape, dt=F32, c=ctx):
            return c.enter_context(nc.sbuf_tensor(name, shape, dt))

        def sem(name):
            return ctx.enter_context(nc.semaphore(name))

        xT = sb("xT", [P, KT, S])
        XH, XL = sb("XH", [P, KT, S], F32R), sb("XL", [P, KT, S], F32R)
        MH, ML = sb("MH", [P, KT, S], F32R), sb("ML", [P, KT, S], F32R)
        raw = sb("raw", [P, 2, KT * 256])
        WH, WL = sb("WH", [P, 4, KT * P], F32R), sb("WL", [P, 4, KT * P], F32R)
        ident = sb("ident", [P, P])
        identb = sb("identb", [P, P], BF16)
        ones = sb("ones", [P, 1])
        mean_w = sb("mean_w", [P, P])
        mask_sw = sb("mask_sw", [P, 256])
        mask_sb = sb("mask_sb", [P, P], BF16)
        mask_df = sb("mask_df", [P, 512])
        inv_n = sb("inv_n", [P, PAD])
        grow = sb("grow", [GROWS, P])
        gain = sb("gain", [P, GROWS])
        sink = sb("sink", [P, 16])
        lamw = sb("lamw", [P, 64])
        lamd = sb("lamd", [P, 2 * DEPTH])
        lame = sb("lame", [P, 2 * DEPTH])
        neglam = sb("neglam", [P, DEPTH])
        sq = sb("sq", [P, 2, S])
        acc = sb("acc", [P, S])
        ms, rstd, nt = sb("ms", [P, NS]), sb("rstd", [P, NS]), sb("nt", [P, NS])
        small = sb("small", [P, 64])
        tb = sb("tb", [P, 2, S])
        lamv = tb[:, 0, 0:4 * DEPTH * 64].rearrange("p (v n) -> p v n", v=4)

        U = ctx.enter_context(nc.psum_tensor("U", [P, 2, 512], F32))
        Z = ctx.enter_context(nc.psum_tensor("Z", [P, 1536], F32))
        PP = ctx.enter_context(nc.psum_tensor("PP", [P, 2, 512], F32))
        O = ctx.enter_context(nc.psum_tensor("O", [P, 512], F32))

        a0 = ExitStack()
        xin = sb("xin", [P, NB, D], c=a0)
        oraw = xin[:].rearrange("p a (b s) -> p (a b) s", s=S)
        q0 = sb("q0", [P, 4, S], c=a0)
        kd = sb("kd", [P, 4, S], c=a0)
        v0 = sb("v0", [P, NB, 256], c=a0)
        pr = sb("pr", [P, 3, 896], c=a0)
        pt0 = sb("pt0", [P, 896], c=a0)
        a0.close()
        a1 = ExitStack()
        pad = sb("pad", [P, 6, PAD + S], c=a1)
        pf = sb("pf", [P, 2, S], c=a1)
        sz = sb("sz", [P, KT, S], c=a1)
        a1.close()
        a2 = ExitStack()
        keys, queries, values = (sb(n, [P, 4, S], c=a2) for n in ("keys", "queries", "values"))
        qk = {"dfk": keys, "dfq": queries, "dfv": values, "sbk": keys, "sbq": queries, "sbv": values}
        cs = sb("cs", [P, 2, S], c=a2)
        ea = sb("ea", [P, 3, 1280], c=a2)
        cc = sb("cc", [P, 1280], c=a2)
        pt = sb("pt", [P, 4, S], c=a2)
        a2.close()
        a3 = ExitStack()
        xf = sb("xf", [P, KT, S], c=a3)
        yrow = sb("yrow", [P, NB, D], c=a3)
        a3.close()

        in_landed, par_landed = sem("in_landed"), sem("par_landed")
        raw_landed = [sem("raw_landed0"), sem("raw_landed1")]
        hi_done, lo_done = sem("hi_done"), sem("lo_done")
        cs_landed, rope_shifted, rope_done = sem("cs_landed"), sem("rope_shifted"), sem("rope_done")
        psum_done, result_taken = sem("psum_done"), sem("result_taken")
        const_ready, const_f = sem("const_ready"), sem("const_f")
        gain_done, gain_ready = sem("gain_done"), sem("gain_ready")
        lam_dot, lam_exp = sem("lam_dot"), sem("lam_exp")
        xh_ready, xg_ready = sem("xh_ready"), sem("xg_ready")
        xt_ready = sem("xt_ready")
        sq_ready, acc_done = sem("sq_ready"), sem("acc_done")
        stat_y, sub_v, sub_y, dfw_ready = sem("stat_y"), sem("sub_v"), sem("sub_y"), sem("dfw_ready")
        z_done, z_free = sem("z_done"), sem("z_free")
        p0_done, p0_free = sem("p0_done"), sem("p0_free")
        p1_done, p1_free = sem("p1_done"), sem("p1_free")
        o_done, o_free = sem("o_done"), sem("o_free")
        negm_ready, exp_done, p_ready = sem("negm_ready"), sem("exp_done"), sem("p_ready")
        gate_e, gate_o, zo_ready, pair_ready = sem("gate_e"), sem("gate_o"), sem("zo_ready"), sem("pair_ready")
        mh_ready, m_ready = sem("mh_ready"), sem("m_ready")
        sbl_ready, sbd_ready, w_ready = sem("sbl_ready"), sem("sbd_ready"), sem("w_ready")
        ss_ready, od_ready, f_hi = sem("ss_ready"), sem("od_ready"), sem("f_hi")
        u_sq = sem("u_sq")
        dve_step, act_step = sem("dve_step"), sem("act_step")
        stored = sem("stored")

        freed, wo_tiles = {}, set()
        for name, part in plan.items():
            if name in ("attn", "pool") or name[0] == "layer":
                for s in part:
                    freed[s["t"]] = s["r"] + s["n"] * (2 if s["kind"][-1] == "v" and s["t"] % 2 == 0 else 1)
                    if s["kind"] == "wo":
                        wo_tiles.add(s["t"])
            elif name[0] == "ff":
                for i in range(16 * BLOCKS):
                    freed[part[0] + i] = part[1] + i + 1
        all_steps = [st for n, part in plan.items() if n in ("attn", "pool") or n[0] == "layer" for s in part for st in s["steps"]]
        all_stats = [st for st in all_steps if st["op"] == "stat"] + [p for n, p in plan.items() if "stat" in n or "stat" in n[0]]
        all_stats.sort(key=lambda st: st["zd"])
        swa_t_of = {st["h"]: st for st in all_steps if st["op"] == "swa_t"}

        def raw_view(t):
            k = 4 if t in wo_tiles else 8
            n = 4 * 256 // k
            return raw[:, t // 2 % 2, :].rearrange("p (k n) -> p k n", k=k)[:, :, n * (t % 2):n * (t % 2) + n], k

        def w_slot(w, t, k):
            return w[:, t % 4, :].rearrange("p (k n) -> p k n", k=k)

        def rev(ap, z0, z1):
            return ap[:, z0:z1][:, ::-1]

        def rows(w, c0, n=256):
            return w[:, c0:c0 + n].rearrange("(k p) n -> p k n", p=P)

        def pair_sources():
            w = attn_w_in[0]
            cols = [1024, 1280] + [256 * i for i in range(4)] + [1536 + 256 * i for i in range(4)]
            out_ = [rows(w, c) for c in cols]
            out_ += [rows(attn_w_out[0], 256 * i) for i in range(4)]
            out_ += [rows(pool_w_in[0], 256 * i) for i in range(8)]
            out_ += [pool_w_mix[0].rearrange("g (k p) n -> p (g k) n", p=P)]
            out_ += [rows(pool_w_out[0], 256 * i) for i in range(4)]
            layers = []
            for l in range(DEPTH):
                w = w_in_2[l]
                dfq, sbq, third = 1536, 0, 512
                pairs = []
                for base in (dfq, sbq):
                    for half in range(2):
                        pairs += [rows(w, base + a * third + 256 * half) for a in (1, 0, 2)]
                for r0 in (512, 0):
                    pairs += [w_o_2[l][r0:r0 + 512, c:c + 512].rearrange("(k p) n -> p k n", p=P) for c in (0, 512)]
                layers.append(pairs)
            return out_, layers

        params = [(grow[G_NORM:G_NORM + 16, :], norm_g.rearrange("l (k p) -> (l k) p", p=P)),
                  (grow[G_FINAL:G_FINAL + 8, :], final_g.rearrange("(k p) -> k p", p=P)),
                  (grow[G_SCALE:G_SCALE + 8, :], pool_scale.rearrange("l (k p) -> (l k) p", p=P)),
                  (grow[G_ATTN:G_ATTN + 16, :], attn_norm_2.rearrange("l (k p) -> (l k) p", p=P)),
                  (grow[G_MLP:G_MLP + 16, :], mlp_norm_2.rearrange("l (k p) -> (l k) p", p=P)),
                  (grow[G_LAST:G_LAST + 8, :], final_norm_2.rearrange("(k p) -> k p", p=P)),
                  (grow[G_SUB:G_SUB + DEPTH, :], subln_norm_2),
                  (sink[:], attn_sinks[0].partition_broadcast(P))]
        params += [(lamv[:, i, :], v.rearrange("l d -> (l d)").partition_broadcast(P))
                   for i, v in enumerate((lam_q1_2, lam_k1_2, lam_q2_2, lam_k2_2))]

        block = ctx.enter_context(nc.Block())

        @block.sync
        def _(sp):
            for s in range(NB):
                sp.dma_start(xin[:, s, :], x[0, s * P:(s + 1) * P, :]).then_inc(in_landed, 16)
            pairs, layers = pair_sources()

            def load(p, src, phase, parity):
                if phase is not None:
                    sp.wait_ge(lo_done, phase)
                k = src.shape[1]
                dst = raw[:, parity, :].rearrange("p (k n) -> p k n", k=k)
                sp.dma_start(dst, src).then_inc(raw_landed[parity], 16)

            p = 0
            for src in pairs[:2]:
                load(p, src, None, p % 2)
                p += 1
            for src in pairs[2:]:
                load(p, src, 2 * p - 2, p % 2)
                p += 1
            for l in range(DEPTH):
                for src in layers[l]:
                    load(p, src, 2 * p - 2, p % 2)
                    p += 1
                with sp.Fori(0, BLOCKS) as b:
                    for i in range(8):
                        if i < 4:
                            src = w_ff1_2[l][:, bass.ds(b * D + 256 * i, 256)].rearrange("(k p) n -> p k n", p=P)
                        else:
                            c = 256 * (i - 4)
                            src = w_ff2_2[l][bass.ds(b * D, D), c:c + 256].rearrange("(k p) n -> p k n", p=P)
                        load(None, src, b * 16 + (2 * (p + i) - 2), (p + i) % 2)
                p += 8 * BLOCKS
            for s in range(NB):
                sp.wait_ge(result_taken, plan["last_r"] + 2 * s + 2)
                sp.dma_start(out[0, s * P:(s + 1) * P, :], yrow[:, s, :]).then_inc(stored, 16)
            sp.wait_ge(stored, 16 * NB)

        @block.gpsimd
        def _(pool):
            g = nc.gpsimd
            g.memset(ident[:], 0.0)
            g.memset(identb[:], 0.0)
            g.memset(ones[:], 1.0)
            g.memset(mean_w[:], 1.0 / D)
            g.memset(mask_sw[:], 0.0)
            g.memset(mask_sb[:], 0.0)
            g.memset(mask_df[:], 0.0)
            for s in range(PAD):
                last = g.memset(inv_n[:, s:s + 1], 1.0 / (s + 1))
            last.then_inc(const_f, 1)
            pool.wait_ge(const_f, 1)
            g.memset(mask_df[0:64, 448:512], NEG)
            for m in (ident, identb):
                g.affine_select(out=m[:], in_=m[:], compare_op=ALU.not_equal, fill=1.0, base=0,
                                pattern=[[-1, P]], channel_multiplier=1)
            g.affine_select(out=mask_sw[:, 0:P], in_=mask_sw[:, 0:P], compare_op=ALU.is_gt, fill=NEG,
                            base=0, pattern=[[1, P]], channel_multiplier=-1)
            g.affine_select(out=mask_sw[:, P:256], in_=mask_sw[:, P:256], compare_op=ALU.is_ge, fill=NEG,
                            base=0, pattern=[[-1, P]], channel_multiplier=1)
            g.affine_select(out=mask_sb[:], in_=mask_sb[:], compare_op=ALU.is_gt, fill=NEG,
                            base=0, pattern=[[-1, P]], channel_multiplier=1).then_inc(const_ready, 1)
            for s in range(4 + 2 * DEPTH):
                if s == 1:
                    for zs in [w for w in plan["attn"] if w["kind"] == "z"]:
                        pool.wait_ge(result_taken, zs["r"] + 1)
                        pool.wait_ge(o_free, zs["j"] + 1)
                        o = oraw[:, zs["j"], :]
                        g.tensor_tensor(o, tb[:, zs["j"] % 2, :], o, ALU.mult).then_inc(zo_ready, 1)
                if s:
                    pool.wait_ge(z_done, all_stats[s - 1]["zd"] + 1)
                if s == 2:
                    for us in [w for w in plan["pool"] if w["kind"] == "pu"]:
                        j = us["j"]
                        pool.wait_ge(result_taken, us["r"] + 1)
                        if j >= 2:
                            pool.wait_ge(gate_o, 8 + j - 1)
                        g.tensor_tensor(pad[:, 2 + j % 2, PAD:], pad[:, j % 2, PAD:], pad[:, j % 2, PAD - 1:PAD + S - 1],
                                        ALU.add).then_inc(pair_ready, 1)
                if s in (3, 5):
                    before = plan["pool"][-1]["r"] + 1 if s == 3 else plan["ff", 0][1]
                    pool.wait_ge(result_taken, before)
                    pool.dma_start(cs[:], rope_table).then_inc(cs_landed, 16)
                for kt in range(KT):
                    n = KT * s + kt
                    pool.wait_ge(sq_ready, n + 1)
                    if kt == 0:
                        g.tensor_copy(acc[:], sq[:, n % 2, :]).then_inc(acc_done, 1)
                    else:
                        pool.wait_ge(acc_done, n)
                        g.tensor_tensor(acc[:], acc[:], sq[:, n % 2, :], ALU.add).then_inc(acc_done, 1)

        @block.scalar
        def _(act):
            a = nc.scalar
            loop_r = [0]
            count = dict(step=0, hi=0, xh=0, sq=0, xt=0, negm=0, mh=0, stat=0, sbl=0, sbd=0, od=0, gate=0)

            def after(ins):
                count["step"] += 1
                ins.then_inc(act_step, 1)
                act.wait_ge(act_step, count["step"])

            def conv(t, loop=None):
                if loop is None:
                    if t >= LAST_T:
                        return
                    act.wait_ge(raw_landed[t // 2 % 2], 16 * (t // 4 + 1))
                    if t >= 4:
                        act.wait_ge(psum_done, freed[t - 4])
                else:
                    act.wait_ge(raw_landed[t // 2 % 2], loop * 64 + 16 * (t // 4 + 1))
                    act.wait_ge(psum_done, loop * 16 + (loop_r[0] + t - 3))
                src, shape = raw_view(t)
                a.activation(w_slot(WH, t, shape), src, ACT.Copy).then_inc(hi_done, 1)

            def prep(row, kt, r, first=False):
                if r is None:
                    act.wait_ge(xt_ready, kt + 1)
                else:
                    act.wait_ge(result_taken, r + 1)
                if row is not None:
                    if first:
                        act.wait_ge(gain_ready, 1)
                    a.activation(XH[:, kt, :], xT[:, kt, :], ACT.Copy, scale=gain[:, row + kt:row + kt + 1]).then_inc(xh_ready, 1)
                n = count["sq"]
                if n >= 2:
                    act.wait_ge(acc_done, n - 1)
                a.activation(sq[:, n % 2, :], xT[:, kt, :], ACT.Square).then_inc(sq_ready, 1)
                count["sq"] += 1

            def stat(st):
                act.wait_ge(z_free, st["z"] + 1)
                after(a.activation(rstd[:], ms[:], ACT.Ln))
                a.activation(rstd[:], rstd[:], ACT.Exp, scale=-0.5).then_inc(stat_y, 1)

            def mh(src, j, dst=None, **kw):
                a.activation((dst or MH)[:, j, :], src, ACT.Copy, **kw).then_inc(mh_ready, 1)
                count["mh"] += 1

            def denominator(s):
                act.wait_ge(result_taken, s["r"] + 1)
                e = sq[:, s["j"] % 2, :]
                after(a.activation(e, tb[:, s["j"] % 2, :], ACT.Exp, scale=-1.0))
                a.activation(e, e, ACT.Copy, bias=1.0).then_inc(gate_e, 1)

            def swa_exp(h):
                act.wait_ge(negm_ready, count["negm"] + 1)
                count["negm"] += 1
                sl = pr[:, h % 3, :]
                for n in range(NB):
                    lo_, hi_ = (0, P) if n == 0 else (256 * n - P, 256 * n + P)
                    a.activation(sl[:, lo_:hi_], sl[:, lo_:hi_], ACT.Exp, bias=small[:, 8 * (h % 2) + n:8 * (h % 2) + n + 1],
                                 accum_out=small[:, 16 + 8 * (h % 2) + n:17 + 8 * (h % 2) + n])
                a.activation(small[:, 20 + 8 * (h % 2):24 + 8 * (h % 2)], small[:, 8 * (h % 2):8 * (h % 2) + 4], ACT.Exp,
                             bias=sink[:, h:h + 1]).then_inc(exp_done, 1)

            def swa_steps(s, half):
                for st in s["steps"]:
                    if st.get("half") != half or st["op"] != "swa_t":
                        continue
                    act.wait_ge(p0_done, st["p0"] + 1)
                    a.activation(pt0[:, 0:512], PP[:, 0, :], ACT.Copy).then_inc(p0_free, 1)
                for st in s["steps"]:
                    if st.get("half") == half and st["op"] == "swa_qk":
                        swa_exp(st["h"])
                for st in s["steps"]:
                    if st.get("half") == half and st["op"] == "swa_t" and st["h"] % 2:
                        act.wait_ge(o_done, st["o"] + 1)
                        a.activation(oraw[:, st["h"] // 2, :], O[:], ACT.Copy).then_inc(o_free, 1)

            def layer_begin(s, l):
                for st in s["steps"]:
                    if st["op"] == "sb_o":
                        act.wait_ge(o_done, st["o"] + 1)
                        mh(O[:], st["h"] // 2)
                    if st["op"] == "df_f":
                        d = st["h"]
                        act.wait_ge(o_done, [y["o"] for x in plan["layer", l] for y in x["steps"] if y["op"] == "t" and y["df"] and y["h"] == d][0] + 1)
                        act.wait_ge(dfw_ready, 4 * l + d + 1)
                        for n in range(NB):
                            i = a.activation(sq[:, 1, n * P:(n + 1) * P], O[:, n * P:(n + 1) * P], ACT.Square,
                                             scale=small[:, 24 + n:25 + n], accum_out=small[:, 40 + n:41 + n])
                        i.then_inc(ss_ready, 1)
                        act.wait_ge(sub_v, 4 * l + d + 1)
                        after(a.activation(small[:, 52:56], small[:, 44:48], ACT.Ln))
                        a.activation(small[:, 52:56], small[:, 52:56], ACT.Exp, scale=-0.5).then_inc(sub_y, 1)
                for st in s["steps"]:
                    if st["op"] == "sb_qk":
                        for c, (c0, cn, _) in enumerate(CHUNKS):
                            act.wait_ge(z_done, st["zd"] + c + 1)
                            e = ea[:, 0, c0:c0 + cn]
                            after(a.activation(e, Z[:, c0:c0 + cn], ACT.Abs))
                            after(a.activation(e, e, ACT.Exp, scale=-1.0))
                            a.activation(e, e, ACT.Ln, bias=1.0).then_inc(sbl_ready, 1)
                    if st["op"] == "df_qk":
                        act.wait_ge(negm_ready, count["negm"] + 1)
                        count["negm"] += 1
                        m = st["m"]
                        for n in range(NB):
                            r = ea[:, m, ZOFF[n]:ZOFF[n] + P * (n + 1)]
                            i = a.activation(r, r, ACT.Exp, bias=small[:, 4 * m + n:4 * m + n + 1],
                                             accum_out=small[:, 16 + 4 * m + n:17 + 4 * m + n])
                        i.then_inc(exp_done, 1)

            def layer_end(s, l):
                for st in s["steps"]:
                    if st["op"] == "sb_qk":
                        for c, (c0, cn, _) in enumerate(CHUNKS):
                            act.wait_ge(sbd_ready, count["sbd"] + 1)
                            count["sbd"] += 1
                            a.activation(ea[:, 1 + st["h"] % 2, c0:c0 + cn], ea[:, 1 + st["h"] % 2, c0:c0 + cn], ACT.Exp).then_inc(w_ready, 1)
                for st in s["steps"]:
                    if st["op"] == "df_f":
                        act.wait_ge(p0_done, st["p0"] + 1)
                        mh(PP[:, 0, :], 4 + st["h"], scale=gain[:, G_SUB + l:G_SUB + l + 1])
                    if st["op"] == "t":
                        act.wait_ge(p0_done, st["p0"] + 1)
                        a.activation(pt[:, :, 384:512], PP[:, 0, :].rearrange("p (k q) -> p k q", q=P), ACT.Copy).then_inc(p0_free, 1)
                        act.wait_ge(p0_done, st["p0"] + 2)
                        a.activation(pt[:, 0:2, 128:256], PP[:, 0, 0:256].rearrange("p (k q) -> p k q", q=P), ACT.Copy).then_inc(p0_free, 1)

            act.preload_act_table_set("natural_log_exp_and_others")
            for dst, src in params:
                act.dma_start(dst, src).then_inc(par_landed, 16)
            act.wait_ge(lam_dot, 2 * DEPTH)
            a.activation(lame[:], lamd[:], ACT.Exp).then_inc(lam_exp, 1)
            conv(0)
            conv(1)
            for kt in range(KT):
                prep(G_NORM, kt, kt, True)
            for s in plan["attn"]:
                t, j = s["t"], s["j"]
                kind = s["kind"]
                conv(t + 2)
                for st in s["steps"]:
                    if st["op"] == "stat":
                        stat(st)
                for half in range(2):
                    swa_steps(s, half)
                if kind == "z":
                    denominator(s)
                    for i in ([j - 1] if j < 7 else [6, 7]):
                        if i >= 0:
                            act.wait_ge(gate_o, i + 1)
                            mh(oraw[:, i, :], i)
                if kind == "out":
                    prep(G_NORM + 8, j, s["r"])
            for s in plan["pool"]:
                t, j, kind = s["t"], s["j"], s["kind"]
                conv(t + 2)
                for st in s["steps"]:
                    stat(st)
                if kind == "pu":
                    for i in ([j - 1] if j < 7 else [6, 7]):
                        if i >= 0:
                            act.wait_ge(gate_o, 8 + i + 1)
                            mh(pf[:, i % 2, :], i)
                if kind == "pz":
                    denominator(s)
                if kind == "mix":
                    for i in range(4):
                        act.wait_ge(result_taken, s["r"] + i + 1)
                        mh(tb[:, i % 2, :], 2 * i + j, XH)
                if kind == "out":
                    prep(None, j, s["r"])
            stat(plan["mid_stat"])
            for kt in range(KT):
                prep(G_ATTN, kt, None)
            for l in range(DEPTH):
                for s in plan["layer", l]:
                    t, j = s["t"], s["j"]
                    conv(t + 2)
                    for st in s["steps"]:
                        if st["op"] == "stat":
                            stat(st)
                    layer_begin(s, l)
                    layer_end(s, l)
                    if s["kind"] in ("dfk", "dfq"):
                        act.wait_ge(psum_done, s["r"] + 1)
                        act.wait_ge(result_taken, s["r"])
                        for q in range(4):
                            o = q ^ 1
                            i = a.activation(tb[32 * q:32 * q + 32, 0, :], U[32 * o:32 * o + 32, s["r"] % 2, :], ACT.Copy)
                        i.then_inc(rope_shifted, 1)
                    if s["kind"] == "wo" and s["second"]:
                        for i in range(2):
                            prep(G_MLP + 8 * l, 2 * (j - 4) + i, s["r"] + i)
                stat(plan["ff_stat", l])
                t0, r0 = plan["ff", l]
                loop_r[0] = r0 - t0
                m0 = count["mh"]

                def ff_block(b, last):
                    for i in range(16):
                        if not (last and i >= 14):
                            conv(t0 + i + 2, b)
                        if i < 8:
                            act.wait_ge(result_taken, b * 16 + (r0 + i + 1))
                            a.activation(sq[:, i % 2, :], tb[:, i % 2, :], ACT.Square).then_inc(u_sq, 1)
                            a.activation(MH[:, i, :], tb[:, i % 2, :], ACT.Square).then_inc(mh_ready, 1)

                if l < DEPTH - 1:
                    with act.Fori(0, BLOCKS) as b:
                        ff_block(b, False)
                else:
                    with act.Fori(0, BLOCKS - 1) as b:
                        ff_block(b, False)
                    ff_block(BLOCKS - 1, True)
                count["mh"] += 8 * BLOCKS
                for kt in range(KT):
                    prep(G_ATTN + 8 * (l + 1) if l < DEPTH - 1 else None, kt, r0 + 16 * BLOCKS - 1)
            stat(plan["last_stat"])

        @block.vector
        def _(dve):
            v = nc.vector
            loop_r = [0]
            count = dict(step=0, xh=0, xg=0, exp=0, gate_e=0, mh=0, stat=0, sbl=0, usq=0, ss=0)

            def after(ins):
                count["step"] += 1
                ins.then_inc(dve_step, 1)
                dve.wait_ge(dve_step, count["step"])

            def conv(t, loop=None):
                if loop is None:
                    if t >= LAST_T:
                        return
                    dve.wait_ge(raw_landed[t // 2 % 2], 16 * (t // 4 + 1))
                    dve.wait_ge(hi_done, t + 1)
                    if t >= 4:
                        dve.wait_ge(psum_done, freed[t - 4])
                else:
                    dve.wait_ge(raw_landed[t // 2 % 2], loop * 64 + 16 * (t // 4 + 1))
                    dve.wait_ge(hi_done, loop * 16 + (t + 1))
                    dve.wait_ge(psum_done, loop * 16 + (loop_r[0] + t - 3))
                src, shape = raw_view(t)
                v.tensor_tensor(w_slot(WL, t, shape), src, w_slot(WH, t, shape).bitcast(F32), ALU.subtract).then_inc(lo_done, 1)

            def prep_lo(row, kt):
                count["xh"] += 1
                dve.wait_ge(xh_ready, count["xh"])
                v.scalar_tensor_tensor(out=XL[:, kt, :], in0=xT[:, kt, :], scalar=gain[:, row + kt:row + kt + 1],
                                       in1=XH[:, kt, :].bitcast(F32), op0=ALU.mult, op1=ALU.subtract).then_inc(xg_ready, 1)

            def stat(st):
                dve.wait_ge(z_done, st["zd"] + 1)
                v.tensor_scalar(ms[:, 0:S], Z[:, 0:S], EPS, None, ALU.add)
                count["stat"] += 1
                v.tensor_scalar(ms[:, S:NS], Z[:, 512:512 + NB], EPS, None, ALU.add).then_inc(z_free, 1)
                dve.wait_ge(z_free, st["z"] + 1)
                dve.wait_ge(stat_y, count["stat"])
                after(v.tensor_tensor(nt[:], rstd[:], rstd[:], ALU.mult))
                after(v.tensor_tensor(nt[:], nt[:], ms[:], ALU.mult))
                after(v.tensor_scalar(nt[:], nt[:], -0.5, 1.5, ALU.mult, ALU.add))
                after(v.tensor_tensor(rstd[:], rstd[:], nt[:], ALU.mult))

            def result(r, loop=None, per=16):
                if loop is None:
                    dve.wait_ge(psum_done, r + 1)
                    if r:
                        dve.wait_ge(result_taken, r)
                else:
                    dve.wait_ge(psum_done, loop * per + (r + 1))
                    dve.wait_ge(result_taken, loop * per + r)
                return U[:, r % 2, :]

            def low(full, j, dst=None, hi=None):
                count["mh"] += 1
                dve.wait_ge(mh_ready, count["mh"])
                v.tensor_tensor((dst or ML)[:, j, :], full, (hi or MH)[:, j, :].bitcast(F32), ALU.subtract).then_inc(m_ready, 1)

            def swa_softmax_a(st):
                h = st["h"]
                sl = pr[:, h % 3, :]
                b = 8 * (h % 2)
                dve.wait_ge(z_done, st["zd"] + 1)
                if h >= 3:
                    dve.wait_ge(p0_done, swa_t_of[h - 3]["p0"] + 1)
                    dve.wait_ge(p1_done, swa_t_of[h - 3]["p1"] + 1)
                for n in range(NB):
                    lo_, hi_ = (0, P) if n == 0 else (256 * n - P, 256 * n + P)
                    i = v.tensor_tensor_reduce(sl[:, lo_:hi_], Z[:, P + lo_:P + hi_], mask_sw[:, (P if n == 0 else 0):256],
                                               1.0, sink[:, h:h + 1], ALU.add, ALU.max, small[:, 32 + b + n:33 + b + n])
                i.then_inc(z_free, 1)
                dve.wait_ge(z_free, st["z"] + 1)
                v.tensor_scalar(small[:, b:b + 4], small[:, 32 + b:36 + b], -1.0, None, ALU.mult).then_inc(negm_ready, 1)

            def swa_softmax_b(h):
                b = 8 * (h % 2)
                dve.wait_ge(exp_done, h + 1)
                after(v.tensor_tensor(small[:, 16 + b:20 + b], small[:, 16 + b:20 + b], small[:, 20 + b:24 + b], ALU.add))
                after(v.reciprocal(small[:, 36 + b:40 + b], small[:, 16 + b:20 + b]))
                for n in range(NB):
                    lo_, hi_ = (0, P) if n == 0 else (256 * n - P, 256 * n + P)
                    r = pr[:, h % 3, lo_:hi_]
                    i = v.tensor_scalar(r, r, small[:, 36 + b + n:37 + b + n], None, ALU.mult)
                i.then_inc(p_ready, 1)

            def swa_steps(s, half):
                for st in s["steps"]:
                    if st.get("half") == half and st["op"] == "swa_qk":
                        swa_softmax_a(st)
                for st in s["steps"]:
                    if st.get("half") == half and st["op"] == "swa_t":
                        if st["h"] + 1 < 16:
                            swa_softmax_b(st["h"] + 1)
                        dve.wait_ge(p1_done, st["p1"] + 1)
                        v.tensor_copy(pt0[:, 512:896], PP[:, 1, 0:384]).then_inc(p1_free, 1)
                    elif st.get("half") == half and st["op"] == "swa_qk" and st["h"] == 1:
                        swa_softmax_b(0)

            def layer_begin(s, l):
                for st in s["steps"]:
                    if st["op"] == "sb_o":
                        count["mh"] += 1
                        dve.wait_ge(mh_ready, count["mh"])
                        j = st["h"] // 2
                        v.tensor_tensor(ML[:, j, :], O[:], MH[:, j, :].bitcast(F32), ALU.subtract).then_inc(m_ready, 1)
                        dve.wait_ge(m_ready, count["mh"])
                        dve.sem_inc(o_free, 1)
                    if st["op"] == "df_f":
                        count["ss"] += 1
                        dve.wait_ge(ss_ready, count["ss"])
                        lam_init = 0.8 - 0.6 * math.exp(-0.3 * l)
                        after(v.tensor_scalar(small[:, 44:48], small[:, 40:44], 1.0 / P, EPS, ALU.mult, ALU.add))
                        v.tensor_copy(small[:, 48:52], small[:, 44:48]).then_inc(sub_v, 1)
                        dve.wait_ge(sub_v, count["ss"])
                        dve.wait_ge(sub_y, count["ss"])
                        after(v.tensor_tensor(small[:, 56:60], small[:, 52:56], small[:, 52:56], ALU.mult))
                        after(v.tensor_tensor(small[:, 56:60], small[:, 56:60], small[:, 44:48], ALU.mult))
                        after(v.tensor_scalar(small[:, 56:60], small[:, 56:60], -0.5, 1.5, ALU.mult, ALU.add))
                        after(v.tensor_tensor(small[:, 56:60], small[:, 56:60], small[:, 52:56], ALU.mult))
                        after(v.scalar_tensor_tensor(out=small[:, 56:60], in0=small[:, 56:60], scalar=1.0 - lam_init,
                                                     in1=small[:, 24:28], op0=ALU.mult, op1=ALU.mult))
                        for n in range(NB):
                            i = v.tensor_scalar(tb[:, 1, n * P:(n + 1) * P], O[:, n * P:(n + 1) * P], small[:, 56 + n:57 + n], None, ALU.mult)
                        i.then_inc(od_ready, 1)
                        dve.wait_ge(od_ready, count["ss"])
                        dve.sem_inc(o_free, 1)
                for st in s["steps"]:
                    if st["op"] == "df_qk":
                        m = st["m"]
                        dve.wait_ge(z_done, st["zd"] + 1)
                        if 4 * l + st["h"]:
                            dve.wait_ge(dfw_ready, 4 * l + st["h"])
                        for n in range(NB):
                            w = P * (n + 1)
                            i = v.tensor_tensor_reduce(ea[:, m, ZOFF[n]:ZOFF[n] + w], Z[:, ZOFF[n]:ZOFF[n] + w], mask_df[:, 512 - w:512],
                                                       1.0, -3.0e38, ALU.add, ALU.max, small[:, 32 + 4 * m + n:33 + 4 * m + n])
                        i.then_inc(z_free, 1)
                        dve.wait_ge(z_free, st["z"] + 1)
                        v.tensor_scalar(small[:, 4 * m:4 * m + 4], small[:, 32 + 4 * m:36 + 4 * m], -1.0, None, ALU.mult).then_inc(negm_ready, 1)
                    if st["op"] == "sb_qk":
                        if st["h"] == 0:
                            dve.wait_ge(dfw_ready, 4 * l + 4)
                        for c, (c0, cn, blocks) in enumerate(CHUNKS):
                            count["sbl"] += 1
                            dve.wait_ge(sbl_ready, count["sbl"])
                            e, z = ea[:, 0, c0:c0 + cn], Z[:, c0:c0 + cn]
                            after(v.scalar_tensor_tensor(out=e, in0=z, scalar=0.0, in1=e, op0=ALU.max, op1=ALU.add))
                            for n in blocks:
                                z0, z1 = ZOFF[n], ZOFF[n] + P * (n + 1)
                                i = v.tensor_tensor_scan(rev(cc, z0, z1), ones[:].to_broadcast([P, z1 - z0]), rev(ea[:, 0, :], z0, z1), 0.0, ALU.mult, ALU.add)
                            after(i)
                            v.tensor_tensor(ea[:, 1 + st["h"] % 2, c0:c0 + cn], z, cc[:, c0:c0 + cn], ALU.subtract).then_inc(sbd_ready, 1)
                        dve.wait_ge(sbd_ready, count["sbl"])
                        dve.sem_inc(z_free, 1)

            def layer_end(s, l):
                for st in s["steps"]:
                    if st["op"] == "df_qk":
                        count["exp"] += 1
                        dve.wait_ge(exp_done, 16 + count["exp"])
                        if st["m"] == 1:
                            after(v.reciprocal(small[:, 24:32], small[:, 16:24]))
                            after(v.scalar_tensor_tensor(out=small[:, 8:12], in0=small[:, 16:20], scalar=neglam[:, l:l + 1],
                                                         in1=small[:, 28:32], op0=ALU.mult, op1=ALU.mult))
                            for n in range(NB):
                                z0, z1 = ZOFF[n], ZOFF[n] + P * (n + 1)
                                i = v.scalar_tensor_tensor(out=cc[:, z0:z1], in0=ea[:, 1, z0:z1], scalar=small[:, 8 + n:9 + n],
                                                           in1=ea[:, 0, z0:z1], op0=ALU.mult, op1=ALU.add)
                            i.then_inc(dfw_ready, 1)
                for st in s["steps"]:
                    if st["op"] == "df_f":
                        count["mh"] += 1
                        dve.wait_ge(mh_ready, count["mh"])
                        j = 4 + st["h"]
                        v.scalar_tensor_tensor(out=ML[:, j, :], in0=PP[:, 0, :], scalar=gain[:, G_SUB + l:G_SUB + l + 1],
                                               in1=MH[:, j, :].bitcast(F32), op0=ALU.mult, op1=ALU.subtract).then_inc(m_ready, 1)
                        dve.wait_ge(m_ready, count["mh"])
                        dve.sem_inc(p0_free, 1)
                    if st["op"] == "t":
                        dve.wait_ge(p1_done, st["p1"] + 1)
                        v.tensor_copy(pt[:, 0:3, 256:384], PP[:, 1, 0:384].rearrange("p (k q) -> p k q", q=P))
                        v.tensor_copy(pt[:, 0, 0:128], PP[:, 1, 384:512]).then_inc(p1_free, 1)

            dve.wait_ge(par_landed, 16 * len(params))
            for l in range(DEPTH):
                for i in range(2):
                    c = slice(64 * l, 64 * l + 64)
                    v.tensor_tensor_reduce(lamw[:], lamv[:, 2 * i, c], lamv[:, 2 * i + 1, c], 1.0, 0.0, ALU.mult, ALU.add,
                                           lamd[:, 2 * l + i:2 * l + i + 1]).then_inc(lam_dot, 1)
                    dve.wait_ge(lam_dot, 2 * l + i + 1)
            dve.wait_ge(lam_exp, 1)
            for l in range(DEPTH):
                lam_init = 0.8 - 0.6 * math.exp(-0.3 * l)
                v.scalar_tensor_tensor(out=neglam[:, l:l + 1], in0=lame[:, 2 * l + 1:2 * l + 2], scalar=-lam_init,
                                       in1=lame[:, 2 * l:2 * l + 1], op0=ALU.add, op1=ALU.subtract)
            dve.wait_ge(gain_done, 1)
            v.tensor_copy(gain[:], Z[:, 0:GROWS]).then_inc(gain_ready, 1)
            dve.wait_ge(gain_ready, 1)
            conv(0)
            conv(1)
            for kt in range(KT):
                ps = result(kt)
                v.tensor_copy(xT[:, kt, :], ps).then_inc(result_taken, 1)
                if kt:
                    prep_lo(G_NORM, kt - 1)
            dve.wait_ge(result_taken, KT)
            prep_lo(G_NORM, KT - 1)
            dve.wait_ge(const_ready, 1)

            def add_x(ps, kt, last, r):
                i = v.tensor_tensor(xT[:, kt, :], xT[:, kt, :], ps, ALU.add)
                i.then_inc(result_taken, 1)
                if last:
                    dve.wait_ge(result_taken, r + 1)

            def sigmoid(j, base):
                dve.wait_ge(gate_e, base + j + 1)
                after(v.reciprocal(sq[:, j % 2, :], sq[:, j % 2, :]))

            for s in plan["attn"]:
                t, j, kind, r = s["t"], s["j"], s["kind"], s["r"]
                conv(t + 2)
                for st in s["steps"]:
                    if st["op"] == "stat":
                        stat(st)
                for half in range(2):
                    swa_steps(s, half)
                ps = result(r)
                rb = rstd[:, 0:S]
                if kind == "k":
                    for g in range(2):
                        src = slice(64 * g, 64 * g + 64)
                        for half in range(2):
                            i = v.tensor_tensor(kd[64 * half:64 * half + 64, 2 * j + g, :], U[src, r % 2, :], rstd[64 * half:64 * half + 64, 0:S], ALU.mult)
                    i.then_inc(result_taken, 1)
                elif kind == "v":
                    for i in range(2):
                        ps = result(r + i)
                        n = 2 * j + i
                        v.tensor_scalar(v0[:, n, :], ps[:, 0:256], rstd[:, S + n:S + n + 1], None, ALU.mult).then_inc(result_taken, 1)
                elif kind == "q":
                    v.scalar_tensor_tensor(out=q0[:, j % 4, :], in0=ps, scalar=0.125, in1=rb, op0=ALU.mult, op1=ALU.mult).then_inc(result_taken, 1)
                elif kind == "z":
                    v.tensor_tensor(tb[:, j % 2, :], ps, rb, ALU.mult).then_inc(result_taken, 1)
                    for i in ([j - 1] if j < 7 else [6, 7]):
                        if i >= 0:
                            sigmoid(i, 0)
                            dve.wait_ge(zo_ready, i + 1)
                            v.tensor_tensor(oraw[:, i, :], sq[:, i % 2, :], oraw[:, i, :], ALU.mult).then_inc(gate_o, 1)
                    for i in ([j - 2] if j < 7 else [5, 6, 7]):
                        if i >= 0:
                            dve.wait_ge(gate_o, i + 1)
                            low(oraw[:, i, :], i)
                elif kind == "out":
                    add_x(ps, j, True, r)
                    prep_lo(G_NORM + 8, j)
            def pooled(j):
                w = POOL_W[j // 2]
                u = pad[:, j % 2, PAD:]
                dve.wait_ge(pair_ready, j + 1)
                dve.wait_ge(gate_o, 8 + j)
                src, sh = 2 + j % 2, 2
                while sh < w:
                    dst = 5 if src == 4 else 4
                    after(v.tensor_tensor(pad[:, dst, PAD:], pad[:, src, PAD:], pad[:, src, PAD - sh:PAD + S - sh], ALU.add))
                    src, sh = dst, 2 * sh
                head = pad[:, src, PAD:PAD + w]
                after(v.scalar_tensor_tensor(out=head, in0=head, scalar=float(w), in1=inv_n[:, 0:w], op0=ALU.mult, op1=ALU.mult))
                if j >= 2:
                    dve.wait_ge(m_ready, 8 + j - 1)
                v.scalar_tensor_tensor(out=pf[:, j % 2, :], in0=pad[:, src, PAD:], scalar=1.0 / w, in1=u,
                                       op0=ALU.mult, op1=ALU.subtract).then_inc(gate_o, 1)

            after(v.memset(pad[:, :, 0:PAD], 0.0))
            for s in plan["pool"]:
                t, j, kind, r = s["t"], s["j"], s["kind"], s["r"]
                conv(t + 2)
                for st in s["steps"]:
                    stat(st)
                ps = result(r)
                rb = rstd[:, 0:S]
                if kind == "pu":
                    v.tensor_tensor(pad[:, j % 2, PAD:], ps, rb, ALU.mult).then_inc(result_taken, 1)
                    for i in ([j - 1] if j < 7 else [6, 7]):
                        if i >= 0:
                            pooled(i)
                        if i >= 1:
                            low(pf[:, (i - 1) % 2, :], i - 1)
                elif kind == "pz":
                    v.tensor_tensor(tb[:, j % 2, :], ps, rb, ALU.mult).then_inc(result_taken, 1)
                    if j == 0:
                        low(pf[:, 1, :], 7)
                    for i in ([j - 1] if j < 7 else [6, 7]):
                        if i >= 0:
                            sigmoid(i, 8)
                            after(v.scalar_tensor_tensor(out=sz[:, i, :], in0=tb[:, i % 2, :], scalar=gain[:, G_SCALE + i:G_SCALE + i + 1],
                                                         in1=sq[:, i % 2, :], op0=ALU.mult, op1=ALU.mult))
                elif kind == "mix":
                    for i in range(4):
                        if i:
                            ps = result(r + i)
                        c = 2 * i + j
                        dve.wait_ge(m_ready, count["mh"])
                        v.tensor_tensor(tb[:, i % 2, :], ps, sz[:, c, :], ALU.mult).then_inc(result_taken, 1)
                        if i:
                            low(tb[:, (i - 1) % 2, :], c - 2, XL, XH)
                    dve.wait_ge(result_taken, r + 4)
                    low(tb[:, 1, :], 6 + j, XL, XH)
                elif kind == "out":
                    add_x(ps, j, True, r)
            stat(plan["mid_stat"])
            for kt in range(KT):
                v.scalar_tensor_tensor(out=xT[:, kt, :], in0=xT[:, kt, :], scalar=gain[:, G_FINAL + kt:G_FINAL + kt + 1],
                                       in1=rstd[:, 0:S], op0=ALU.mult, op1=ALU.mult).then_inc(xt_ready, 1)
            dve.wait_ge(xt_ready, KT)
            for kt in range(KT):
                prep_lo(G_ATTN, kt)
            rope = [0]
            for l in range(DEPTH):
                for s in plan["layer", l]:
                    t, j, kind, r = s["t"], s["j"], s["kind"], s["r"]
                    conv(t + 2)
                    for st in s["steps"]:
                        if st["op"] == "stat":
                            stat(st)
                            dve.wait_ge(cs_landed, 16 * (l + 1))
                            for i in range(2):
                                after(v.tensor_tensor(cs[:, i, :], cs[:, i, :], rstd[:, 0:S], ALU.mult))
                    layer_begin(s, l)
                    layer_end(s, l)
                    ps = result(r)
                    rb = rstd[:, 0:S]
                    if kind in ("dfk", "dfq"):
                        rope[0] += 1
                        dve.wait_ge(rope_shifted, rope[0])
                        scale = 0.125 if kind == "dfq" else 1.0
                        v.tensor_tensor(qk[kind][:, j, :], ps, cs[:, 0, :], ALU.mult)
                        after(v.tensor_tensor(tb[:, 0, :], tb[:, 0, :], cs[:, 1, :], ALU.mult))
                        if kind == "dfq":
                            after(v.tensor_tensor(tb[:, 0, :], tb[:, 0, :], qk[kind][:, j, :], ALU.add))
                            v.tensor_scalar(qk[kind][:, j, :], tb[:, 0, :], scale, None, ALU.mult).then_inc(result_taken, 1)
                        else:
                            v.tensor_tensor(qk[kind][:, j, :], tb[:, 0, :], qk[kind][:, j, :], ALU.add).then_inc(result_taken, 1)
                    elif kind == "sbk":
                        v.tensor_tensor(qk[kind][:, j, :], ps, rb, ALU.mult).then_inc(result_taken, 1)
                    elif kind == "sbq":
                        v.scalar_tensor_tensor(out=qk[kind][:, j, :], in0=ps, scalar=0.125, in1=rb, op0=ALU.mult, op1=ALU.mult).then_inc(result_taken, 1)
                    elif kind in ("dfv", "sbv"):
                        for i in range(2):
                            if i:
                                ps = result(r + i)
                            n = 2 * (j % 2) + i
                            c = 256 * (j // 2)
                            v.tensor_scalar(qk[kind][:, n, c:c + 256], ps[:, 0:256], rstd[:, S + n:S + n + 1], None, ALU.mult).then_inc(result_taken, 1)
                    elif kind == "wo":
                        for i in range(2):
                            if i:
                                ps = result(r + i)
                            kt = 2 * (j % 4) + i
                            add_x(ps, kt, s["second"], r + i)
                            if s["second"]:
                                prep_lo(G_MLP + 8 * l, kt)
                stat(plan["ff_stat", l])
                t0, r0 = plan["ff", l]
                loop_r[0] = r0 - t0
                m0 = count["mh"]
                u0 = count["usq"]

                def ff_block(b, last):
                    for i in range(16):
                        if not (last and i >= 14):
                            conv(t0 + i + 2, b)
                        ps = result(r0 + i, b)
                        if i < 8:
                            v.scalar_tensor_tensor(out=tb[:, i % 2, :], in0=ps, scalar=0.0, in1=rstd[:, 0:S], op0=ALU.max,
                                                   op1=ALU.mult).then_inc(result_taken, 1)
                            dve.wait_ge(u_sq, b * 8 + (u0 + i + 1))
                            dve.wait_ge(mh_ready, b * 8 + (m0 + i + 1))
                            v.tensor_tensor(ML[:, i, :], sq[:, i % 2, :], MH[:, i, :].bitcast(F32), ALU.subtract).then_inc(m_ready, 1)
                        else:
                            v.tensor_tensor(xT[:, i - 8, :], xT[:, i - 8, :], ps, ALU.add).then_inc(result_taken, 1)

                if l < DEPTH - 1:
                    with dve.Fori(0, BLOCKS) as b:
                        ff_block(b, False)
                else:
                    with dve.Fori(0, BLOCKS - 1) as b:
                        ff_block(b, False)
                    ff_block(BLOCKS - 1, True)
                count["mh"] += 8 * BLOCKS
                count["usq"] += 8 * BLOCKS
                dve.wait_ge(result_taken, r0 + 16 * BLOCKS)
                for kt in range(KT):
                    if l == DEPTH - 1:
                        v.tensor_scalar(xf[:, kt, :], xT[:, kt, :], gain[:, G_LAST + kt:G_LAST + kt + 1], None, ALU.mult).then_inc(xt_ready, 1)
                if l < DEPTH - 1:
                    for kt in range(KT):
                        prep_lo(G_ATTN + 8 * (l + 1), kt)
            stat(plan["last_stat"])
            for s in range(NB):
                for half in range(2):
                    ps = result(plan["last_r"] + 2 * s + half)
                    v.tensor_scalar(yrow[:, s, 512 * half:512 * half + 512], ps, rstd[:, S + s:S + s + 1], None, ALU.mult).then_inc(result_taken, 1)

        @block.tensor
        def _(pe):
            mm = nc.tensor.matmul
            xg = [0]

            def begin(r, loop=None):
                if loop is None:
                    if r >= 2:
                        pe.wait_ge(result_taken, r - 1)
                else:
                    pe.wait_ge(result_taken, loop * 16 + (r - 1))
                return U[:, r % 2, :]

            def three(o, wh, wl, xh, xl, first, last, **kw):
                mm(o, wl, xh, start=first, stop=False, **kw)
                mm(o, wh, xl, start=False, stop=False, **kw)
                return mm(o, wh, xh, start=False, stop=last, **kw)

            def tile_parts(s, kts=None, ready=None):
                kind, t, r = s["kind"], s["t"], s["r"]
                a, al = (MH, ML) if kind == "wo" or kind == "out" and s["src"] == "M" or kind == "mix" else (XH, XL)

                def part(i):
                    if i == 0 and kind[-1] != "v":
                        pe.wait_ge(lo_done, t + 1)
                    if i == 0 and kind[-1] == "v":
                        pe.wait_ge(lo_done, t - t % 2 + 2)
                    if kind == "wo":
                        res, k0 = r + i // 2, 2 * (i % 2)
                        o = begin(res) if i % 2 == 0 else U[:, res % 2, :]
                        base = 0 if s["second"] else 4
                        for k in range(k0, k0 + 2):
                            if ready and i < 2:
                                pe.wait_ge(m_ready, ready[k])
                            c = slice(256 * k + P * (i // 2), 256 * k + P * (i // 2) + P)
                            last = three(o, WH[:, t % 4, c], WL[:, t % 4, c], a[:, base + k, :], al[:, base + k, :], k == 0, k == 3)
                        if i % 2:
                            last.then_inc(psum_done, 1)
                    elif kind == "mix":
                        g = i
                        o = begin(r + g)
                        for k in range(2):
                            c = slice(P * (2 * g + k), P * (2 * g + k) + P)
                            last = three(o, WH[:, t % 4, c], WL[:, t % 4, c], MH[:, 2 * g + k, :], ML[:, 2 * g + k, :], k == 0, k == 1)
                        last.then_inc(psum_done, 1)
                    elif kind[-1] == "v":
                        res = r + i // 2
                        n = 2 * (s["j"] % 2) + i // 2
                        o = begin(res) if i % 2 == 0 else U[:, res % 2, :]
                        t2 = t - t % 2
                        s2 = t2 % 4
                        q = slice(P * n, P * n + P)
                        for k in range(4 * (i % 2), 4 * (i % 2) + 4):
                            c = slice(P * k, P * k + P)
                            wh, wl = WH[:, s2:s2 + 2, c], WL[:, s2:s2 + 2, c]
                            o2 = o[:, 0:256]
                            mm(o2, XH[:, k, q], wl, start=k == 0, stop=False)
                            mm(o2, XL[:, k, q], wh, start=False, stop=False)
                            last = mm(o2, XH[:, k, q], wh, start=False, stop=k == 7)
                        if i % 2:
                            last.then_inc(psum_done, 1)
                    else:
                        o = begin(r) if i == 0 else U[:, r % 2, :]
                        order = kts or list(range(8))
                        for k in order[2 * i:2 * i + 2]:
                            if ready:
                                pe.wait_ge(ready["sem"], ready[k])
                            c = slice(P * k, P * k + P)
                            last = three(o, WH[:, t % 4, c], WL[:, t % 4, c], a[:, k, :], al[:, k, :], k == order[0], k == order[7])
                        if i == 3:
                            last.then_inc(psum_done, 1)
                return [lambda i=i: part(i) for i in range(4)]

            def stat(st):
                pe.wait_ge(acc_done, KT * (stats[0] + 1))
                stats[0] += 1
                if st["z"]:
                    pe.wait_ge(z_free, st["z"])
                mm(Z[:, 0:S], mean_w[:], acc[:], start=True, stop=True)
                for n in range(NB):
                    i = mm(Z[:, 512 + n:513 + n], acc[:, P * n:P * n + P], mean_w[:, 0:1], start=True, stop=True)
                i.then_inc(z_done, 1)

            stats = [0]
            pe.wait_ge(const_ready, 1)
            pe.wait_ge(par_landed, 16 * len(params))
            nc.tensor.transpose(Z[:, 0:GROWS], grow[:], ident[0:GROWS, 0:GROWS]).then_inc(gain_done, 1)
            pe.wait_ge(in_landed, 16 * NB)
            for kt in range(KT):
                o = begin(kt)
                for n in range(NB):
                    i = nc.tensor.transpose(o[:, P * n:P * n + P], xin[:, n, P * kt:P * kt + P], ident[:])
                i.then_inc(psum_done, 1)
            pe.wait_ge(gain_ready, 1)

            def swa_qk(st):
                h = st["h"]
                j, g, b = h // 2, h // 4, 64 * (h % 2)
                q = [s for s in plan["attn"] if s["kind"] == "q" and s["j"] == j][0]
                pe.wait_ge(result_taken, q["r"] + 1)
                pe.wait_ge(z_free, st["z"])
                rows_ = slice(b, b + 64)
                for n in range(NB):
                    k0 = max(n - 1, 0) * P
                    o0 = 256 * n + (P if n == 0 else 0)
                    i = mm(Z[:, o0:256 * n + 256], q0[rows_, j % 4, P * n:P * n + P], kd[rows_, g, k0:P * n + P], start=True, stop=True)
                i.then_inc(z_done, 1)

            def swa_t(st):
                h = st["h"]
                pe.wait_ge(p_ready, h + 1)
                if st["p0"]:
                    pe.wait_ge(p0_free, st["p0"])
                for k in range(4):
                    i = nc.tensor.transpose(PP[:, 0, P * k:P * k + P], pr[:, h % 3, P * k:P * k + P], ident[:])
                i.then_inc(p0_done, 1)
                if st["p1"]:
                    pe.wait_ge(p1_free, st["p1"])
                for k in range(3):
                    i = nc.tensor.transpose(PP[:, 1, P * k:P * k + P], pr[:, h % 3, 512 + P * k:640 + P * k], ident[:])
                i.then_inc(p1_done, 1)

            def swa_pv(st):
                h = st["h"]
                g, b = h // 4, 64 * (h % 2)
                pe.wait_ge(p0_free, st["p0"] + 1)
                pe.wait_ge(p1_free, st["p1"] + 1)
                if h % 2 == 0 and st["o"]:
                    pe.wait_ge(o_free, st["o"])
                for n in range(NB):
                    w = 256 if n < NB - 1 else P
                    i = mm(O[b:b + 64, P * n:P * n + w], v0[:, n, 64 * g:64 * g + 64], pt0[:, 256 * n:256 * n + w],
                           start=n == 0, stop=n == NB - 1, skip_group_check=True)
                if h % 2:
                    i.then_inc(o_done, 1)

            xg_base = {"sem": xg_ready, **{k: k + 1 for k in range(8)}}
            m_count = [0]
            for s in plan["attn"]:
                kind = s["kind"]
                s["src"] = "M"
                ready = None
                if s["t"] == 0:
                    ready = xg_base
                if kind == "out" and s["j"] == 0:
                    ready = {"sem": m_ready, **{k: k + 1 for k in range(8)}}
                parts = tile_parts(s, ready=ready)
                for half in range(2):
                    steps = [st for st in s["steps"] if st.get("half") == half]
                    for st in steps:
                        if st["op"] == "swa_qk":
                            swa_qk(st)
                    for st in steps:
                        if st["op"] == "swa_t":
                            swa_t(st)
                    parts[2 * half]()
                    parts[2 * half + 1]()
                    for st in steps:
                        if st["op"] == "swa_t":
                            swa_pv(st)
                for st in s["steps"]:
                    if st["op"] == "stat":
                        stat(st)
            for s in plan["pool"]:
                kind = s["kind"]
                s["src"] = "X"
                ready, kts = None, None
                if kind == "pu" and s["j"] == 0:
                    ready = {"sem": xg_ready, **{k: 8 + k + 1 for k in range(8)}}
                if kind == "mix" and s["j"] == 0:
                    pe.wait_ge(m_ready, 16)
                if kind == "out" and s["j"] == 0:
                    kts = [0, 2, 4, 6, 1, 3, 5, 7]
                    ready = {"sem": m_ready, **{c: 16 + n + 1 for n, c in enumerate(kts)}}
                for part in tile_parts(s, kts=kts, ready=ready):
                    part()
                for st in s["steps"]:
                    stat(st)
            stat(plan["mid_stat"])

            def pair_slot(l, kind, j):
                return [s for s in plan["layer", l] if s["kind"] == kind and s["j"] == j][0]

            def qk_step(st, l):
                df = st["op"] == "df_qk"
                name = "df" if df else "sb"
                j, b = (st["h"], 64 * st["m"]) if df else (st["h"] // 2, 64 * (st["h"] % 2))
                pe.wait_ge(result_taken, pair_slot(l, name + "q", j)["r"] + 1)
                pe.wait_ge(z_free, st["z"])
                rows_ = slice(b, b + 64)
                for c, (_, _, blocks) in enumerate(CHUNKS):
                    for n in blocks:
                        z0, w = ZOFF[n], P * (n + 1)
                        i = mm(Z[:, z0:z0 + w], qk[name + "q"][rows_, j, P * n:P * n + P], qk[name + "k"][rows_, j, 0:w],
                               start=True, stop=True)
                        if not df:
                            i = mm(Z[:, z0 + w - P:z0 + w], identb[:], mask_sb[:], start=False, stop=True, skip_group_check=True)
                    if not df:
                        i.then_inc(z_done, 1)
                if df:
                    i.then_inc(z_done, 1)

            def t_src(st):
                return cc[:] if st["df"] else ea[:, 1 + st["h"] % 2, :]

            def t1(st, l):
                w = t_src(st)
                if st["df"]:
                    pe.wait_ge(dfw_ready, 4 * l + st["h"] + 1)
                else:
                    pe.wait_ge(w_ready, 3 * (8 * l + st["h"]) + 3)
                pe.wait_ge(p0_free, st["p0"])
                for k in range(4):
                    i = nc.tensor.transpose(PP[:, 0, P * k:P * k + P], w[:, P * k:P * k + P], ident[:])
                i.then_inc(p0_done, 1)
                pe.wait_ge(p1_free, st["p1"])
                for k in range(4):
                    i = nc.tensor.transpose(PP[:, 1, P * k:P * k + P], w[:, 512 + P * k:640 + P * k], ident[:])
                i.then_inc(p1_done, 1)

            def t2(st):
                w = t_src(st)
                pe.wait_ge(p0_free, st["p0"] + 1)
                for k in range(2):
                    i = nc.tensor.transpose(PP[:, 0, P * k:P * k + P], w[:, 1024 + P * k:1152 + P * k], ident[:])
                i.then_inc(p0_done, 1)

            def pv(st, l):
                h = st["h"]
                pe.wait_ge(p0_free, st["p0"] + 2)
                pe.wait_ge(p1_free, st["p1"] + 1)
                last_v = pair_slot(l, "dfv" if st["df"] else "sbv", 1 + 2 * (h // (2 if st["df"] else 4)))
                pe.wait_ge(result_taken, last_v["r"] + 2)
                if st["df"] or h % 2 == 0:
                    pe.wait_ge(o_free, st["o"])
                if st["df"]:
                    for n in range(NB):
                        for k in range(n + 1):
                            i = mm(O[:, P * n:P * n + P], pt[:, k, P * n:P * n + P], qk["dfv"][:, k, P * h:P * h + P],
                                   start=k == 0, stop=k == n)
                    i.then_inc(o_done, 1)
                else:
                    b = 64 * (h % 2)
                    for k in range(NB):
                        i = mm(O[b:b + 64, P * k:S], qk["sbv"][:, k, 64 * h:64 * h + 64], pt[:, k, P * k:S],
                               start=k == 0, stop=k == NB - 1, skip_group_check=True)
                    if h % 2:
                        i.then_inc(o_done, 1)

            def df_f(st, l):
                pe.wait_ge(od_ready, 4 * l + st["h"] + 1)
                pe.wait_ge(p0_free, st["p0"])
                for n in range(NB):
                    i = nc.tensor.transpose(PP[:, 0, P * n:P * n + P], tb[:, 1, P * n:P * n + P], ident[:])
                i.then_inc(p0_done, 1)

            m_seen = 24
            for l in range(DEPTH):
                for s in plan["layer", l]:
                    ready = None
                    if s["kind"] == "dfk" and s["j"] == 0:
                        ready = {"sem": xg_ready, **{k: 16 + 16 * l + k + 1 for k in range(8)}}
                    if s["kind"] == "wo" and s["j"] == 0:
                        ready = {k: m_seen + [1, 2, 3, 4][k] for k in range(4)}
                    if s["kind"] == "wo" and s["j"] == 4:
                        ready = {k: m_seen + 4 + k + 1 for k in range(4)}
                    parts = tile_parts(s, ready=ready)
                    ts = [st for st in s["steps"] if st["op"] == "t"]
                    for st in s["steps"]:
                        if st["op"] in ("sb_qk", "df_qk"):
                            qk_step(st, l)
                    parts[0]()
                    parts[1]()
                    for st in s["steps"]:
                        if st["op"] == "df_f":
                            df_f(st, l)
                    for st in ts:
                        t1(st, l)
                    parts[2]()
                    for st in ts:
                        t2(st)
                    parts[3]()
                    for st in ts:
                        pv(st, l)
                    for st in s["steps"]:
                        if st["op"] == "stat":
                            stat(st)
                stat(plan["ff_stat", l])
                m_seen += 8
                t0, r0 = plan["ff", l]
                pe.wait_ge(xg_ready, 16 + 16 * l + 16)
                with pe.Fori(0, BLOCKS) as b:
                    for i in range(16):
                        t, r = t0 + i, r0 + i
                        pe.wait_ge(lo_done, b * 16 + (t + 1))
                        o = begin(r, b)
                        for k in range(KT):
                            if i == 8:
                                pe.wait_ge(m_ready, b * 8 + (m_seen + k + 1))
                            h_, l_ = (XH, XL) if i < 8 else (MH, ML)
                            c = slice(P * k, P * k + P)
                            last = three(o, WH[:, t % 4, c], WL[:, t % 4, c], h_[:, k, :], l_[:, k, :], k == 0, k == KT - 1)
                        last.then_inc(psum_done, 1)
                m_seen += 8 * BLOCKS
            pe.wait_ge(xt_ready, 2 * KT)
            stat(plan["last_stat"])
            for n in range(NB):
                for half in range(2):
                    r = plan["last_r"] + 2 * n + half
                    o = begin(r)
                    for k in range(4):
                        i = nc.tensor.transpose(o[:, P * k:P * k + P], xf[:, 4 * half + k, P * n:P * n + P], ident[:])
                    i.then_inc(psum_done, 1)


INPUTS = ["x", "norm_g", "attn_w_in", "attn_sinks", "attn_w_out", "pool_w_in", "pool_w_mix", "pool_scale",
          "pool_w_out", "final_g", "w_in_2", "w_o_2", "attn_norm_2", "subln_norm_2", "lam_q1_2", "lam_k1_2",
          "lam_q2_2", "lam_k2_2", "mlp_norm_2", "w_ff1_2", "w_ff2_2", "final_norm_2"]


def kernel(**inputs):
    import numpy as np
    import concourse.bacc as bacc
    from concourse.bass_utils import run_bass_kernel_spmd as run

    nc = bacc.Bacc("TRN2", target_bir_lowering=False, num_devices=1)
    arrays, args = {}, []
    for name in INPUTS:
        a = np.ascontiguousarray(inputs[name])
        arrays["in_" + name] = a
        args.append(nc.dram_tensor("in_" + name, a.shape, mybir.dt.from_np(a.dtype), kind="ExternalInput").ap())
    freq = (1.0 / (np.float32(10000.0) ** (np.arange(0, 64, 2, dtype=np.float32) / np.float32(64)))).astype(np.float32)
    angle = (freq[:, None] * np.arange(512, dtype=np.float32)[None, :]).astype(np.float32)
    cos, sin = np.cos(angle), np.sin(angle)
    table = np.stack([np.concatenate([cos] * 4), np.concatenate([-sin, sin] * 2)], axis=1).astype(np.float32)
    table = np.ascontiguousarray(table)
    arrays["in_rope_table"] = table
    args.append(nc.dram_tensor("in_rope_table", table.shape, mybir.dt.float32, kind="ExternalInput").ap())
    args.append(nc.dram_tensor("out_x", inputs["x"].shape, mybir.dt.float32, kind="ExternalOutput").ap())
    build(nc, *args)
    return run(nc, [arrays], core_ids=[0]).results[0]["out_x"]
```

```python
import math
from contextlib import ExitStack

import concourse.bass as bass
from concourse import mybir

F32 = mybir.dt.float32
F32R = mybir.dt.float32r
BF16 = mybir.dt.bfloat16
ALU = mybir.AluOpType
ACT = mybir.ActivationFunctionType

P = 128
EPS = 1e-6
NEG = -1e30


class Tally:

    def __init__(self):
        self.n = {}

    def take(self, name, k=1):
        before = self.n.get(name, 0)
        self.n[name] = before + k
        return before


def make_plan(depth):
    tally = Tally()

    def slot(kind, j, results, **more):
        return dict(kind=kind, j=j, t=tally.take("t"), r=tally.take("r", results), n=results, steps=[], **more)

    def use(**step):
        k = step["op"]
        if k in ("swa_qk", "df_qk", "sb_qk", "stat"):
            step["z"] = tally.take("z")
            step["zd"] = tally.take("z_done", 3 if k == "sb_qk" else 1)
        if k in ("swa_t", "t", "df_f"):
            step["p0"] = tally.take("p0", 2 if k == "t" else 1)
        if k in ("swa_t", "t"):
            step["p1"] = tally.take("p1")
        if k == "swa_t" and step["h"] % 2 == 0 or k == "t" and (step["df"] or step["h"] % 2 == 0):
            step["o"] = tally.take("o")
        elif k in ("swa_t", "t"):
            step["o"] = tally.n["o"] - 1
        return step

    plan = {}
    tally.take("r", 8)
    attn = [slot("k", j, 1) for j in range(2)] + [slot("v", j, 2) for j in range(2)]
    attn += [slot("q", j, 1) for j in range(8)] + [slot("z", j, 1) for j in range(8)]
    attn += [slot("out", j, 1) for j in range(8)]
    plan["attn"] = attn
    for s in attn:
        s["operand"] = "M" if s["kind"] == "out" else "X"
    attn[0]["steps"].append(use(op="stat"))
    for i in range(18):
        s = attn[6 + i // 2]
        if i < 16:
            s["steps"].append(use(op="swa_qk", h=i, half=i % 2))
        if i >= 2:
            s["steps"].append(use(op="swa_t", h=i - 2, half=i % 2))
    pool = [slot("pu", j, 1) for j in range(8)] + [slot("pz", j, 1) for j in range(8)]
    pool += [slot("mix", j, 4) for j in range(2)] + [slot("out", j, 1) for j in range(8)]
    plan["pool"] = pool
    for s in pool:
        s["operand"] = "M" if s["kind"] == "mix" else "X"
    pool[0]["steps"].append(use(op="stat"))
    for l in range(depth):
        s = []
        for name in ("df", "df", "sb", "sb"):
            half = len(s) // 6 % 2
            s += [slot(name + "k", 2 * half + j, 1) for j in range(2)]
            s += [slot(name + "q", 2 * half + j, 1) for j in range(2)]
            s += [slot(name + "v", 2 * half + j, 2) for j in range(2)]
        s += [slot("wo", j, 2, second=j >= 4) for j in range(8)]
        plan["layer", l] = s
        for x in s:
            x["operand"] = "X" if x["kind"] == "wo" else "M"
        s[0]["steps"].append(use(op="stat", mid=l == 0))
        if l == 0:
            s[4]["steps"].append(use(op="stat", res=True))
        todo = {}
        for d in range(4):
            at = 6 * (1 + d // 2) + 2 * (d % 2)
            for m in range(2):
                todo.setdefault(at + m, []).append(dict(op="df_qk", h=d, m=m))
            todo.setdefault(at + 2, []).append(dict(op="t", h=d, df=True))
            todo.setdefault(at + 3, []).append(dict(op="df_f", h=d))
        for h in range(8):
            todo.setdefault(18 + h, []).append(dict(op="sb_qk", h=h))
            todo.setdefault(19 + h, []).append(dict(op="t", h=h, df=False))
            if h % 2:
                todo.setdefault(20 + h, []).append(dict(op="sb_o", h=h))
        order = ["sb_qk", "df_qk", "df_f", "t", "sb_o"]
        for k in sorted(todo):
            for step in sorted(todo[k], key=lambda x: order.index(x["op"])):
                s[k]["steps"].append(use(**step))
        for step in [st for x in s for st in x["steps"] if st["op"] == "sb_o"]:
            step["o"] = [st["o"] for x in s for st in x["steps"] if st["op"] == "t" and not st["df"] and st["h"] == step["h"]][0]
        plan["ff_stat", l] = use(op="stat")
        plan["ff", l] = (tally.take("t", 64), tally.take("r", 64))
    plan["last_stat"] = use(op="stat")
    plan["o"] = tally.n["o"]
    plan["tiles"] = tally.n["t"]
    return plan


def build(nc, x, norm_g, attn_w_in, attn_sinks, attn_w_out, pool_w_in, pool_w_mix, pool_scale,
          pool_w_out, final_g, w_in_2, w_o_2, attn_norm_2, subln_norm_2, lam_q1_2, lam_k1_2,
          lam_q2_2, lam_k2_2, mlp_norm_2, w_ff1_2, w_ff2_2, final_norm_2, rope_table, out):
    S, D = x.shape[1], x.shape[2]
    KT = D // P
    NB = S // P
    DEPTH = w_in_2.shape[0]
    FF = w_ff1_2.shape[2]
    BLOCKS = FF // D
    plan = make_plan(DEPTH)
    LAST_T = plan["tiles"]
    NS = S + NB
    POOL_W = (2, 4, 8, 16)
    PAD = max(POOL_W)
    ZOFF = {3: 0, 2: 512, 0: 896, 1: 1024}
    CHUNKS = [(0, 512, [3]), (512, 512, [2, 0]), (1024, 256, [1])]
    G_NORM, G_FINAL, G_SCALE, G_ATTN, G_MLP, G_LAST, G_SUB = 0, 16, 24, 32, 48, 64, 72
    GROWS = G_SUB + DEPTH
    G_MID = GROWS

    with ExitStack() as ctx:
        def sb(name, shape, dt=F32, c=ctx):
            return c.enter_context(nc.sbuf_tensor(name, shape, dt))

        def sem(name):
            return ctx.enter_context(nc.semaphore(name))

        xT = sb("xT", [P, KT, S])
        XH, XL = sb("XH", [P, KT, S], F32R), sb("XL", [P, KT, S], F32R)
        MH, ML = sb("MH", [P, KT, S], F32R), sb("ML", [P, KT, S], F32R)
        operands = {"X": (XH, XL), "M": (MH, ML)}
        raw = sb("raw", [P, 2, KT * 256])
        WH, WL = sb("WH", [P, 4, KT * P], F32R), sb("WL", [P, 4, KT * P], F32R)
        ident = sb("ident", [P, P])
        identb = sb("identb", [P, P], BF16)
        ones = sb("ones", [P, 1])
        mean_w = sb("mean_w", [P, P])
        eps_w = sb("eps_w", [P, P])
        mask_sw = sb("mask_sw", [P, 256])
        mask_sb = sb("mask_sb", [P, P], BF16)
        mask_df = sb("mask_df", [P, 512])
        inv_n = sb("inv_n", [P, PAD])
        grow = sb("grow", [GROWS, P])
        gain = sb("gain", [P, GROWS + KT])
        sink = sb("sink", [P, 16])
        lamw = sb("lamw", [P, 64])
        lamd = sb("lamd", [P, 2 * DEPTH])
        lame = sb("lame", [P, 2 * DEPTH])
        neglam = sb("neglam", [P, DEPTH])
        sq = sb("sq", [P, 2, S])
        acc = sb("acc", [P, S])
        rstd, res_rstd, nt = sb("rstd", [P, NS]), sb("res_rstd", [P, NS]), sb("nt", [P, NS])
        small = sb("small", [P, 64])
        tb = sb("tb", [P, 2, S])
        lamv = tb[:, 0, 0:4 * DEPTH * 64].rearrange("p (v n) -> p v n", v=4)

        U = ctx.enter_context(nc.psum_tensor("U", [P, 2, 512], F32))
        Z = ctx.enter_context(nc.psum_tensor("Z", [P, 1536], F32))
        PP = ctx.enter_context(nc.psum_tensor("PP", [P, 2, 512], F32))
        O = ctx.enter_context(nc.psum_tensor("O", [P, 512], F32))

        a0 = ExitStack()
        xin = sb("xin", [P, NB, D], c=a0)
        oraw = xin[:].rearrange("p a (b s) -> p (a b) s", s=S)
        q0 = sb("q0", [P, 4, S], c=a0)
        kd = sb("kd", [P, 4, S], c=a0)
        v0 = sb("v0", [P, NB, 256], c=a0)
        pr = sb("pr", [P, 3, 896], c=a0)
        pt0 = sb("pt0", [P, 896], c=a0)
        a0.close()
        a1 = ExitStack()
        pad = sb("pad", [P, 6, PAD + S], c=a1)
        pf = sb("pf", [P, 2, S], c=a1)
        sz = sb("sz", [P, KT, S], c=a1)
        acc_mid = sb("acc_mid", [P, S], c=a1)
        a1.close()
        a2 = ExitStack()
        keys, queries, values = (sb(n, [P, 4, S], c=a2) for n in ("keys", "queries", "values"))
        qk = {"dfk": keys, "dfq": queries, "dfv": values, "sbk": keys, "sbq": queries, "sbv": values}
        cs = sb("cs", [P, 2, S], c=a2)
        ea = sb("ea", [P, 3, 1280], c=a2)
        cc = sb("cc", [P, 1280], c=a2)
        pt = sb("pt", [P, 4, S], c=a2)
        a2.close()
        a3 = ExitStack()
        xf = sb("xf", [P, KT, S], c=a3)
        yrow = sb("yrow", [P, NB, D], c=a3)
        a3.close()

        in_landed, gains_landed, par_landed = sem("in_landed"), sem("gains_landed"), sem("par_landed")
        raw_landed = [sem("raw_landed0"), sem("raw_landed1")]
        hi_done, lo_done = sem("hi_done"), sem("lo_done")
        cs_landed, rope_shifted, rope_done = sem("cs_landed"), sem("rope_shifted"), sem("rope_done")
        psum_done, result_taken = sem("psum_done"), sem("result_taken")
        const_ready, const_f = sem("const_ready"), sem("const_f")
        gain_done, gain_ready = sem("gain_done"), sem("gain_ready")
        lam_dot, lam_exp = sem("lam_dot"), sem("lam_exp")
        xh_ready, xg_ready = sem("xh_ready"), sem("xg_ready")
        xt_ready, scaled = sem("xt_ready"), sem("scaled")
        sq_ready, acc_done = sem("sq_ready"), sem("acc_done")
        stat_y, sub_v, sub_y, dfw_ready = sem("stat_y"), sem("sub_v"), sem("sub_y"), sem("dfw_ready")
        z_done, z_free = sem("z_done"), sem("z_free")
        p0_done, p0_free = sem("p0_done"), sem("p0_free")
        p1_done, p1_free = sem("p1_done"), sem("p1_free")
        o_done, o_free = sem("o_done"), sem("o_free")
        negm_ready, exp_done, p_ready = sem("negm_ready"), sem("exp_done"), sem("p_ready")
        gate_e, gate_o, zo_ready, pair_ready = sem("gate_e"), sem("gate_o"), sem("zo_ready"), sem("pair_ready")
        mh_ready, m_ready = sem("mh_ready"), sem("m_ready")
        sbl_ready, sbd_ready, w_ready = sem("sbl_ready"), sem("sbd_ready"), sem("w_ready")
        ss_ready, od_ready, f_hi = sem("ss_ready"), sem("od_ready"), sem("f_hi")
        u_sq = sem("u_sq")
        dve_step, act_step = sem("dve_step"), sem("act_step")
        y_done, y_dve, y_act, rstd_done = sem("y_done"), sem("y_dve"), sem("y_act"), sem("rstd_done")
        stored = sem("stored")

        freed, wo_tiles = {}, set()
        for name, part in plan.items():
            if name in ("attn", "pool") or name[0] == "layer":
                for s in part:
                    freed[s["t"]] = s["r"] + s["n"] * (2 if s["kind"][-1] == "v" and s["t"] % 2 == 0 else 1)
                    if s["kind"] == "wo":
                        wo_tiles.add(s["t"])
            elif name[0] == "ff":
                for i in range(16 * BLOCKS):
                    freed[part[0] + i] = part[1] + i + 1
        all_steps = [st for n, part in plan.items() if n in ("attn", "pool") or n[0] == "layer" for s in part for st in s["steps"]]
        all_stats = [st for st in all_steps if st["op"] == "stat"] + [p for n, p in plan.items() if "stat" in n or "stat" in n[0]]
        all_stats.sort(key=lambda st: st["zd"])
        NORMS = 3 + 2 * DEPTH
        MID = 2
        squares = [KT * (2 if s == MID else 1) for s in range(NORMS)]
        sums = [n - (s == NORMS - 1) for s, n in enumerate(squares)]
        swa_t_of = {st["h"]: st for st in all_steps if st["op"] == "swa_t"}

        def raw_view(t):
            k = 4 if t in wo_tiles else 8
            n = 4 * 256 // k
            return raw[:, t // 2 % 2, :].rearrange("p (k n) -> p k n", k=k)[:, :, n * (t % 2):n * (t % 2) + n], k

        def w_slot(w, t, k):
            return w[:, t % 4, :].rearrange("p (k n) -> p k n", k=k)

        def y_bank(m):
            return [PP[:, 0, :], PP[:, 1, :], O[:], Z[:, 0:512], Z[:, 1024:1536], U[:, 0, :], U[:, 1, :], PP[:, 0, :]][m]

        def rev(ap, z0, z1):
            return ap[:, z0:z1][:, ::-1]

        def rows(w, c0, n=256):
            return w[:, c0:c0 + n].rearrange("(k p) n -> p k n", p=P)

        def pair_sources():
            w = attn_w_in[0]
            cols = [1024, 1280] + [256 * i for i in range(4)] + [1536 + 256 * i for i in range(4)]
            out_ = [rows(w, c) for c in cols]
            out_ += [rows(attn_w_out[0], 256 * i) for i in range(4)]
            out_ += [rows(pool_w_in[0], 256 * i) for i in range(8)]
            out_ += [pool_w_mix[0].rearrange("g (k p) n -> p (g k) n", p=P)]
            out_ += [rows(pool_w_out[0], 256 * i) for i in range(4)]
            layers = []
            for l in range(DEPTH):
                w = w_in_2[l]
                dfq, sbq, third = 1536, 0, 512
                pairs = []
                for base in (dfq, sbq):
                    for half in range(2):
                        pairs += [rows(w, base + a * third + 256 * half) for a in (1, 0, 2)]
                for r0 in (512, 0):
                    pairs += [w_o_2[l][r0:r0 + 512, c:c + 512].rearrange("(k p) n -> p k n", p=P) for c in (0, 512)]
                layers.append(pairs)
            return out_, layers

        gains = [(grow[G_NORM:G_NORM + 16, :], norm_g.rearrange("l (k p) -> (l k) p", p=P)),
                  (grow[G_FINAL:G_FINAL + 8, :], final_g.rearrange("(k p) -> k p", p=P)),
                  (grow[G_SCALE:G_SCALE + 8, :], pool_scale.rearrange("l (k p) -> (l k) p", p=P)),
                  (grow[G_ATTN:G_ATTN + 16, :], attn_norm_2.rearrange("l (k p) -> (l k) p", p=P)),
                  (grow[G_MLP:G_MLP + 16, :], mlp_norm_2.rearrange("l (k p) -> (l k) p", p=P)),
                  (grow[G_LAST:G_LAST + 8, :], final_norm_2.rearrange("(k p) -> k p", p=P)),
                  (grow[G_SUB:G_SUB + DEPTH, :], subln_norm_2)]
        common = [(sink[:], attn_sinks[0].partition_broadcast(P))]
        common += [(lamv[:, i, :], v.rearrange("l d -> (l d)").partition_broadcast(P))
                   for i, v in enumerate((lam_q1_2, lam_k1_2, lam_q2_2, lam_k2_2))]

        block = ctx.enter_context(nc.Block())

        @block.sync
        def _(sp):
            for s in range(NB):
                sp.dma_start(xin[:, s, :], x[0, s * P:(s + 1) * P, :]).then_inc(in_landed, 16)
                if s:
                    dst, src = gains[3 + s]
                    sp.dma_start(dst, src).then_inc(gains_landed, 16)
            pairs, layers = pair_sources()

            def load(p, src, phase, parity):
                if phase is not None:
                    sp.wait_ge(lo_done, phase)
                k = src.shape[1]
                dst = raw[:, parity, :].rearrange("p (k n) -> p k n", k=k)
                sp.dma_start(dst, src).then_inc(raw_landed[parity], 16)

            p = 0
            for src in pairs[:2]:
                load(p, src, None, p % 2)
                p += 1
            for src in pairs[2:]:
                load(p, src, 2 * p - 2, p % 2)
                p += 1
            for l in range(DEPTH):
                for src in layers[l]:
                    load(p, src, 2 * p - 2, p % 2)
                    p += 1
                with sp.Fori(0, BLOCKS) as b:
                    for i in range(8):
                        if i < 4:
                            src = w_ff1_2[l][:, bass.ds(b * D + 256 * i, 256)].rearrange("(k p) n -> p k n", p=P)
                        else:
                            c = 256 * (i - 4)
                            src = w_ff2_2[l][bass.ds(b * D, D), c:c + 256].rearrange("(k p) n -> p k n", p=P)
                        load(None, src, b * 16 + (2 * (p + i) - 2), (p + i) % 2)
                p += 8 * BLOCKS
            for m in range(2 * NB):
                n, c = m % NB, slice(512 * (m // NB), 512 * (m // NB) + 512)
                sp.wait_ge(y_act if m % 2 else y_dve, m // 2 + 1)
                sp.dma_start(out[0, n * P:(n + 1) * P, c], yrow[:, n, c]).then_inc(stored, 16)
            sp.wait_ge(stored, 16 * 2 * NB)

        @block.gpsimd
        def _(pool):
            g = nc.gpsimd
            g.memset(ident[:], 0.0)
            g.memset(identb[:], 0.0)
            g.memset(ones[:], 1.0)
            g.memset(mean_w[:], 1.0 / D)
            g.memset(eps_w[:], EPS / D)
            g.memset(mask_sw[:], 0.0)
            g.memset(mask_sb[:], 0.0)
            g.memset(mask_df[:], 0.0)
            for s in range(PAD):
                last = g.memset(inv_n[:, s:s + 1], 1.0 / (s + 1))
            last.then_inc(const_f, 1)
            pool.wait_ge(const_f, 1)
            g.memset(mask_df[0:64, 448:512], NEG)
            for m in (ident, identb):
                g.affine_select(out=m[:], in_=m[:], compare_op=ALU.not_equal, fill=1.0, base=0,
                                pattern=[[-1, P]], channel_multiplier=1)
            g.affine_select(out=mask_sw[:, 0:P], in_=mask_sw[:, 0:P], compare_op=ALU.is_gt, fill=NEG,
                            base=0, pattern=[[1, P]], channel_multiplier=-1)
            g.affine_select(out=mask_sw[:, P:256], in_=mask_sw[:, P:256], compare_op=ALU.is_ge, fill=NEG,
                            base=0, pattern=[[-1, P]], channel_multiplier=1)
            g.affine_select(out=mask_sb[:], in_=mask_sb[:], compare_op=ALU.is_gt, fill=NEG,
                            base=0, pattern=[[-1, P]], channel_multiplier=1).then_inc(const_ready, 1)
            n = 0
            for s in range(NORMS):
                if s == 1:
                    for zs in [w for w in plan["attn"] if w["kind"] == "z"]:
                        pool.wait_ge(result_taken, zs["r"] + 1)
                        pool.wait_ge(o_free, zs["j"] + 1)
                        o = oraw[:, zs["j"], :]
                        g.tensor_tensor(o, tb[:, zs["j"] % 2, :], o, ALU.mult).then_inc(zo_ready, 1)
                if s == 2:
                    for us in [w for w in plan["pool"] if w["kind"] == "pu"]:
                        j = us["j"]
                        pool.wait_ge(result_taken, us["r"] + 1)
                        if j >= 2:
                            pool.wait_ge(gate_o, 8 + j - 1)
                        g.tensor_tensor(pad[:, 2 + j % 2, PAD:], pad[:, j % 2, PAD:], pad[:, j % 2, PAD - 1:PAD + S - 1],
                                        ALU.add).then_inc(pair_ready, 1)
                if s == MID + 1:
                    pool.wait_ge(rstd_done, 1)
                    pool.wait_ge(xg_ready, KT * s)
                    for kt in range(KT):
                        g.tensor_tensor(xT[:, kt, :], xT[:, kt, :], res_rstd[:, 0:S], ALU.mult).then_inc(scaled, 1)
                        pool.wait_ge(scaled, kt + 1)
                        g.tensor_tensor(xT[:, kt, :], xT[:, kt, :], gain[:, G_FINAL + kt:G_FINAL + kt + 1].to_broadcast([P, S]),
                                        ALU.mult).then_inc(xt_ready, 1)
                if s in (2, 4):
                    before = [w for w in plan["pool"] if w["kind"] == "out"][0]["r"] if s == 2 else plan["ff", 0][1]
                    pool.wait_ge(result_taken, before)
                    pool.dma_start(cs[:], rope_table).then_inc(cs_landed, 16)
                if s:
                    pool.wait_ge(z_done, all_stats[s - 1 if s <= MID else s]["zd"] + 1)
                for i in range(sums[s]):
                    pool.wait_ge(sq_ready, n + 1)
                    dst = acc_mid if s == MID and i % 2 else acc
                    ahead = 2 if s == MID else 1
                    if i < ahead:
                        g.tensor_scalar(dst[:], sq[:, n % 2, :], EPS * D / P if dst is acc else 0.0, None, ALU.add).then_inc(acc_done, 1)
                    else:
                        pool.wait_ge(acc_done, n + 1 - ahead)
                        g.tensor_tensor(dst[:], dst[:], sq[:, n % 2, :], ALU.add).then_inc(acc_done, 1)
                    n += 1

        @block.scalar
        def _(act):
            a = nc.scalar
            loop_r = [0]
            count = dict(step=0, hi=0, xh=0, sq=0, xt=0, negm=0, mh=0, stat=0, sbl=0, sbd=0, od=0, gate=0)

            def after(ins):
                count["step"] += 1
                ins.then_inc(act_step, 1)
                act.wait_ge(act_step, count["step"])

            def conv(t, loop=None):
                if loop is None:
                    if t >= LAST_T:
                        return
                    act.wait_ge(raw_landed[t // 2 % 2], 16 * (t // 4 + 1))
                    if t >= 4:
                        act.wait_ge(psum_done, freed[t - 4])
                else:
                    act.wait_ge(raw_landed[t // 2 % 2], loop * 64 + 16 * (t // 4 + 1))
                    act.wait_ge(psum_done, loop * 16 + (loop_r[0] + t - 3))
                src, shape = raw_view(t)
                a.activation(w_slot(WH, t, shape), src, ACT.Copy).then_inc(hi_done, 1)

            def prep(row, kt, r, first=False, dst=XH, mid=False):
                act.wait_ge(result_taken, r + 1)
                if row is not None:
                    if first:
                        act.wait_ge(gain_ready, 1)
                    a.activation(dst[:, kt, :], xT[:, kt, :], ACT.Copy, scale=gain[:, row + kt:row + kt + 1]).then_inc(xh_ready, 1)
                for i in range(2 if mid else 1):
                    n = count["sq"]
                    if n >= 2:
                        act.wait_ge(acc_done, n - 1)
                    kw = dict(scale=gain[:, G_FINAL + kt:G_FINAL + kt + 1]) if i else {}
                    a.activation(sq[:, n % 2, :], xT[:, kt, :], ACT.Square, **kw).then_inc(sq_ready, 1)
                    count["sq"] += 1

            def stat(st, c0=0):
                act.wait_ge(z_done, st["zd"] + 1)
                y = (res_rstd if st.get("res") else rstd)[:, c0:]
                after(a.activation(y, Z[:, c0:NS], ACT.Ln))
                a.activation(y, y, ACT.Exp, scale=-0.5).then_inc(stat_y, 1)

            def mh(src, j, dst=None, **kw):
                a.activation((dst or MH)[:, j, :], src, ACT.Copy, **kw).then_inc(mh_ready, 1)
                count["mh"] += 1

            def sigmoid(s):
                act.wait_ge(result_taken, s["r"] + 1)
                e = sq[:, s["j"] % 2, :]
                after(a.activation(e, tb[:, s["j"] % 2, :], ACT.Exp, scale=-1.0))
                after(a.activation(e, e, ACT.Ln, bias=1.0))
                a.activation(e, e, ACT.Exp, scale=-1.0).then_inc(gate_e, 1)

            def swa_exp(h):
                act.wait_ge(negm_ready, count["negm"] + 1)
                count["negm"] += 1
                sl = pr[:, h % 3, :]
                for n in range(NB):
                    lo_, hi_ = (0, P) if n == 0 else (256 * n - P, 256 * n + P)
                    a.activation(sl[:, lo_:hi_], sl[:, lo_:hi_], ACT.Exp, bias=small[:, 8 * (h % 2) + n:8 * (h % 2) + n + 1],
                                 accum_out=small[:, 16 + 8 * (h % 2) + n:17 + 8 * (h % 2) + n])
                a.activation(small[:, 20 + 8 * (h % 2):24 + 8 * (h % 2)], small[:, 8 * (h % 2):8 * (h % 2) + 4], ACT.Exp,
                             bias=sink[:, h:h + 1]).then_inc(exp_done, 1)

            def swa_steps(s, half):
                for st in s["steps"]:
                    if st.get("half") != half or st["op"] != "swa_t":
                        continue
                    act.wait_ge(p0_done, st["p0"] + 1)
                    a.activation(pt0[:, 0:512], PP[:, 0, :], ACT.Copy).then_inc(p0_free, 1)
                for st in s["steps"]:
                    if st.get("half") == half and st["op"] == "swa_qk":
                        swa_exp(st["h"])
                for st in s["steps"]:
                    if st.get("half") == half and st["op"] == "swa_t" and st["h"] % 2:
                        act.wait_ge(o_done, st["o"] + 1)
                        a.activation(oraw[:, st["h"] // 2, :], O[:], ACT.Copy).then_inc(o_free, 1)

            def t_first(st):
                act.wait_ge(p0_done, st["p0"] + 1)
                a.activation(pt[:, :, 384:512], PP[:, 0, :].rearrange("p (k q) -> p k q", q=P), ACT.Copy).then_inc(p0_free, 1)

            def layer_begin(s, l):
                late = any(st["op"] == "sb_qk" for st in s["steps"])
                if late:
                    conv(s["t"] + 2)
                for st in s["steps"]:
                    if st["op"] == "sb_o":
                        act.wait_ge(o_done, st["o"] + 1)
                        mh(O[:], st["h"] // 2, XH)
                    if st["op"] == "df_f":
                        d = st["h"]
                        act.wait_ge(o_done, [y["o"] for x in plan["layer", l] for y in x["steps"] if y["op"] == "t" and y["df"] and y["h"] == d][0] + 1)
                        act.wait_ge(dfw_ready, 4 * l + d + 1)
                        for n in range(NB):
                            i = a.activation(sq[:, 1, n * P:(n + 1) * P], O[:, n * P:(n + 1) * P], ACT.Square,
                                             scale=small[:, 24 + n:25 + n], accum_out=small[:, 40 + n:41 + n])
                        i.then_inc(ss_ready, 1)
                        act.wait_ge(sub_v, 4 * l + d + 1)
                        after(a.activation(small[:, 52:56], small[:, 44:48], ACT.Ln))
                        a.activation(small[:, 52:56], small[:, 52:56], ACT.Exp, scale=-0.5).then_inc(sub_y, 1)
                if not late:
                    conv(s["t"] + 2)
                for st in s["steps"]:
                    if st["op"] == "sb_qk":
                        for c, (c0, cn, _) in enumerate(CHUNKS):
                            act.wait_ge(z_done, st["zd"] + c + 1)
                            e = ea[:, 0, c0:c0 + cn]
                            after(a.activation(e, Z[:, c0:c0 + cn], ACT.Abs))
                            after(a.activation(e, e, ACT.Exp, scale=-1.0))
                            a.activation(e, e, ACT.Ln, bias=1.0).then_inc(sbl_ready, 1)
                    if st["op"] == "df_qk":
                        for other in s["steps"]:
                            if other["op"] == "t":
                                t_first(other)
                        act.wait_ge(negm_ready, count["negm"] + 1)
                        count["negm"] += 1
                        m = st["m"]
                        for n in range(NB):
                            r = ea[:, m, ZOFF[n]:ZOFF[n] + P * (n + 1)]
                            i = a.activation(r, r, ACT.Exp, bias=small[:, 4 * m + n:4 * m + n + 1],
                                             accum_out=small[:, 16 + 4 * m + n:17 + 4 * m + n])
                        i.then_inc(exp_done, 1)

            def layer_end(s, l):
                for st in s["steps"]:
                    if st["op"] == "df_f":
                        act.wait_ge(p0_done, st["p0"] + 1)
                        mh(PP[:, 0, :], 4 + st["h"], XH, scale=gain[:, G_SUB + l:G_SUB + l + 1])
                    if st["op"] == "t" and not any(x["op"] == "df_qk" for x in s["steps"]):
                        t_first(st)
                for st in s["steps"]:
                    if st["op"] == "sb_qk":
                        for c, (c0, cn, _) in enumerate(CHUNKS):
                            act.wait_ge(sbd_ready, count["sbd"] + 1)
                            count["sbd"] += 1
                            a.activation(ea[:, 1 + st["h"] % 2, c0:c0 + cn], ea[:, 1 + st["h"] % 2, c0:c0 + cn], ACT.Exp).then_inc(w_ready, 1)
                for st in s["steps"]:
                    if st["op"] == "t":
                        act.wait_ge(p0_done, st["p0"] + 2)
                        a.activation(pt[:, 0:2, 128:256], PP[:, 0, 0:256].rearrange("p (k q) -> p k q", q=P), ACT.Copy).then_inc(p0_free, 1)

            act.preload_act_table_set("natural_log_exp_and_others")
            for dst, src in gains[:4]:
                act.dma_start(dst, src).then_inc(gains_landed, 16)
            for dst, src in common:
                act.dma_start(dst, src).then_inc(par_landed, 16)
            for kt in range(KT):
                prep(G_NORM, kt, kt, True)
                if kt in (1, 4):
                    conv(kt // 4)
            act.wait_ge(lam_dot, 2 * DEPTH)
            a.activation(lame[:], lamd[:], ACT.Exp).then_inc(lam_exp, 1)
            for s in plan["attn"]:
                t, j = s["t"], s["j"]
                kind = s["kind"]
                conv(t + 2)
                for st in s["steps"]:
                    if st["op"] == "stat":
                        stat(st)
                for half in range(2):
                    swa_steps(s, half)
                if kind == "z":
                    if j:
                        act.wait_ge(gate_o, j)
                        mh(oraw[:, j - 1, :], j - 1)
                    sigmoid(s)
                    if j == 7:
                        act.wait_ge(gate_o, 8)
                        mh(oraw[:, 7, :], 7)
                if kind == "out":
                    prep(G_NORM + 8, j, s["r"])
            for s in plan["pool"]:
                t, j, kind = s["t"], s["j"], s["kind"]
                if kind != "mix":
                    conv(t + 2)
                for st in s["steps"]:
                    stat(st)
                if kind == "pu" and j or kind == "pz" and j == 0:
                    i = j - 1 if j else 7
                    act.wait_ge(gate_o, 8 + i + 1)
                    mh(pf[:, i % 2, :], i)
                if kind == "pz" and j < 7:
                    sigmoid(s)
                if kind == "mix":
                    if j == 0:
                        sigmoid(plan["pool"][15])
                    for i in range(4):
                        act.wait_ge(result_taken, s["r"] + i + 1)
                        mh(tb[:, i % 2, :], 2 * i + j, XH)
                        if i == 1:
                            conv(t + 2)
                if kind == "out":
                    prep(G_MID, j, s["r"], dst=MH, mid=True)
            for l in range(DEPTH):
                for s in plan["layer", l]:
                    t, j = s["t"], s["j"]
                    layer_begin(s, l)
                    for st in s["steps"]:
                        if st["op"] == "stat":
                            stat(st)
                    layer_end(s, l)
                    if s["kind"] in ("dfk", "dfq"):
                        act.wait_ge(psum_done, s["r"] + 1)
                        act.wait_ge(result_taken, s["r"])
                        for q in range(4):
                            o = q ^ 1
                            i = a.activation(tb[32 * q:32 * q + 32, 0, :], U[32 * o:32 * o + 32, s["r"] % 2, :], ACT.Copy)
                        i.then_inc(rope_shifted, 1)
                    if s["kind"] == "wo" and s["second"]:
                        for i in range(2):
                            prep(G_MLP + 8 * l, 2 * (j - 4) + i, s["r"] + i, dst=MH)
                t0, r0 = plan["ff", l]
                loop_r[0] = r0 - t0
                m0 = count["mh"]

                def ff_block(b, first=False, last=False):
                    for i in range(16):
                        if t0 + 16 * (BLOCKS - 1) + i + 2 < LAST_T or not last:
                            conv(t0 + i + 2, b)
                        if first and i == 0:
                            stat(plan["ff_stat", l])
                        if i < 8:
                            act.wait_ge(result_taken, b * 16 + (r0 + i + 1))
                            a.activation(sq[:, i % 2, :], tb[:, i % 2, :], ACT.Square).then_inc(u_sq, 1)
                            a.activation(XH[:, i, :], tb[:, i % 2, :], ACT.Square).then_inc(mh_ready, 1)
                        elif last:
                            prep(G_ATTN + 8 * (l + 1) if l < DEPTH - 1 else None, i - 8, r0 + 16 * b + i, dst=MH)

                ff_block(0, first=True)
                with act.Fori(1, BLOCKS - 1) as b:
                    ff_block(b)
                ff_block(BLOCKS - 1, last=True)
                count["mh"] += 8 * BLOCKS
            stat(plan["last_stat"], S)
            act.wait_ge(rstd_done, 2)
            for m in range(1, 2 * NB, 2):
                n, c = m % NB, 512 * (m // NB)
                act.wait_ge(y_done, m + 1)
                a.activation(yrow[:, n, c:c + 512], y_bank(m), ACT.Copy, scale=rstd[:, S + n:S + n + 1]).then_inc(y_act, 1)

        @block.vector
        def _(dve):
            v = nc.vector
            loop_r = [0]
            count = dict(step=0, xh=0, xg=0, exp=0, gate_e=0, mh=0, stat=0, sbl=0, usq=0, ss=0)

            def after(ins):
                count["step"] += 1
                ins.then_inc(dve_step, 1)
                dve.wait_ge(dve_step, count["step"])

            def conv(t, loop=None):
                if loop is None:
                    if t >= LAST_T:
                        return
                    dve.wait_ge(raw_landed[t // 2 % 2], 16 * (t // 4 + 1))
                    dve.wait_ge(hi_done, t + 1)
                    if t >= 4:
                        dve.wait_ge(psum_done, freed[t - 4])
                else:
                    dve.wait_ge(raw_landed[t // 2 % 2], loop * 64 + 16 * (t // 4 + 1))
                    dve.wait_ge(hi_done, loop * 16 + (t + 1))
                    dve.wait_ge(psum_done, loop * 16 + (loop_r[0] + t - 3))
                src, shape = raw_view(t)
                v.tensor_tensor(w_slot(WL, t, shape), src, w_slot(WH, t, shape).bitcast(F32), ALU.subtract).then_inc(lo_done, 1)

            def prep_lo(row, kt, to=(XH, XL)):
                count["xh"] += 1
                dve.wait_ge(xh_ready, count["xh"])
                v.scalar_tensor_tensor(out=to[1][:, kt, :], in0=xT[:, kt, :], scalar=gain[:, row + kt:row + kt + 1],
                                       in1=to[0][:, kt, :].bitcast(F32), op0=ALU.mult, op1=ALU.subtract).then_inc(xg_ready, 1)

            def stat(st, c0=0):
                count["stat"] += 1
                dve.wait_ge(z_done, st["zd"] + 1)
                dve.wait_ge(stat_y, count["stat"])
                y, t = (res_rstd if st.get("res") else rstd)[:, c0:], nt[:, c0:]
                after(v.scalar_tensor_tensor(out=t, in0=y, scalar=-0.5, in1=y, op0=ALU.mult, op1=ALU.mult))
                v.tensor_tensor(t, t, Z[:, c0:NS], ALU.mult).then_inc(z_free, 1)
                dve.wait_ge(z_free, st["z"] + 1)
                i = v.scalar_tensor_tensor(out=y, in0=t, scalar=1.5, in1=y, op0=ALU.add, op1=ALU.mult)
                if c0 == 0 and not st.get("res"):
                    after(i)
                else:
                    i.then_inc(rstd_done, 1)

            def result(r, loop=None, per=16):
                if loop is None:
                    dve.wait_ge(psum_done, r + 1)
                    if r:
                        dve.wait_ge(result_taken, r)
                else:
                    dve.wait_ge(psum_done, loop * per + (r + 1))
                    dve.wait_ge(result_taken, loop * per + r)
                return U[:, r % 2, :]

            def low(full, j, dst=None, hi=None):
                count["mh"] += 1
                dve.wait_ge(mh_ready, count["mh"])
                v.tensor_tensor((dst or ML)[:, j, :], full, (hi or MH)[:, j, :].bitcast(F32), ALU.subtract).then_inc(m_ready, 1)

            def swa_softmax_a(st):
                h = st["h"]
                sl = pr[:, h % 3, :]
                b = 8 * (h % 2)
                dve.wait_ge(z_done, st["zd"] + 1)
                if h >= 3:
                    dve.wait_ge(p0_done, swa_t_of[h - 3]["p0"] + 1)
                    dve.wait_ge(p1_done, swa_t_of[h - 3]["p1"] + 1)
                for n in range(NB):
                    lo_, hi_ = (0, P) if n == 0 else (256 * n - P, 256 * n + P)
                    i = v.tensor_tensor_reduce(sl[:, lo_:hi_], Z[:, P + lo_:P + hi_], mask_sw[:, (P if n == 0 else 0):256],
                                               1.0, sink[:, h:h + 1], ALU.add, ALU.max, small[:, 32 + b + n:33 + b + n])
                i.then_inc(z_free, 1)
                dve.wait_ge(z_free, st["z"] + 1)
                v.tensor_scalar(small[:, b:b + 4], small[:, 32 + b:36 + b], -1.0, None, ALU.mult).then_inc(negm_ready, 1)

            def swa_softmax_b(h):
                b = 8 * (h % 2)
                dve.wait_ge(exp_done, h + 1)
                after(v.tensor_tensor(small[:, 16 + b:20 + b], small[:, 16 + b:20 + b], small[:, 20 + b:24 + b], ALU.add))
                after(v.reciprocal(small[:, 36 + b:40 + b], small[:, 16 + b:20 + b]))
                for n in range(NB):
                    lo_, hi_ = (0, P) if n == 0 else (256 * n - P, 256 * n + P)
                    r = pr[:, h % 3, lo_:hi_]
                    i = v.tensor_scalar(r, r, small[:, 36 + b + n:37 + b + n], None, ALU.mult)
                i.then_inc(p_ready, 1)

            def swa_steps(s, half):
                for st in s["steps"]:
                    if st.get("half") == half and st["op"] == "swa_qk":
                        swa_softmax_a(st)
                for st in s["steps"]:
                    if st.get("half") == half and st["op"] == "swa_t":
                        dve.wait_ge(p1_done, st["p1"] + 1)
                        v.tensor_copy(pt0[:, 512:896], PP[:, 1, 0:384]).then_inc(p1_free, 1)
                        if st["h"] + 1 < 16:
                            swa_softmax_b(st["h"] + 1)
                    elif st.get("half") == half and st["op"] == "swa_qk" and st["h"] == 1:
                        swa_softmax_b(0)

            def layer_begin(s, l):
                for st in s["steps"]:
                    if st["op"] == "sb_o":
                        count["mh"] += 1
                        dve.wait_ge(mh_ready, count["mh"])
                        j = st["h"] // 2
                        v.tensor_tensor(XL[:, j, :], O[:], XH[:, j, :].bitcast(F32), ALU.subtract).then_inc(m_ready, 1)
                        dve.wait_ge(m_ready, count["mh"])
                        dve.sem_inc(o_free, 1)
                    if st["op"] == "df_f":
                        count["ss"] += 1
                        dve.wait_ge(ss_ready, count["ss"])
                        lam_init = 0.8 - 0.6 * math.exp(-0.3 * l)
                        after(v.tensor_scalar(small[:, 44:48], small[:, 40:44], 1.0 / P, EPS, ALU.mult, ALU.add))
                        v.tensor_copy(small[:, 48:52], small[:, 44:48]).then_inc(sub_v, 1)
                        dve.wait_ge(sub_v, count["ss"])
                        dve.wait_ge(sub_y, count["ss"])
                        after(v.tensor_tensor(small[:, 56:60], small[:, 52:56], small[:, 52:56], ALU.mult))
                        after(v.tensor_tensor(small[:, 56:60], small[:, 56:60], small[:, 44:48], ALU.mult))
                        after(v.tensor_scalar(small[:, 56:60], small[:, 56:60], -0.5, 1.5, ALU.mult, ALU.add))
                        after(v.tensor_tensor(small[:, 56:60], small[:, 56:60], small[:, 52:56], ALU.mult))
                        after(v.scalar_tensor_tensor(out=small[:, 56:60], in0=small[:, 56:60], scalar=1.0 - lam_init,
                                                     in1=small[:, 24:28], op0=ALU.mult, op1=ALU.mult))
                        for n in range(NB):
                            i = v.tensor_scalar(tb[:, 1, n * P:(n + 1) * P], O[:, n * P:(n + 1) * P], small[:, 56 + n:57 + n], None, ALU.mult)
                        i.then_inc(od_ready, 1)
                        dve.wait_ge(od_ready, count["ss"])
                        dve.sem_inc(o_free, 1)
                for st in s["steps"]:
                    if st["op"] == "df_qk":
                        m = st["m"]
                        dve.wait_ge(z_done, st["zd"] + 1)
                        if 4 * l + st["h"]:
                            dve.wait_ge(dfw_ready, 4 * l + st["h"])
                        for n in range(NB):
                            w = P * (n + 1)
                            i = v.tensor_tensor_reduce(ea[:, m, ZOFF[n]:ZOFF[n] + w], Z[:, ZOFF[n]:ZOFF[n] + w], mask_df[:, 512 - w:512],
                                                       1.0, -3.0e38, ALU.add, ALU.max, small[:, 32 + 4 * m + n:33 + 4 * m + n])
                        i.then_inc(z_free, 1)
                        dve.wait_ge(z_free, st["z"] + 1)
                        v.tensor_scalar(small[:, 4 * m:4 * m + 4], small[:, 32 + 4 * m:36 + 4 * m], -1.0, None, ALU.mult).then_inc(negm_ready, 1)
                    if st["op"] == "sb_qk":
                        if st["h"] == 0:
                            dve.wait_ge(dfw_ready, 4 * l + 4)
                        for c, (c0, cn, blocks) in enumerate(CHUNKS):
                            count["sbl"] += 1
                            dve.wait_ge(sbl_ready, count["sbl"])
                            e, z = ea[:, 0, c0:c0 + cn], Z[:, c0:c0 + cn]
                            after(v.scalar_tensor_tensor(out=e, in0=z, scalar=0.0, in1=e, op0=ALU.max, op1=ALU.add))
                            for n in blocks:
                                z0, z1 = ZOFF[n], ZOFF[n] + P * (n + 1)
                                i = v.tensor_tensor_scan(rev(cc, z0, z1), ones[:].to_broadcast([P, z1 - z0]), rev(ea[:, 0, :], z0, z1), 0.0, ALU.mult, ALU.add)
                            after(i)
                            v.tensor_tensor(ea[:, 1 + st["h"] % 2, c0:c0 + cn], z, cc[:, c0:c0 + cn], ALU.subtract).then_inc(sbd_ready, 1)
                        dve.wait_ge(sbd_ready, count["sbl"])
                        dve.sem_inc(z_free, 1)

            def layer_end(s, l):
                for st in s["steps"]:
                    if st["op"] == "df_qk":
                        count["exp"] += 1
                        dve.wait_ge(exp_done, 16 + count["exp"])
                        if st["m"] == 1:
                            after(v.reciprocal(small[:, 24:32], small[:, 16:24]))
                            after(v.scalar_tensor_tensor(out=small[:, 8:12], in0=small[:, 16:20], scalar=neglam[:, l:l + 1],
                                                         in1=small[:, 28:32], op0=ALU.mult, op1=ALU.mult))
                            for n in range(NB):
                                z0, z1 = ZOFF[n], ZOFF[n] + P * (n + 1)
                                i = v.scalar_tensor_tensor(out=cc[:, z0:z1], in0=ea[:, 1, z0:z1], scalar=small[:, 8 + n:9 + n],
                                                           in1=ea[:, 0, z0:z1], op0=ALU.mult, op1=ALU.add)
                            i.then_inc(dfw_ready, 1)
                for st in s["steps"]:
                    if st["op"] == "df_f":
                        count["mh"] += 1
                        dve.wait_ge(mh_ready, count["mh"])
                        j = 4 + st["h"]
                        v.scalar_tensor_tensor(out=XL[:, j, :], in0=PP[:, 0, :], scalar=gain[:, G_SUB + l:G_SUB + l + 1],
                                               in1=XH[:, j, :].bitcast(F32), op0=ALU.mult, op1=ALU.subtract).then_inc(m_ready, 1)
                        dve.wait_ge(m_ready, count["mh"])
                        dve.sem_inc(p0_free, 1)
                    if st["op"] == "t":
                        dve.wait_ge(p1_done, st["p1"] + 1)
                        v.tensor_copy(pt[:, 0:3, 256:384], PP[:, 1, 0:384].rearrange("p (k q) -> p k q", q=P))
                        v.tensor_copy(pt[:, 0, 0:128], PP[:, 1, 384:512]).then_inc(p1_free, 1)

            dve.wait_ge(gain_done, 1)
            v.tensor_copy(gain[:, 0:GROWS], Z[:, 0:GROWS]).then_inc(gain_ready, 1)
            dve.wait_ge(gain_ready, 1)
            v.tensor_tensor(gain[:, G_MID:G_MID + KT], gain[:, G_FINAL:G_FINAL + KT], gain[:, G_ATTN:G_ATTN + KT], ALU.mult)
            for kt in range(KT):
                ps = result(kt)
                v.tensor_copy(xT[:, kt, :], ps).then_inc(result_taken, 1)
                if kt:
                    prep_lo(G_NORM, kt - 1)
                if kt in (3, 6):
                    conv(kt // 6)
            dve.wait_ge(result_taken, KT)
            prep_lo(G_NORM, KT - 1)
            dve.wait_ge(par_landed, 16 * len(common))
            for l in range(DEPTH):
                for i in range(2):
                    c = slice(64 * l, 64 * l + 64)
                    v.tensor_tensor_reduce(lamw[:], lamv[:, 2 * i, c], lamv[:, 2 * i + 1, c], 1.0, 0.0, ALU.mult, ALU.add,
                                           lamd[:, 2 * l + i:2 * l + i + 1]).then_inc(lam_dot, 1)
                    dve.wait_ge(lam_dot, 2 * l + i + 1)
            dve.wait_ge(lam_exp, 1)
            for l in range(DEPTH):
                lam_init = 0.8 - 0.6 * math.exp(-0.3 * l)
                v.scalar_tensor_tensor(out=neglam[:, l:l + 1], in0=lame[:, 2 * l + 1:2 * l + 2], scalar=-lam_init,
                                       in1=lame[:, 2 * l:2 * l + 1], op0=ALU.add, op1=ALU.subtract)
            dve.wait_ge(const_ready, 1)

            def add_x(ps, kt, last, r):
                i = v.tensor_tensor(xT[:, kt, :], xT[:, kt, :], ps, ALU.add)
                i.then_inc(result_taken, 1)
                if last:
                    dve.wait_ge(result_taken, r + 1)

            def gated(i):
                dve.wait_ge(gate_e, i + 1)
                dve.wait_ge(zo_ready, i + 1)
                v.tensor_tensor(oraw[:, i, :], sq[:, i % 2, :], oraw[:, i, :], ALU.mult).then_inc(gate_o, 1)

            def silu_scale(i):
                dve.wait_ge(gate_e, 8 + i + 1)
                after(v.scalar_tensor_tensor(out=sz[:, i, :], in0=tb[:, i % 2, :], scalar=gain[:, G_SCALE + i:G_SCALE + i + 1],
                                             in1=sq[:, i % 2, :], op0=ALU.mult, op1=ALU.mult))

            for s in plan["attn"]:
                t, j, kind, r = s["t"], s["j"], s["kind"], s["r"]
                if kind == "z" and j:
                    gated(j - 1)
                    if j >= 2:
                        low(oraw[:, j - 2, :], j - 2)
                conv(t + 2)
                for st in s["steps"]:
                    if st["op"] == "stat":
                        stat(st)
                for half in range(2):
                    swa_steps(s, half)
                ps = result(r)
                rb = rstd[:, 0:S]
                if kind == "k":
                    for g in range(2):
                        src = slice(64 * g, 64 * g + 64)
                        for half in range(2):
                            i = v.tensor_tensor(kd[64 * half:64 * half + 64, 2 * j + g, :], U[src, r % 2, :], rstd[64 * half:64 * half + 64, 0:S], ALU.mult)
                    i.then_inc(result_taken, 1)
                elif kind == "v":
                    for i in range(2):
                        ps = result(r + i)
                        n = 2 * j + i
                        v.tensor_scalar(v0[:, n, :], ps[:, 0:256], rstd[:, S + n:S + n + 1], None, ALU.mult).then_inc(result_taken, 1)
                elif kind == "q":
                    v.scalar_tensor_tensor(out=q0[:, j % 4, :], in0=ps, scalar=0.125, in1=rb, op0=ALU.mult, op1=ALU.mult).then_inc(result_taken, 1)
                elif kind == "z":
                    v.tensor_tensor(tb[:, j % 2, :], ps, rb, ALU.mult).then_inc(result_taken, 1)
                    if j == 7:
                        low(oraw[:, 6, :], 6)
                        gated(7)
                        dve.wait_ge(gate_o, 8)
                        low(oraw[:, 7, :], 7)
                elif kind == "out":
                    add_x(ps, j, True, r)
                    prep_lo(G_NORM + 8, j)
            def pooled(j):
                w = POOL_W[j // 2]
                u = pad[:, j % 2, PAD:]
                dve.wait_ge(pair_ready, j + 1)
                dve.wait_ge(gate_o, 8 + j)
                src, sh = 2 + j % 2, 2
                while sh < w:
                    dst = 5 if src == 4 else 4
                    after(v.tensor_tensor(pad[:, dst, PAD:], pad[:, src, PAD:], pad[:, src, PAD - sh:PAD + S - sh], ALU.add))
                    src, sh = dst, 2 * sh
                head = pad[:, src, PAD:PAD + w]
                after(v.scalar_tensor_tensor(out=head, in0=head, scalar=float(w), in1=inv_n[:, 0:w], op0=ALU.mult, op1=ALU.mult))
                if j >= 2:
                    dve.wait_ge(m_ready, 8 + j - 1)
                v.scalar_tensor_tensor(out=pf[:, j % 2, :], in0=pad[:, src, PAD:], scalar=1.0 / w, in1=u,
                                       op0=ALU.mult, op1=ALU.subtract).then_inc(gate_o, 1)

            after(v.memset(pad[:, :, 0:PAD], 0.0))
            for s in plan["pool"]:
                t, j, kind, r = s["t"], s["j"], s["kind"], s["r"]
                i = j + 8 * (kind == "pz")
                if kind in ("pu", "pz") and 2 <= i <= 9:
                    low(pf[:, i % 2, :], i - 2)
                if kind in ("pu", "pz") and 1 <= i <= 8:
                    pooled(i - 1)
                if kind == "pz" and j:
                    silu_scale(j - 1)
                if kind != "mix":
                    conv(t + 2)
                for st in s["steps"]:
                    stat(st)
                ps = result(r)
                rb = rstd[:, 0:S]
                if kind == "pu":
                    v.tensor_tensor(pad[:, j % 2, PAD:], ps, rb, ALU.mult).then_inc(result_taken, 1)
                elif kind == "pz":
                    v.tensor_tensor(tb[:, j % 2, :], ps, rb, ALU.mult).then_inc(result_taken, 1)
                elif kind == "mix":
                    for i in range(4):
                        if i:
                            ps = result(r + i)
                        c = 2 * i + j
                        dve.wait_ge(m_ready, count["mh"])
                        v.tensor_tensor(tb[:, i % 2, :], ps, sz[:, c, :], ALU.mult).then_inc(result_taken, 1)
                        if i == 0 and j == 0:
                            silu_scale(7)
                        if i:
                            low(tb[:, (i - 1) % 2, :], c - 2, XL, XH)
                        if i == 1:
                            conv(t + 2)
                    dve.wait_ge(result_taken, r + 4)
                    low(tb[:, 1, :], 6 + j, XL, XH)
                elif kind == "out":
                    add_x(ps, j, True, r)
                    prep_lo(G_MID, j, (MH, ML))
            rope = [0]
            for l in range(DEPTH):
                for s in plan["layer", l]:
                    t, j, kind, r = s["t"], s["j"], s["kind"], s["r"]
                    first = any(st["op"] == "sb_qk" for st in s["steps"])
                    if first:
                        conv(t + 2)
                    layer_begin(s, l)
                    if not first:
                        conv(t + 2)
                    for st in s["steps"]:
                        if st["op"] == "stat" and not st.get("res"):
                            stat(st)
                            dve.wait_ge(cs_landed, 16 * (l + 1))
                            for i in range(2):
                                after(v.tensor_tensor(cs[:, i, :], cs[:, i, :], rstd[:, 0:S], ALU.mult))
                    layer_end(s, l)
                    ps = result(r)
                    rb = rstd[:, 0:S]
                    if kind in ("dfk", "dfq"):
                        rope[0] += 1
                        dve.wait_ge(rope_shifted, rope[0])
                        scale = 0.125 if kind == "dfq" else 1.0
                        v.scalar_tensor_tensor(out=qk[kind][:, j, :], in0=ps, scalar=scale, in1=cs[:, 0, :], op0=ALU.mult, op1=ALU.mult)
                        after(v.scalar_tensor_tensor(out=tb[:, 0, :], in0=tb[:, 0, :], scalar=scale, in1=cs[:, 1, :], op0=ALU.mult, op1=ALU.mult))
                        v.tensor_tensor(qk[kind][:, j, :], tb[:, 0, :], qk[kind][:, j, :], ALU.add).then_inc(result_taken, 1)
                    elif kind == "sbk":
                        v.tensor_tensor(qk[kind][:, j, :], ps, rb, ALU.mult).then_inc(result_taken, 1)
                    elif kind == "sbq":
                        v.scalar_tensor_tensor(out=qk[kind][:, j, :], in0=ps, scalar=0.125, in1=rb, op0=ALU.mult, op1=ALU.mult).then_inc(result_taken, 1)
                    elif kind in ("dfv", "sbv"):
                        for i in range(2):
                            if i:
                                ps = result(r + i)
                            n = 2 * (j % 2) + i
                            c = 256 * (j // 2)
                            v.tensor_scalar(qk[kind][:, n, c:c + 256], ps[:, 0:256], rstd[:, S + n:S + n + 1], None, ALU.mult).then_inc(result_taken, 1)
                    elif kind == "wo":
                        if l == 0 and j == 0:
                            dve.wait_ge(xt_ready, KT)
                        for i in range(2):
                            if i:
                                ps = result(r + i)
                            kt = 2 * (j % 4) + i
                            add_x(ps, kt, s["second"], r + i)
                            if s["second"]:
                                prep_lo(G_MLP + 8 * l, kt, (MH, ML))
                    for st in s["steps"]:
                        if st.get("res"):
                            stat(st)
                t0, r0 = plan["ff", l]
                loop_r[0] = r0 - t0
                m0 = count["mh"]
                u0 = count["usq"]

                def ff_block(b, first=False, last=False):
                    for i in range(16):
                        if t0 + 16 * (BLOCKS - 1) + i + 2 < LAST_T or not last:
                            conv(t0 + i + 2, b)
                        if first and i == 0:
                            stat(plan["ff_stat", l])
                        ps = result(r0 + i, b)
                        if i < 8:
                            v.scalar_tensor_tensor(out=tb[:, i % 2, :], in0=ps, scalar=0.0, in1=rstd[:, 0:S], op0=ALU.max,
                                                   op1=ALU.mult).then_inc(result_taken, 1)
                            dve.wait_ge(u_sq, b * 8 + (u0 + i + 1))
                            dve.wait_ge(mh_ready, b * 8 + (m0 + i + 1))
                            v.tensor_tensor(XL[:, i, :], sq[:, i % 2, :], XH[:, i, :].bitcast(F32), ALU.subtract).then_inc(m_ready, 1)
                        else:
                            kt = i - 8
                            add_x(ps, kt, last, r0 + 16 * b + i if last else None)
                            if last and l < DEPTH - 1:
                                prep_lo(G_ATTN + 8 * (l + 1), kt, (MH, ML))
                            elif last:
                                v.tensor_scalar(xf[:, kt, :], xT[:, kt, :], gain[:, G_LAST + kt:G_LAST + kt + 1], None, ALU.mult).then_inc(xt_ready, 1)

                ff_block(0, first=True)
                with dve.Fori(1, BLOCKS - 1) as b:
                    ff_block(b)
                ff_block(BLOCKS - 1, last=True)
                count["mh"] += 8 * BLOCKS
                count["usq"] += 8 * BLOCKS
            stat(plan["last_stat"], S)
            dve.wait_ge(rstd_done, 2)
            for m in range(0, 2 * NB, 2):
                n, c = m % NB, 512 * (m // NB)
                dve.wait_ge(y_done, m + 1)
                v.tensor_scalar(yrow[:, n, c:c + 512], y_bank(m), rstd[:, S + n:S + n + 1], None, ALU.mult).then_inc(y_dve, 1)

        @block.tensor
        def _(pe):
            mm = nc.tensor.matmul
            xg = [0]

            def begin(r, loop=None):
                if loop is None:
                    if r >= 2:
                        pe.wait_ge(result_taken, r - 1)
                else:
                    pe.wait_ge(result_taken, loop * 16 + (r - 1))
                return U[:, r % 2, :]

            def three(o, wh, wl, xh, xl, first, last, **kw):
                mm(o, wl, xh, start=first, stop=False, **kw)
                mm(o, wh, xl, start=False, stop=False, **kw)
                return mm(o, wh, xh, start=False, stop=last, **kw)

            def tile_parts(s, kts=None, ready=None):
                kind, t, r = s["kind"], s["t"], s["r"]
                a, al = operands[s["operand"]]

                def part(i):
                    if i == 0 and kind[-1] != "v":
                        pe.wait_ge(lo_done, t + 1)
                    if i == 0 and kind[-1] == "v":
                        pe.wait_ge(lo_done, t - t % 2 + 2)
                    if kind == "wo":
                        res, k0 = r + i // 2, 2 * (i % 2)
                        o = begin(res) if i % 2 == 0 else U[:, res % 2, :]
                        base = 0 if s["second"] else 4
                        for k in range(k0, k0 + 2):
                            if ready and i < 2:
                                pe.wait_ge(m_ready, ready[k])
                            c = slice(256 * k + P * (i // 2), 256 * k + P * (i // 2) + P)
                            last = three(o, WH[:, t % 4, c], WL[:, t % 4, c], a[:, base + k, :], al[:, base + k, :], k == 0, k == 3)
                        if i % 2:
                            last.then_inc(psum_done, 1)
                    elif kind == "mix":
                        g = i
                        o = begin(r + g)
                        for k in range(2):
                            c = slice(P * (2 * g + k), P * (2 * g + k) + P)
                            last = three(o, WH[:, t % 4, c], WL[:, t % 4, c], a[:, 2 * g + k, :], al[:, 2 * g + k, :], k == 0, k == 1)
                        last.then_inc(psum_done, 1)
                    elif kind[-1] == "v":
                        res = r + i // 2
                        n = 2 * (s["j"] % 2) + i // 2
                        o = begin(res) if i % 2 == 0 else U[:, res % 2, :]
                        t2 = t - t % 2
                        s2 = t2 % 4
                        q = slice(P * n, P * n + P)
                        for k in range(4 * (i % 2), 4 * (i % 2) + 4):
                            c = slice(P * k, P * k + P)
                            wh, wl = WH[:, s2:s2 + 2, c], WL[:, s2:s2 + 2, c]
                            o2 = o[:, 0:256]
                            mm(o2, a[:, k, q], wl, start=k == 0, stop=False)
                            mm(o2, al[:, k, q], wh, start=False, stop=False)
                            last = mm(o2, a[:, k, q], wh, start=False, stop=k == 7)
                        if i % 2:
                            last.then_inc(psum_done, 1)
                    else:
                        o = begin(r) if i == 0 else U[:, r % 2, :]
                        order = kts or list(range(8))
                        for k in order[2 * i:2 * i + 2]:
                            if ready:
                                pe.wait_ge(ready["sem"], ready[k])
                            c = slice(P * k, P * k + P)
                            last = three(o, WH[:, t % 4, c], WL[:, t % 4, c], a[:, k, :], al[:, k, :], k == order[0], k == order[7])
                        if i == 3:
                            last.then_inc(psum_done, 1)
                return [lambda i=i: part(i) for i in range(4)]

            def stat(st):
                if not st.get("res"):
                    pe.wait_ge(acc_done, sum(squares[:stats[0] + 1]))
                    stats[0] += 1
                if st["z"]:
                    pe.wait_ge(z_free, st["z"])
                terms = [(eps_w, acc), (mean_w, acc_mid)] if st.get("mid") else [(mean_w, acc)]
                for i, (w, x) in enumerate(terms):
                    mm(Z[:, 0:S], w[:], x[:], start=i == 0, stop=i == len(terms) - 1)
                for n in range(NB):
                    for i, (w, x) in enumerate(terms):
                        last = mm(Z[:, 512 + n:513 + n], x[:, P * n:P * n + P], w[:, 0:1], start=i == 0, stop=i == len(terms) - 1)
                last.then_inc(z_done, 1)

            stats = [0]
            pe.wait_ge(const_ready, 1)
            pe.wait_ge(gains_landed, 16 * len(gains))
            nc.tensor.transpose(Z[:, 0:GROWS], grow[:], ident[0:GROWS, 0:GROWS]).then_inc(gain_done, 1)
            pe.wait_ge(in_landed, 16 * NB)
            for kt in range(KT):
                o = begin(kt)
                for n in range(NB):
                    i = nc.tensor.transpose(o[:, P * n:P * n + P], xin[:, n, P * kt:P * kt + P], ident[:])
                i.then_inc(psum_done, 1)
            pe.wait_ge(gain_ready, 1)

            def swa_qk(st):
                h = st["h"]
                j, g, b = h // 2, h // 4, 64 * (h % 2)
                q = [s for s in plan["attn"] if s["kind"] == "q" and s["j"] == j][0]
                pe.wait_ge(result_taken, q["r"] + 1)
                pe.wait_ge(z_free, st["z"])
                rows_ = slice(b, b + 64)
                for n in range(NB):
                    k0 = max(n - 1, 0) * P
                    o0 = 256 * n + (P if n == 0 else 0)
                    i = mm(Z[:, o0:256 * n + 256], q0[rows_, j % 4, P * n:P * n + P], kd[rows_, g, k0:P * n + P], start=True, stop=True)
                i.then_inc(z_done, 1)

            def swa_t(st):
                h = st["h"]
                pe.wait_ge(p_ready, h + 1)
                if st["p0"]:
                    pe.wait_ge(p0_free, st["p0"])
                for k in range(4):
                    i = nc.tensor.transpose(PP[:, 0, P * k:P * k + P], pr[:, h % 3, P * k:P * k + P], ident[:])
                i.then_inc(p0_done, 1)
                if st["p1"]:
                    pe.wait_ge(p1_free, st["p1"])
                for k in range(3):
                    i = nc.tensor.transpose(PP[:, 1, P * k:P * k + P], pr[:, h % 3, 512 + P * k:640 + P * k], ident[:])
                i.then_inc(p1_done, 1)

            def swa_pv(st):
                h = st["h"]
                g, b = h // 4, 64 * (h % 2)
                pe.wait_ge(p0_free, st["p0"] + 1)
                pe.wait_ge(p1_free, st["p1"] + 1)
                if h % 2 == 0 and st["o"]:
                    pe.wait_ge(o_free, st["o"])
                for n in range(NB):
                    w = 256 if n < NB - 1 else P
                    i = mm(O[b:b + 64, P * n:P * n + w], v0[:, n, 64 * g:64 * g + 64], pt0[:, 256 * n:256 * n + w],
                           start=n == 0, stop=n == NB - 1, skip_group_check=True)
                if h % 2:
                    i.then_inc(o_done, 1)

            xg_base = {"sem": xg_ready, **{k: k + 1 for k in range(8)}}
            m_count = [0]
            for s in plan["attn"]:
                kind = s["kind"]
                ready = None
                if s["t"] == 0:
                    ready = xg_base
                if kind == "out" and s["j"] == 0:
                    ready = {"sem": m_ready, **{k: k + 1 for k in range(8)}}
                parts = tile_parts(s, ready=ready)
                for half in range(2):
                    steps = [st for st in s["steps"] if st.get("half") == half]
                    for st in steps:
                        if st["op"] == "swa_qk":
                            swa_qk(st)
                    for st in steps:
                        if st["op"] == "swa_t":
                            swa_t(st)
                    parts[2 * half]()
                    parts[2 * half + 1]()
                    for st in steps:
                        if st["op"] == "swa_t":
                            swa_pv(st)
                for st in s["steps"]:
                    if st["op"] == "stat":
                        stat(st)
            for s in plan["pool"]:
                kind = s["kind"]
                ready, kts = None, None
                if kind == "pu" and s["j"] == 0:
                    ready = {"sem": xg_ready, **{k: 8 + k + 1 for k in range(8)}}
                if kind == "mix" and s["j"] == 0:
                    pe.wait_ge(m_ready, 16)
                if kind == "out" and s["j"] == 0:
                    kts = [0, 2, 4, 6, 1, 3, 5, 7]
                    ready = {"sem": m_ready, **{c: 16 + n + 1 for n, c in enumerate(kts)}}
                for part in tile_parts(s, kts=kts, ready=ready):
                    part()
                for st in s["steps"]:
                    stat(st)

            def pair_slot(l, kind, j):
                return [s for s in plan["layer", l] if s["kind"] == kind and s["j"] == j][0]

            def qk_step(st, l):
                df = st["op"] == "df_qk"
                name = "df" if df else "sb"
                j, b = (st["h"], 64 * st["m"]) if df else (st["h"] // 2, 64 * (st["h"] % 2))
                pe.wait_ge(result_taken, pair_slot(l, name + "q", j)["r"] + 1)
                pe.wait_ge(z_free, st["z"])
                rows_ = slice(b, b + 64)
                for c, (_, _, blocks) in enumerate(CHUNKS):
                    for n in blocks:
                        z0, w = ZOFF[n], P * (n + 1)
                        i = mm(Z[:, z0:z0 + w], qk[name + "q"][rows_, j, P * n:P * n + P], qk[name + "k"][rows_, j, 0:w],
                               start=True, stop=True)
                        if not df:
                            i = mm(Z[:, z0 + w - P:z0 + w], identb[:], mask_sb[:], start=False, stop=True, skip_group_check=True)
                    if not df:
                        i.then_inc(z_done, 1)
                if df:
                    i.then_inc(z_done, 1)

            def t_src(st):
                return cc[:] if st["df"] else ea[:, 1 + st["h"] % 2, :]

            def t1(st, l):
                w = t_src(st)
                if st["df"]:
                    pe.wait_ge(dfw_ready, 4 * l + st["h"] + 1)
                else:
                    pe.wait_ge(w_ready, 3 * (8 * l + st["h"]) + 3)
                pe.wait_ge(p0_free, st["p0"])
                for k in range(4):
                    i = nc.tensor.transpose(PP[:, 0, P * k:P * k + P], w[:, P * k:P * k + P], ident[:])
                i.then_inc(p0_done, 1)
                pe.wait_ge(p1_free, st["p1"])
                for k in range(4):
                    i = nc.tensor.transpose(PP[:, 1, P * k:P * k + P], w[:, 512 + P * k:640 + P * k], ident[:])
                i.then_inc(p1_done, 1)

            def t2(st):
                w = t_src(st)
                pe.wait_ge(p0_free, st["p0"] + 1)
                for k in range(2):
                    i = nc.tensor.transpose(PP[:, 0, P * k:P * k + P], w[:, 1024 + P * k:1152 + P * k], ident[:])
                i.then_inc(p0_done, 1)

            def pv(st, l):
                h = st["h"]
                pe.wait_ge(p0_free, st["p0"] + 2)
                pe.wait_ge(p1_free, st["p1"] + 1)
                last_v = pair_slot(l, "dfv" if st["df"] else "sbv", 1 + 2 * (h // (2 if st["df"] else 4)))
                pe.wait_ge(result_taken, last_v["r"] + 2)
                if st["df"] or h % 2 == 0:
                    pe.wait_ge(o_free, st["o"])
                if st["df"]:
                    for n in range(NB):
                        for k in range(n + 1):
                            i = mm(O[:, P * n:P * n + P], pt[:, k, P * n:P * n + P], qk["dfv"][:, k, P * h:P * h + P],
                                   start=k == 0, stop=k == n)
                    i.then_inc(o_done, 1)
                else:
                    b = 64 * (h % 2)
                    for k in range(NB):
                        i = mm(O[b:b + 64, P * k:S], qk["sbv"][:, k, 64 * h:64 * h + 64], pt[:, k, P * k:S],
                               start=k == 0, stop=k == NB - 1, skip_group_check=True)
                    if h % 2:
                        i.then_inc(o_done, 1)

            def df_f(st, l):
                pe.wait_ge(od_ready, 4 * l + st["h"] + 1)
                pe.wait_ge(p0_free, st["p0"])
                for n in range(NB):
                    i = nc.tensor.transpose(PP[:, 0, P * n:P * n + P], tb[:, 1, P * n:P * n + P], ident[:])
                i.then_inc(p0_done, 1)

            m_seen = 24
            for l in range(DEPTH):
                for s in plan["layer", l]:
                    ready = None
                    if s["kind"] == "dfk" and s["j"] == 0:
                        ready = {"sem": xg_ready, **{k: 16 + 16 * l + k + 1 for k in range(8)}}
                    if s["kind"] == "wo" and s["j"] == 0:
                        ready = {k: m_seen + [1, 2, 3, 4][k] for k in range(4)}
                    if s["kind"] == "wo" and s["j"] == 4:
                        ready = {k: m_seen + 4 + k + 1 for k in range(4)}
                    parts = tile_parts(s, ready=ready)
                    ts = [st for st in s["steps"] if st["op"] == "t"]
                    for st in s["steps"]:
                        if st["op"] in ("sb_qk", "df_qk"):
                            qk_step(st, l)
                    parts[0]()
                    parts[1]()
                    for st in ts:
                        t1(st, l)
                    parts[2]()
                    for st in s["steps"]:
                        if st["op"] == "df_f":
                            df_f(st, l)
                    for st in ts:
                        t2(st)
                    parts[3]()
                    for st in ts:
                        pv(st, l)
                    for st in s["steps"]:
                        if st["op"] == "stat":
                            stat(st)
                m_seen += 8
                t0, r0 = plan["ff", l]

                def ff_block(b, first=False):
                    for i in range(16):
                        t, r = t0 + i, r0 + i
                        pe.wait_ge(lo_done, b * 16 + (t + 1))
                        o = begin(r, b)
                        for k in range(KT):
                            if first and i == 0:
                                pe.wait_ge(xg_ready, 24 + 16 * l + k + 1)
                            if i == 8:
                                pe.wait_ge(m_ready, b * 8 + (m_seen + k + 1))
                            h_, l_ = (MH, ML) if i < 8 else (XH, XL)
                            c = slice(P * k, P * k + P)
                            last = three(o, WH[:, t % 4, c], WL[:, t % 4, c], h_[:, k, :], l_[:, k, :], k == 0, k == KT - 1)
                        last.then_inc(psum_done, 1)
                        if first and i == 0:
                            stat(plan["ff_stat", l])

                ff_block(0, first=True)
                with pe.Fori(1, BLOCKS) as b:
                    ff_block(b)
                m_seen += 8 * BLOCKS
            def y_turn(m):
                half, n = m // NB, m % NB
                for k in range(4):
                    pe.wait_ge(xt_ready, KT + 4 * half + k + 1)
                    i = nc.tensor.transpose(y_bank(m)[:, P * k:P * k + P], xf[:, 4 * half + k, P * n:P * n + P], ident[:])
                i.then_inc(y_done, 1)

            st = plan["last_stat"]
            pe.wait_ge(z_free, st["z"])
            pe.wait_ge(o_free, plan["o"])
            for m in range(NB):
                y_turn(m)
            pe.wait_ge(acc_done, sum(sums))
            pe.wait_ge(sq_ready, sum(squares))
            for n in range(NB):
                q = slice(P * n, P * n + P)
                mm(Z[:, 512 + n:513 + n], acc[:, q], mean_w[:, 0:1], start=True, stop=False)
                i = mm(Z[:, 512 + n:513 + n], sq[:, (KT - 1) % 2, q], mean_w[:, 0:1], start=False, stop=True)
            i.then_inc(z_done, 1)
            for m in range(NB, 2 * NB):
                if m > NB:
                    pe.wait_ge(result_taken, r0 + 16 * BLOCKS)
                if m == 2 * NB - 1:
                    pe.wait_ge(y_dve, 1)
                y_turn(m)


INPUTS = ["x", "norm_g", "attn_w_in", "attn_sinks", "attn_w_out", "pool_w_in", "pool_w_mix", "pool_scale",
          "pool_w_out", "final_g", "w_in_2", "w_o_2", "attn_norm_2", "subln_norm_2", "lam_q1_2", "lam_k1_2",
          "lam_q2_2", "lam_k2_2", "mlp_norm_2", "w_ff1_2", "w_ff2_2", "final_norm_2"]


def kernel(**inputs):
    import numpy as np
    import concourse.bacc as bacc
    from concourse.bass_utils import run_bass_kernel_spmd as run

    nc = bacc.Bacc("TRN2", target_bir_lowering=False, num_devices=1)
    arrays, args = {}, []
    for name in INPUTS:
        a = np.ascontiguousarray(inputs[name])
        arrays["in_" + name] = a
        args.append(nc.dram_tensor("in_" + name, a.shape, mybir.dt.from_np(a.dtype), kind="ExternalInput").ap())
    freq = (1.0 / (np.float32(10000.0) ** (np.arange(0, 64, 2, dtype=np.float32) / np.float32(64)))).astype(np.float32)
    angle = (freq[:, None] * np.arange(512, dtype=np.float32)[None, :]).astype(np.float32)
    cos, sin = np.cos(angle), np.sin(angle)
    table = np.stack([np.concatenate([cos] * 4), np.concatenate([-sin, sin] * 2)], axis=1).astype(np.float32)
    table = np.ascontiguousarray(table)
    arrays["in_rope_table"] = table
    args.append(nc.dram_tensor("in_rope_table", table.shape, mybir.dt.float32, kind="ExternalInput").ap())
    args.append(nc.dram_tensor("out_x", inputs["x"].shape, mybir.dt.float32, kind="ExternalOutput").ap())
    build(nc, *args)
    return run(nc, [arrays], core_ids=[0]).results[0]["out_x"]
```

```python
import math
from contextlib import ExitStack

import concourse.bass as bass
from concourse import mybir

F32 = mybir.dt.float32
F32R = mybir.dt.float32r
BF16 = mybir.dt.bfloat16
ALU = mybir.AluOpType
ACT = mybir.ActivationFunctionType

P = 128
EPS = 1e-6
NEG = -1e30


class Tally:

    def __init__(self):
        self.n = {}

    def take(self, name, k=1):
        before = self.n.get(name, 0)
        self.n[name] = before + k
        return before


def make_plan(depth):
    tally = Tally()

    def slot(kind, j, results, **more):
        return dict(kind=kind, j=j, t=tally.take("t"), r=tally.take("r", results), n=results, steps=[], **more)

    def use(**step):
        k = step["op"]
        if k in ("swa_qk", "df_qk", "sb_qk", "stat"):
            step["z"] = tally.take("z")
            step["zd"] = tally.take("z_done", 3 if k == "sb_qk" else 1)
        if k in ("swa_t", "t", "df_f"):
            step["p0"] = tally.take("p0", 2 if k == "t" else 1)
        if k in ("swa_t", "t"):
            step["p1"] = tally.take("p1")
        if k == "swa_t" and step["h"] % 2 == 0 or k == "t" and (step["df"] or step["h"] % 2 == 0):
            step["o"] = tally.take("o")
        elif k in ("swa_t", "t"):
            step["o"] = tally.n["o"] - 1
        return step

    plan = {}
    tally.take("r", 8)
    attn = [slot("k", j, 1) for j in range(2)] + [slot("v", j, 2) for j in range(2)]
    attn += [slot("q", j, 1) for j in range(8)] + [slot("z", j, 1) for j in range(8)]
    attn += [slot("out", j, 1) for j in range(8)]
    plan["attn"] = attn
    for s in attn:
        s["operand"] = "M" if s["kind"] == "out" else "X"
    attn[0]["steps"].append(use(op="stat"))
    for i in range(18):
        s = attn[6 + i // 2]
        if i < 16:
            s["steps"].append(use(op="swa_qk", h=i, half=i % 2))
        if i >= 2:
            s["steps"].append(use(op="swa_t", h=i - 2, half=i % 2))
    pool = [slot("pu", j, 1) for j in range(8)] + [slot("pz", j, 1) for j in range(8)]
    pool += [slot("mix", j, 4) for j in range(2)] + [slot("out", j, 1) for j in range(8)]
    plan["pool"] = pool
    for s in pool:
        s["operand"] = "M" if s["kind"] == "mix" else "X"
    pool[0]["steps"].append(use(op="stat"))
    for l in range(depth):
        s = []
        for name in ("df", "df", "sb", "sb"):
            half = len(s) // 6 % 2
            s += [slot(name + "k", 2 * half + j, 1) for j in range(2)]
            s += [slot(name + "q", 2 * half + j, 1) for j in range(2)]
            s += [slot(name + "v", 2 * half + j, 2) for j in range(2)]
        s += [slot("wo", j, 2, second=j >= 4) for j in range(8)]
        plan["layer", l] = s
        for x in s:
            x["operand"] = "X" if x["kind"] == "wo" else "M"
        s[0]["steps"].append(use(op="stat", mid=l == 0))
        if l == 0:
            s[4]["steps"].append(use(op="stat", res=True))
        todo = {}
        for d in range(4):
            at = 6 * (1 + d // 2) + 2 * (d % 2)
            for m in range(2):
                todo.setdefault(at + m, []).append(dict(op="df_qk", h=d, m=m))
            todo.setdefault(at + 2, []).append(dict(op="t", h=d, df=True))
            todo.setdefault(at + 3, []).append(dict(op="df_f", h=d))
        for h in range(8):
            todo.setdefault(18 + h, []).append(dict(op="sb_qk", h=h))
            todo.setdefault(19 + h, []).append(dict(op="t", h=h, df=False))
            if h % 2:
                todo.setdefault(20 + h, []).append(dict(op="sb_o", h=h))
        order = ["sb_qk", "df_qk", "df_f", "t", "sb_o"]
        for k in sorted(todo):
            for step in sorted(todo[k], key=lambda x: order.index(x["op"])):
                s[k]["steps"].append(use(**step))
        for step in [st for x in s for st in x["steps"] if st["op"] == "sb_o"]:
            step["o"] = [st["o"] for x in s for st in x["steps"] if st["op"] == "t" and not st["df"] and st["h"] == step["h"]][0]
        plan["ff_stat", l] = use(op="stat")
        plan["ff", l] = (tally.take("t", 64), tally.take("r", 64))
    plan["last_stat"] = use(op="stat")
    plan["o"] = tally.n["o"]
    plan["tiles"] = tally.n["t"]
    return plan


def build(nc, x, norm_g, attn_w_in, attn_sinks, attn_w_out, pool_w_in, pool_w_mix, pool_scale,
          pool_w_out, final_g, w_in_2, w_o_2, attn_norm_2, subln_norm_2, lam_q1_2, lam_k1_2,
          lam_q2_2, lam_k2_2, mlp_norm_2, w_ff1_2, w_ff2_2, final_norm_2, rope_table, out):
    S, D = x.shape[1], x.shape[2]
    KT = D // P
    NB = S // P
    DEPTH = w_in_2.shape[0]
    FF = w_ff1_2.shape[2]
    BLOCKS = FF // D
    plan = make_plan(DEPTH)
    LAST_T = plan["tiles"]
    NS = S + NB
    POOL_W = (2, 4, 8, 16)
    PAD = max(POOL_W)
    ZOFF = {3: 0, 2: 512, 0: 896, 1: 1024}
    CHUNKS = [(0, 512, [3]), (512, 512, [2, 0]), (1024, 256, [1])]
    G_NORM, G_FINAL, G_SCALE, G_ATTN, G_MLP, G_LAST, G_SUB = 0, 16, 24, 32, 48, 64, 72
    GROWS = G_SUB + DEPTH
    G_MID = GROWS

    with ExitStack() as ctx:
        def sb(name, shape, dt=F32, c=ctx):
            return c.enter_context(nc.sbuf_tensor(name, shape, dt))

        def sem(name):
            return ctx.enter_context(nc.semaphore(name))

        xT = sb("xT", [P, KT, S])
        XH, XL = sb("XH", [P, KT, S], F32R), sb("XL", [P, KT, S], F32R)
        MH, ML = sb("MH", [P, KT, S], F32R), sb("ML", [P, KT, S], F32R)
        operands = {"X": (XH, XL), "M": (MH, ML)}
        raw = sb("raw", [P, 2, KT * 256])
        WH, WL = sb("WH", [P, 4, KT * P], F32R), sb("WL", [P, 4, KT * P], F32R)
        ident = sb("ident", [P, P])
        identb = sb("identb", [P, P], BF16)
        ones = sb("ones", [P, 1])
        mean_w = sb("mean_w", [P, P])
        eps_w = sb("eps_w", [P, P])
        mask_sw = sb("mask_sw", [P, 256])
        mask_sb = sb("mask_sb", [P, P], BF16)
        mask_df = sb("mask_df", [P, 512])
        inv_n = sb("inv_n", [P, PAD])
        grow = sb("grow", [GROWS, P])
        gain = sb("gain", [P, GROWS + KT])
        sink = sb("sink", [P, 16])
        lamw = sb("lamw", [P, 64])
        lamd = sb("lamd", [P, 2 * DEPTH])
        lame = sb("lame", [P, 2 * DEPTH])
        neglam = sb("neglam", [P, DEPTH])
        sq = sb("sq", [P, 2, S])
        acc = sb("acc", [P, S])
        rstd, res_rstd, nt = sb("rstd", [P, NS]), sb("res_rstd", [P, NS]), sb("nt", [P, NS])
        small = sb("small", [P, 64])
        tb = sb("tb", [P, 2, S])
        lamv = tb[:, 0, 0:4 * DEPTH * 64].rearrange("p (v n) -> p v n", v=4)

        U = ctx.enter_context(nc.psum_tensor("U", [P, 2, 512], F32))
        Z = ctx.enter_context(nc.psum_tensor("Z", [P, 1536], F32))
        PP = ctx.enter_context(nc.psum_tensor("PP", [P, 2, 512], F32))
        O = ctx.enter_context(nc.psum_tensor("O", [P, 512], F32))

        a0 = ExitStack()
        xin = sb("xin", [P, NB, D], c=a0)
        oraw = xin[:].rearrange("p a (b s) -> p (a b) s", s=S)
        q0 = sb("q0", [P, 4, S], c=a0)
        kd = sb("kd", [P, 4, S], c=a0)
        v0 = sb("v0", [P, NB, 256], c=a0)
        pr = sb("pr", [P, 3, 896], c=a0)
        pt0 = sb("pt0", [P, 896], c=a0)
        a0.close()
        a1 = ExitStack()
        pad = sb("pad", [P, 6, PAD + S], c=a1)
        pf = sb("pf", [P, 2, S], c=a1)
        sz = sb("sz", [P, KT, S], c=a1)
        acc_mid = sb("acc_mid", [P, S], c=a1)
        a1.close()
        a2 = ExitStack()
        keys, queries, values = (sb(n, [P, 4, S], c=a2) for n in ("keys", "queries", "values"))
        qk = {"dfk": keys, "dfq": queries, "dfv": values, "sbk": keys, "sbq": queries, "sbv": values}
        cs = sb("cs", [P, 2, S], c=a2)
        ea = sb("ea", [P, 3, 1280], c=a2)
        cc = sb("cc", [P, 1280], c=a2)
        pt = sb("pt", [P, 4, S], c=a2)
        a2.close()
        a3 = ExitStack()
        xf = sb("xf", [P, KT, S], c=a3)
        yrow = sb("yrow", [P, NB, D], c=a3)
        a3.close()

        in_landed, gains_landed, par_landed = sem("in_landed"), sem("gains_landed"), sem("par_landed")
        raw_landed = [sem("raw_landed0"), sem("raw_landed1")]
        cs_landed = sem("cs_landed")
        hi_done, lo_done = sem("hi_done"), sem("lo_done")
        psum_done, result_taken = sem("psum_done"), sem("result_taken")
        const_f, const_ready = sem("const_f"), sem("const_ready")
        gain_done, gain_ready = sem("gain_done"), sem("gain_ready")
        lam_dot, lam_exp = sem("lam_dot"), sem("lam_exp")
        normed_hi_ready, normed_ready = sem("normed_hi_ready"), sem("normed_ready")
        second_hi_ready, second_ready = sem("second_hi_ready"), sem("second_ready")
        scaled, xt_ready = sem("scaled"), sem("xt_ready")
        sq_ready, acc_done = sem("sq_ready"), sem("acc_done")
        rsqrt_ready, rstd_done = sem("rsqrt_ready"), sem("rstd_done")
        z_done, z_free = sem("z_done"), sem("z_free")
        p0_done, p0_free = sem("p0_done"), sem("p0_free")
        p1_done, p1_free = sem("p1_done"), sem("p1_free")
        o_done, o_free = sem("o_done"), sem("o_free")
        negm_ready, exp_done, probs_ready = sem("negm_ready"), sem("exp_done"), sem("probs_ready")
        sigmoid_ready, zo_ready = sem("sigmoid_ready"), sem("zo_ready")
        product_ready, pair_ready = sem("product_ready"), sem("pair_ready")
        rope_shifted = sem("rope_shifted")
        df_weights_ready, sub_squares_ready = sem("df_weights_ready"), sem("sub_squares_ready")
        sub_ms_ready, sub_rsqrt_ready, df_out_ready = sem("sub_ms_ready"), sem("sub_rsqrt_ready"), sem("df_out_ready")
        softplus_ready, sb_logs_ready, sb_weights_ready = sem("softplus_ready"), sem("sb_logs_ready"), sem("sb_weights_ready")
        relu_squared = sem("relu_squared")
        dve_step, act_step = sem("dve_step"), sem("act_step")
        y_done, y_dve, y_act = sem("y_done"), sem("y_dve"), sem("y_act")
        stored = sem("stored")

        freed, wo_tiles = {}, set()
        for name, part in plan.items():
            if name in ("attn", "pool") or name[0] == "layer":
                for s in part:
                    freed[s["t"]] = s["r"] + s["n"] * (2 if s["kind"][-1] == "v" and s["t"] % 2 == 0 else 1)
                    if s["kind"] == "wo":
                        wo_tiles.add(s["t"])
            elif name[0] == "ff":
                for i in range(16 * BLOCKS):
                    freed[part[0] + i] = part[1] + i + 1
        all_steps = [st for n, part in plan.items() if n in ("attn", "pool") or n[0] == "layer" for s in part for st in s["steps"]]
        all_stats = [st for st in all_steps if st["op"] == "stat"] + [p for n, p in plan.items() if "stat" in n or "stat" in n[0]]
        all_stats.sort(key=lambda st: st["zd"])
        NORMS = 3 + 2 * DEPTH
        MID = 2
        squares = [KT * (2 if s == MID else 1) for s in range(NORMS)]
        sums = [n - (s == NORMS - 1) for s, n in enumerate(squares)]
        swa_t_of = {st["h"]: st for st in all_steps if st["op"] == "swa_t"}

        def raw_view(t):
            k = 4 if t in wo_tiles else 8
            n = 4 * 256 // k
            return raw[:, t // 2 % 2, :].rearrange("p (k n) -> p k n", k=k)[:, :, n * (t % 2):n * (t % 2) + n], k

        def w_slot(w, t, k):
            return w[:, t % 4, :].rearrange("p (k n) -> p k n", k=k)

        def x_bank(kt):
            return [U[:, 0, :], U[:, 1, :], PP[:, 0, :], PP[:, 1, :], O[:], Z[:, 512:1024], Z[:, 1024:1536], U[:, 1, :]][kt]

        def y_bank(m):
            return [PP[:, 0, :], PP[:, 1, :], O[:], Z[:, 0:512], Z[:, 1024:1536], U[:, 0, :], U[:, 1, :], PP[:, 0, :]][m]

        def rev(ap, z0, z1):
            return ap[:, z0:z1][:, ::-1]

        def rows(w, c0, n=256):
            return w[:, c0:c0 + n].rearrange("(k p) n -> p k n", p=P)

        def pair_sources():
            w = attn_w_in[0]
            cols = [1024, 1280] + [256 * i for i in range(4)] + [1536 + 256 * i for i in range(4)]
            out_ = [rows(w, c) for c in cols]
            out_ += [rows(attn_w_out[0], 256 * i) for i in range(4)]
            out_ += [rows(pool_w_in[0], 256 * i) for i in range(8)]
            out_ += [pool_w_mix[0].rearrange("g (k p) n -> p (g k) n", p=P)]
            out_ += [rows(pool_w_out[0], 256 * i) for i in range(4)]
            layers = []
            for l in range(DEPTH):
                w = w_in_2[l]
                dfq, sbq, third = 1536, 0, 512
                pairs = []
                for base in (dfq, sbq):
                    for half in range(2):
                        pairs += [rows(w, base + a * third + 256 * half) for a in (1, 0, 2)]
                for r0 in (512, 0):
                    pairs += [w_o_2[l][r0:r0 + 512, c:c + 512].rearrange("(k p) n -> p k n", p=P) for c in (0, 512)]
                layers.append(pairs)
            return out_, layers

        gains = [(grow[G_NORM:G_NORM + 16, :], norm_g.rearrange("l (k p) -> (l k) p", p=P)),
                  (grow[G_FINAL:G_FINAL + 8, :], final_g.rearrange("(k p) -> k p", p=P)),
                  (grow[G_SCALE:G_SCALE + 8, :], pool_scale.rearrange("l (k p) -> (l k) p", p=P)),
                  (grow[G_ATTN:G_ATTN + 16, :], attn_norm_2.rearrange("l (k p) -> (l k) p", p=P)),
                  (grow[G_MLP:G_MLP + 16, :], mlp_norm_2.rearrange("l (k p) -> (l k) p", p=P)),
                  (grow[G_LAST:G_LAST + 8, :], final_norm_2.rearrange("(k p) -> k p", p=P)),
                  (grow[G_SUB:G_SUB + DEPTH, :], subln_norm_2)]
        common = [(sink[:], attn_sinks[0].partition_broadcast(P))]
        common += [(lamv[:, i, :], v.rearrange("l d -> (l d)").partition_broadcast(P))
                   for i, v in enumerate((lam_q1_2, lam_k1_2, lam_q2_2, lam_k2_2))]

        block = ctx.enter_context(nc.Block())

        @block.sync
        def _(sp):
            for half in range(2):
                c = slice(D // 2 * half, D // 2 * (half + 1))
                sp.dma_start(xin[:, :, c], x[0][:, c].rearrange("(s p) n -> p s n", p=P)).then_inc(in_landed, 16)
                if half == 0:
                    for dst, src in gains[4:]:
                        sp.dma_start(dst, src).then_inc(gains_landed, 16)
            pairs, layers = pair_sources()

            def load(p, src, phase, parity):
                if phase is not None:
                    sp.wait_ge(lo_done, phase)
                k = src.shape[1]
                dst = raw[:, parity, :].rearrange("p (k n) -> p k n", k=k)
                sp.dma_start(dst, src).then_inc(raw_landed[parity], 16)

            p = 0
            for src in pairs[:2]:
                load(p, src, None, p % 2)
                p += 1
            for src in pairs[2:]:
                load(p, src, 2 * p - 2, p % 2)
                p += 1
            for l in range(DEPTH):
                for src in layers[l]:
                    load(p, src, 2 * p - 2, p % 2)
                    p += 1
                with sp.Fori(0, BLOCKS) as b:
                    for i in range(8):
                        if i < 4:
                            src = w_ff1_2[l][:, bass.ds(b * D + 256 * i, 256)].rearrange("(k p) n -> p k n", p=P)
                        else:
                            c = 256 * (i - 4)
                            src = w_ff2_2[l][bass.ds(b * D, D), c:c + 256].rearrange("(k p) n -> p k n", p=P)
                        load(None, src, b * 16 + (2 * (p + i) - 2), (p + i) % 2)
                p += 8 * BLOCKS
            for m in range(2 * NB):
                n, c = m % NB, slice(512 * (m // NB), 512 * (m // NB) + 512)
                sp.wait_ge(y_act if m % 2 else y_dve, m // 2 + 1)
                sp.dma_start(out[0, n * P:(n + 1) * P, c], yrow[:, n, c]).then_inc(stored, 16)
            sp.wait_ge(stored, 16 * 2 * NB)

        @block.gpsimd
        def _(pool):
            g = nc.gpsimd
            g.memset(ident[:], 0.0)
            g.memset(identb[:], 0.0)
            g.memset(ones[:], 1.0)
            g.memset(mean_w[:], 1.0 / D)
            g.memset(eps_w[:], EPS / D)
            g.memset(mask_sw[:], 0.0)
            g.memset(mask_sb[:], 0.0)
            g.memset(mask_df[:], 0.0)
            for s in range(PAD):
                last = g.memset(inv_n[:, s:s + 1], 1.0 / (s + 1))
            last.then_inc(const_f, 1)
            pool.wait_ge(const_f, 1)
            g.memset(mask_df[0:64, 448:512], NEG)
            for m in (ident, identb):
                g.affine_select(out=m[:], in_=m[:], compare_op=ALU.not_equal, fill=1.0, base=0,
                                pattern=[[-1, P]], channel_multiplier=1)
            g.affine_select(out=mask_sw[:, 0:P], in_=mask_sw[:, 0:P], compare_op=ALU.is_gt, fill=NEG,
                            base=0, pattern=[[1, P]], channel_multiplier=-1)
            g.affine_select(out=mask_sw[:, P:256], in_=mask_sw[:, P:256], compare_op=ALU.is_ge, fill=NEG,
                            base=0, pattern=[[-1, P]], channel_multiplier=1)
            g.affine_select(out=mask_sb[:], in_=mask_sb[:], compare_op=ALU.is_gt, fill=NEG,
                            base=0, pattern=[[-1, P]], channel_multiplier=1).then_inc(const_ready, 1)
            n = 0
            for s in range(NORMS):
                if s == 1:
                    for zs in [w for w in plan["attn"] if w["kind"] == "z"]:
                        pool.wait_ge(result_taken, zs["r"] + 1)
                        pool.wait_ge(o_free, zs["j"] + 1)
                        o = oraw[:, zs["j"], :]
                        g.tensor_tensor(o, tb[:, zs["j"] % 2, :], o, ALU.mult).then_inc(zo_ready, 1)
                if s == 2:
                    for us in [w for w in plan["pool"] if w["kind"] == "pu"]:
                        j = us["j"]
                        pool.wait_ge(result_taken, us["r"] + 1)
                        if j >= 2:
                            pool.wait_ge(product_ready, 8 + j - 1)
                        g.tensor_tensor(pad[:, 2 + j % 2, PAD:], pad[:, j % 2, PAD:], pad[:, j % 2, PAD - 1:PAD + S - 1],
                                        ALU.add).then_inc(pair_ready, 1)
                if s == MID + 1:
                    pool.wait_ge(rstd_done, 1)
                    pool.wait_ge(normed_ready, KT * s)
                    for kt in range(KT):
                        g.tensor_tensor(xT[:, kt, :], xT[:, kt, :], res_rstd[:, 0:S], ALU.mult).then_inc(scaled, 1)
                        pool.wait_ge(scaled, kt + 1)
                        g.tensor_tensor(xT[:, kt, :], xT[:, kt, :], gain[:, G_FINAL + kt:G_FINAL + kt + 1].to_broadcast([P, S]),
                                        ALU.mult).then_inc(xt_ready, 1)
                if s in (2, 4):
                    before = [w for w in plan["pool"] if w["kind"] == "out"][0]["r"] if s == 2 else plan["ff", 0][1]
                    pool.wait_ge(result_taken, before)
                    pool.dma_start(cs[:], rope_table).then_inc(cs_landed, 16)
                if s:
                    pool.wait_ge(z_done, all_stats[s - 1 if s <= MID else s]["zd"] + 1)
                for i in range(sums[s]):
                    pool.wait_ge(sq_ready, n + 1)
                    dst = acc_mid if s == MID and i % 2 else acc
                    ahead = 2 if s == MID else 1
                    if i < ahead:
                        g.tensor_scalar(dst[:], sq[:, n % 2, :], EPS * D / P if dst is acc else 0.0, None, ALU.add).then_inc(acc_done, 1)
                    else:
                        pool.wait_ge(acc_done, n + 1 - ahead)
                        g.tensor_tensor(dst[:], dst[:], sq[:, n % 2, :], ALU.add).then_inc(acc_done, 1)
                    n += 1

        @block.scalar
        def _(act):
            a = nc.scalar
            loop_r = [0]
            count = dict(step=0, sq=0, negm=0, sbd=0)

            def after(ins):
                count["step"] += 1
                ins.then_inc(act_step, 1)
                act.wait_ge(act_step, count["step"])

            def conv(t, loop=None):
                if loop is None:
                    if t >= LAST_T:
                        return
                    act.wait_ge(raw_landed[t // 2 % 2], 16 * (t // 4 + 1))
                    if t >= 4:
                        act.wait_ge(psum_done, freed[t - 4])
                else:
                    act.wait_ge(raw_landed[t // 2 % 2], loop * 64 + 16 * (t // 4 + 1))
                    act.wait_ge(psum_done, loop * 16 + (loop_r[0] + t - 3))
                src, shape = raw_view(t)
                a.activation(w_slot(WH, t, shape), src, ACT.Copy).then_inc(hi_done, 1)

            def prep(row, kt, r, first=False, dst=XH, mid=False):
                act.wait_ge(result_taken, r + 1)
                if row is not None:
                    if first:
                        act.wait_ge(gain_ready, 1)
                    a.activation(dst[:, kt, :], xT[:, kt, :], ACT.Copy, scale=gain[:, row + kt:row + kt + 1]).then_inc(normed_hi_ready, 1)
                for i in range(2 if mid else 1):
                    n = count["sq"]
                    if n >= 2:
                        act.wait_ge(acc_done, n - 1)
                    kw = dict(scale=gain[:, G_FINAL + kt:G_FINAL + kt + 1]) if i else {}
                    a.activation(sq[:, n % 2, :], xT[:, kt, :], ACT.Square, **kw).then_inc(sq_ready, 1)
                    count["sq"] += 1

            def stat(st, c0=0):
                act.wait_ge(z_done, st["zd"] + 1)
                y = (res_rstd if st.get("res") else rstd)[:, c0:]
                after(a.activation(y, Z[:, c0:NS], ACT.Ln))
                a.activation(y, y, ACT.Exp, scale=-0.5).then_inc(rsqrt_ready, 1)

            def mh(src, j, dst=None, **kw):
                a.activation((dst or MH)[:, j, :], src, ACT.Copy, **kw).then_inc(second_hi_ready, 1)

            def sigmoid(s):
                act.wait_ge(result_taken, s["r"] + 1)
                e = sq[:, s["j"] % 2, :]
                after(a.activation(e, tb[:, s["j"] % 2, :], ACT.Exp, scale=-1.0))
                after(a.activation(e, e, ACT.Ln, bias=1.0))
                a.activation(e, e, ACT.Exp, scale=-1.0).then_inc(sigmoid_ready, 1)

            def swa_exp(h):
                act.wait_ge(negm_ready, count["negm"] + 1)
                count["negm"] += 1
                sl = pr[:, h % 3, :]
                for n in range(NB):
                    lo_, hi_ = (0, P) if n == 0 else (256 * n - P, 256 * n + P)
                    a.activation(sl[:, lo_:hi_], sl[:, lo_:hi_], ACT.Exp, bias=small[:, 8 * (h % 2) + n:8 * (h % 2) + n + 1],
                                 accum_out=small[:, 16 + 8 * (h % 2) + n:17 + 8 * (h % 2) + n])
                a.activation(small[:, 20 + 8 * (h % 2):24 + 8 * (h % 2)], small[:, 8 * (h % 2):8 * (h % 2) + 4], ACT.Exp,
                             bias=sink[:, h:h + 1]).then_inc(exp_done, 1)

            def swa_steps(s, half):
                for st in s["steps"]:
                    if st.get("half") != half or st["op"] != "swa_t":
                        continue
                    act.wait_ge(p0_done, st["p0"] + 1)
                    a.activation(pt0[:, 0:512], PP[:, 0, :], ACT.Copy).then_inc(p0_free, 1)
                for st in s["steps"]:
                    if st.get("half") == half and st["op"] == "swa_qk":
                        swa_exp(st["h"])
                for st in s["steps"]:
                    if st.get("half") == half and st["op"] == "swa_t" and st["h"] % 2:
                        act.wait_ge(o_done, st["o"] + 1)
                        a.activation(oraw[:, st["h"] // 2, :], O[:], ACT.Copy).then_inc(o_free, 1)

            def df_out(st, l):
                act.wait_ge(p0_done, st["p0"] + 1)
                mh(PP[:, 0, :], 4 + st["h"], XH, scale=gain[:, G_SUB + l:G_SUB + l + 1])

            def t_first(st):
                act.wait_ge(p0_done, st["p0"] + 1)
                a.activation(pt[:, :, 384:512], PP[:, 0, :].rearrange("p (k q) -> p k q", q=P), ACT.Copy).then_inc(p0_free, 1)

            def layer_begin(s, l):
                beside_sb = any(st["op"] == "sb_qk" for st in s["steps"])
                if beside_sb:
                    conv(s["t"] + 2)
                for st in s["steps"]:
                    if st["op"] == "sb_o":
                        act.wait_ge(o_done, st["o"] + 1)
                        mh(O[:], st["h"] // 2, XH)
                    if st["op"] == "df_f":
                        d = st["h"]
                        outputs = [y for x in plan["layer", l] for y in x["steps"] if y["op"] == "t" and y["df"] and y["h"] == d][0]
                        act.wait_ge(o_done, outputs["o"] + 1)
                        act.wait_ge(df_weights_ready, 3 * (4 * l + d + 1))
                        for n in range(NB):
                            i = a.activation(sq[:, 1, n * P:(n + 1) * P], O[:, n * P:(n + 1) * P], ACT.Square,
                                             scale=small[:, 24 + n:25 + n], accum_out=small[:, 40 + n:41 + n])
                        i.then_inc(sub_squares_ready, 1)
                        act.wait_ge(sub_ms_ready, 4 * l + d + 1)
                        after(a.activation(small[:, 52:56], small[:, 44:48], ACT.Ln))
                        a.activation(small[:, 52:56], small[:, 52:56], ACT.Exp, scale=-0.5).then_inc(sub_rsqrt_ready, 1)
                if not beside_sb:
                    conv(s["t"] + 2)
                for st in s["steps"]:
                    if st["op"] == "sb_qk":
                        for c, (c0, cn, _) in enumerate(CHUNKS):
                            act.wait_ge(z_done, st["zd"] + c + 1)
                            e = ea[:, 0, c0:c0 + cn]
                            after(a.activation(e, Z[:, c0:c0 + cn], ACT.Abs))
                            after(a.activation(e, e, ACT.Exp, scale=-1.0))
                            a.activation(e, e, ACT.Ln, bias=1.0).then_inc(softplus_ready, 1)
                    if st["op"] == "df_qk":
                        for other in s["steps"]:
                            if other["op"] == "t":
                                t_first(other)
                            if other["op"] == "df_f":
                                df_out(other, l)
                        act.wait_ge(negm_ready, count["negm"] + 1)
                        count["negm"] += 1
                        m = st["m"]
                        for n in range(NB):
                            r = ea[:, m, ZOFF[n]:ZOFF[n] + P * (n + 1)]
                            i = a.activation(r, r, ACT.Exp, bias=small[:, 4 * m + n:4 * m + n + 1],
                                             accum_out=small[:, 16 + 4 * m + n:17 + 4 * m + n])
                        i.then_inc(exp_done, 1)

            def layer_end(s, l):
                for st in s["steps"]:
                    if st["op"] == "df_f" and not any(x["op"] == "df_qk" for x in s["steps"]):
                        df_out(st, l)
                    if st["op"] == "t" and not any(x["op"] == "df_qk" for x in s["steps"]):
                        t_first(st)
                for st in s["steps"]:
                    if st["op"] == "sb_qk":
                        for c, (c0, cn, _) in enumerate(CHUNKS):
                            act.wait_ge(sb_logs_ready, count["sbd"] + 1)
                            count["sbd"] += 1
                            a.activation(ea[:, 1 + st["h"] % 2, c0:c0 + cn], ea[:, 1 + st["h"] % 2, c0:c0 + cn], ACT.Exp).then_inc(sb_weights_ready, 1)
                for st in s["steps"]:
                    if st["op"] == "t" and not st["df"]:
                        act.wait_ge(p0_done, st["p0"] + 2)
                        a.activation(pt[:, 0:2, 128:256], PP[:, 0, 0:256].rearrange("p (k q) -> p k q", q=P), ACT.Copy).then_inc(p0_free, 1)

            act.preload_act_table_set("natural_log_exp_and_others")
            for dst, src in gains[:4]:
                act.dma_start(dst, src).then_inc(gains_landed, 16)
            for dst, src in common:
                act.dma_start(dst, src).then_inc(par_landed, 16)
            for kt in range(KT):
                prep(G_NORM, kt, kt, True)
                if kt in (3, 6):
                    conv(kt // 6)
            act.wait_ge(lam_dot, 2 * DEPTH)
            a.activation(lame[:], lamd[:], ACT.Exp).then_inc(lam_exp, 1)
            for s in plan["attn"]:
                t, j = s["t"], s["j"]
                kind = s["kind"]
                conv(t + 2)
                for st in s["steps"]:
                    if st["op"] == "stat":
                        stat(st)
                for half in range(2):
                    swa_steps(s, half)
                if kind == "z":
                    if j:
                        act.wait_ge(product_ready, j)
                        mh(oraw[:, j - 1, :], j - 1)
                    sigmoid(s)
                    if j == 7:
                        act.wait_ge(product_ready, 8)
                        mh(oraw[:, 7, :], 7)
                if kind == "out":
                    prep(G_NORM + 8, j, s["r"])
            for s in plan["pool"]:
                t, j, kind = s["t"], s["j"], s["kind"]
                if kind != "mix":
                    conv(t + 2)
                for st in s["steps"]:
                    stat(st)
                if kind == "pu" and j or kind == "pz" and j == 0:
                    i = j - 1 if j else 7
                    act.wait_ge(product_ready, 8 + i + 1)
                    mh(pf[:, i % 2, :], i)
                if kind == "pz" and j < 7:
                    sigmoid(s)
                if kind == "mix":
                    if j == 0:
                        sigmoid(plan["pool"][15])
                    conv(t + 2)
                    for i in range(4):
                        act.wait_ge(result_taken, s["r"] + i + 1)
                        mh(tb[:, i % 2, :], 2 * i + j, XH)
                if kind == "out":
                    prep(G_MID, j, s["r"], dst=MH, mid=True)
            for l in range(DEPTH):
                for s in plan["layer", l]:
                    t, j = s["t"], s["j"]
                    layer_begin(s, l)
                    layer_end(s, l)
                    if s["kind"] in ("dfk", "dfq"):
                        act.wait_ge(psum_done, s["r"] + 1)
                        act.wait_ge(result_taken, s["r"])
                        for q in range(4):
                            o = q ^ 1
                            i = a.activation(tb[32 * q:32 * q + 32, 0, :], U[32 * o:32 * o + 32, s["r"] % 2, :], ACT.Copy)
                        i.then_inc(rope_shifted, 1)
                    for st in s["steps"]:
                        if st["op"] == "stat":
                            stat(st)
                    if s["kind"] == "wo" and s["second"]:
                        for i in range(2):
                            prep(G_MLP + 8 * l, 2 * (j - 4) + i, s["r"] + i, dst=MH)
                t0, r0 = plan["ff", l]
                loop_r[0] = r0 - t0

                def ff_block(b, first=False, last=False):
                    for i in range(16):
                        if t0 + 16 * (BLOCKS - 1) + i + 2 < LAST_T or not last:
                            conv(t0 + i + 2, b)
                        if first and i == 0:
                            stat(plan["ff_stat", l])
                        if i < 8:
                            act.wait_ge(result_taken, b * 16 + (r0 + i + 1))
                            a.activation(sq[:, i % 2, :], tb[:, i % 2, :], ACT.Square).then_inc(relu_squared, 1)
                            a.activation(XH[:, i, :], tb[:, i % 2, :], ACT.Square).then_inc(second_hi_ready, 1)
                        elif last:
                            prep(G_ATTN + 8 * (l + 1) if l < DEPTH - 1 else None, i - 8, r0 + 16 * b + i, dst=MH)

                ff_block(0, first=True)
                with act.Fori(1, BLOCKS - 1) as b:
                    ff_block(b)
                ff_block(BLOCKS - 1, last=True)
            stat(plan["last_stat"], S)
            act.wait_ge(rstd_done, 2)
            for m in range(1, 2 * NB, 2):
                n, c = m % NB, 512 * (m // NB)
                act.wait_ge(y_done, m + 1)
                a.activation(yrow[:, n, c:c + 512], y_bank(m), ACT.Copy, scale=rstd[:, S + n:S + n + 1]).then_inc(y_act, 1)

        @block.vector
        def _(dve):
            v = nc.vector
            loop_r = [0]
            count = dict(step=0, xh=0, exp=0, mh=0, stat=0, sbl=0, usq=0, ss=0)

            def after(ins):
                count["step"] += 1
                ins.then_inc(dve_step, 1)
                dve.wait_ge(dve_step, count["step"])

            def conv(t, loop=None):
                if loop is None:
                    if t >= LAST_T:
                        return
                    dve.wait_ge(raw_landed[t // 2 % 2], 16 * (t // 4 + 1))
                    dve.wait_ge(hi_done, t + 1)
                    if t >= 4:
                        dve.wait_ge(psum_done, freed[t - 4])
                else:
                    dve.wait_ge(raw_landed[t // 2 % 2], loop * 64 + 16 * (t // 4 + 1))
                    dve.wait_ge(hi_done, loop * 16 + (t + 1))
                    dve.wait_ge(psum_done, loop * 16 + (loop_r[0] + t - 3))
                src, shape = raw_view(t)
                v.tensor_tensor(w_slot(WL, t, shape), src, w_slot(WH, t, shape).bitcast(F32), ALU.subtract).then_inc(lo_done, 1)

            def prep_lo(row, kt, to=(XH, XL)):
                count["xh"] += 1
                dve.wait_ge(normed_hi_ready, count["xh"])
                v.scalar_tensor_tensor(out=to[1][:, kt, :], in0=xT[:, kt, :], scalar=gain[:, row + kt:row + kt + 1],
                                       in1=to[0][:, kt, :].bitcast(F32), op0=ALU.mult, op1=ALU.subtract).then_inc(normed_ready, 1)

            def stat(st, c0=0):
                count["stat"] += 1
                dve.wait_ge(z_done, st["zd"] + 1)
                dve.wait_ge(rsqrt_ready, count["stat"])
                y, t = (res_rstd if st.get("res") else rstd)[:, c0:], nt[:, c0:]
                after(v.scalar_tensor_tensor(out=t, in0=y, scalar=-0.5, in1=y, op0=ALU.mult, op1=ALU.mult))
                v.tensor_tensor(t, t, Z[:, c0:NS], ALU.mult).then_inc(z_free, 1)
                dve.wait_ge(z_free, st["z"] + 1)
                i = v.scalar_tensor_tensor(out=y, in0=t, scalar=1.5, in1=y, op0=ALU.add, op1=ALU.mult)
                if c0 == 0 and not st.get("res"):
                    after(i)
                else:
                    i.then_inc(rstd_done, 1)

            def result(r, loop=None):
                if loop is None:
                    dve.wait_ge(psum_done, r + 1)
                    if r:
                        dve.wait_ge(result_taken, r)
                else:
                    dve.wait_ge(psum_done, loop * 16 + (r + 1))
                    dve.wait_ge(result_taken, loop * 16 + r)
                return U[:, r % 2, :]

            def low(full, j, dst=None, hi=None):
                count["mh"] += 1
                dve.wait_ge(second_hi_ready, count["mh"])
                v.tensor_tensor((dst or ML)[:, j, :], full, (hi or MH)[:, j, :].bitcast(F32), ALU.subtract).then_inc(second_ready, 1)

            def swa_softmax_a(st):
                h = st["h"]
                sl = pr[:, h % 3, :]
                b = 8 * (h % 2)
                dve.wait_ge(z_done, st["zd"] + 1)
                if h >= 3:
                    dve.wait_ge(p0_done, swa_t_of[h - 3]["p0"] + 1)
                    dve.wait_ge(p1_done, swa_t_of[h - 3]["p1"] + 1)
                for n in range(NB):
                    lo_, hi_ = (0, P) if n == 0 else (256 * n - P, 256 * n + P)
                    i = v.tensor_tensor_reduce(sl[:, lo_:hi_], Z[:, P + lo_:P + hi_], mask_sw[:, (P if n == 0 else 0):256],
                                               1.0, sink[:, h:h + 1], ALU.add, ALU.max, small[:, 32 + b + n:33 + b + n])
                i.then_inc(z_free, 1)
                dve.wait_ge(z_free, st["z"] + 1)
                v.tensor_scalar(small[:, b:b + 4], small[:, 32 + b:36 + b], -1.0, None, ALU.mult).then_inc(negm_ready, 1)

            def swa_softmax_b(h):
                b = 8 * (h % 2)
                dve.wait_ge(exp_done, h + 1)
                after(v.tensor_tensor(small[:, 16 + b:20 + b], small[:, 16 + b:20 + b], small[:, 20 + b:24 + b], ALU.add))
                after(v.reciprocal(small[:, 36 + b:40 + b], small[:, 16 + b:20 + b]))
                for n in range(NB):
                    lo_, hi_ = (0, P) if n == 0 else (256 * n - P, 256 * n + P)
                    r = pr[:, h % 3, lo_:hi_]
                    i = v.tensor_scalar(r, r, small[:, 36 + b + n:37 + b + n], None, ALU.mult)
                i.then_inc(probs_ready, 1)

            def swa_steps(s, half):
                for st in s["steps"]:
                    if st.get("half") == half and st["op"] == "swa_qk":
                        swa_softmax_a(st)
                for st in s["steps"]:
                    if st.get("half") == half and st["op"] == "swa_t":
                        dve.wait_ge(p1_done, st["p1"] + 1)
                        v.tensor_copy(pt0[:, 512:896], PP[:, 1, 0:384]).then_inc(p1_free, 1)
                        if st["h"] + 1 < 16:
                            swa_softmax_b(st["h"] + 1)
                    elif st.get("half") == half and st["op"] == "swa_qk" and st["h"] == 1:
                        swa_softmax_b(0)

            def t_rest(st):
                dve.wait_ge(p1_done, st["p1"] + 1)
                v.tensor_copy(pt[:, 0:3, 256:384], PP[:, 1, 0:384].rearrange("p (k q) -> p k q", q=P))
                v.tensor_copy(pt[:, 0, 0:128], PP[:, 1, 384:512]).then_inc(p1_free, 1)
                if st["df"]:
                    dve.wait_ge(p0_done, st["p0"] + 2)
                    v.tensor_copy(pt[:, 0:2, 128:256], PP[:, 0, 0:256].rearrange("p (k q) -> p k q", q=P)).then_inc(p0_free, 1)

            def layer_begin(s, l):
                for st in s["steps"]:
                    if st["op"] == "sb_o":
                        count["mh"] += 1
                        dve.wait_ge(second_hi_ready, count["mh"])
                        j = st["h"] // 2
                        v.tensor_tensor(XL[:, j, :], O[:], XH[:, j, :].bitcast(F32), ALU.subtract).then_inc(second_ready, 1)
                        dve.wait_ge(second_ready, count["mh"])
                        dve.sem_inc(o_free, 1)
                    if st["op"] == "df_f":
                        count["ss"] += 1
                        dve.wait_ge(sub_squares_ready, count["ss"])
                        lam_init = 0.8 - 0.6 * math.exp(-0.3 * l)
                        after(v.tensor_scalar(small[:, 44:48], small[:, 40:44], 1.0 / P, EPS, ALU.mult, ALU.add))
                        v.tensor_copy(small[:, 48:52], small[:, 44:48]).then_inc(sub_ms_ready, 1)
                        dve.wait_ge(sub_ms_ready, count["ss"])
                        dve.wait_ge(sub_rsqrt_ready, count["ss"])
                        after(v.tensor_tensor(small[:, 56:60], small[:, 52:56], small[:, 52:56], ALU.mult))
                        after(v.tensor_tensor(small[:, 56:60], small[:, 56:60], small[:, 44:48], ALU.mult))
                        after(v.tensor_scalar(small[:, 56:60], small[:, 56:60], -0.5, 1.5, ALU.mult, ALU.add))
                        after(v.tensor_tensor(small[:, 56:60], small[:, 56:60], small[:, 52:56], ALU.mult))
                        after(v.scalar_tensor_tensor(out=small[:, 56:60], in0=small[:, 56:60], scalar=1.0 - lam_init,
                                                     in1=small[:, 24:28], op0=ALU.mult, op1=ALU.mult))
                        for n in range(NB):
                            i = v.tensor_scalar(tb[:, 1, n * P:(n + 1) * P], O[:, n * P:(n + 1) * P], small[:, 56 + n:57 + n], None, ALU.mult)
                        i.then_inc(df_out_ready, 1)
                        dve.wait_ge(df_out_ready, count["ss"])
                        dve.sem_inc(o_free, 1)
                for st in s["steps"]:
                    if st["op"] == "df_qk":
                        m = st["m"]
                        dve.wait_ge(z_done, st["zd"] + 1)
                        if 4 * l + st["h"]:
                            dve.wait_ge(df_weights_ready, 3 * (4 * l + st["h"]))
                        for n in range(NB):
                            w = P * (n + 1)
                            i = v.tensor_tensor_reduce(ea[:, m, ZOFF[n]:ZOFF[n] + w], Z[:, ZOFF[n]:ZOFF[n] + w], mask_df[:, 512 - w:512],
                                                       1.0, -3.0e38, ALU.add, ALU.max, small[:, 32 + 4 * m + n:33 + 4 * m + n])
                        i.then_inc(z_free, 1)
                        dve.wait_ge(z_free, st["z"] + 1)
                        v.tensor_scalar(small[:, 4 * m:4 * m + 4], small[:, 32 + 4 * m:36 + 4 * m], -1.0, None, ALU.mult).then_inc(negm_ready, 1)
                    if st["op"] == "sb_qk":
                        if st["h"] == 0:
                            dve.wait_ge(df_weights_ready, 3 * (4 * l + 4))
                        for c, (c0, cn, blocks) in enumerate(CHUNKS):
                            count["sbl"] += 1
                            dve.wait_ge(softplus_ready, count["sbl"])
                            e, z = ea[:, 0, c0:c0 + cn], Z[:, c0:c0 + cn]
                            after(v.scalar_tensor_tensor(out=e, in0=z, scalar=0.0, in1=e, op0=ALU.max, op1=ALU.add))
                            for n in blocks:
                                z0, z1 = ZOFF[n], ZOFF[n] + P * (n + 1)
                                i = v.tensor_tensor_scan(rev(cc, z0, z1), ones[:].to_broadcast([P, z1 - z0]), rev(ea[:, 0, :], z0, z1), 0.0, ALU.mult, ALU.add)
                            after(i)
                            v.tensor_tensor(ea[:, 1 + st["h"] % 2, c0:c0 + cn], z, cc[:, c0:c0 + cn], ALU.subtract).then_inc(sb_logs_ready, 1)
                        dve.wait_ge(sb_logs_ready, count["sbl"])
                        dve.sem_inc(z_free, 1)

            def combine(s, l):
                for st in s["steps"]:
                    if st["op"] == "df_qk":
                        count["exp"] += 1
                        if st["m"] == 1:
                            dve.wait_ge(exp_done, 16 + count["exp"])
                            after(v.reciprocal(small[:, 24:32], small[:, 16:24]))
                            after(v.scalar_tensor_tensor(out=small[:, 8:12], in0=small[:, 16:20], scalar=neglam[:, l:l + 1],
                                                         in1=small[:, 28:32], op0=ALU.mult, op1=ALU.mult))
                            for _, _, blocks in CHUNKS:
                                for n in blocks:
                                    z0, z1 = ZOFF[n], ZOFF[n] + P * (n + 1)
                                    i = v.scalar_tensor_tensor(out=cc[:, z0:z1], in0=ea[:, 1, z0:z1], scalar=small[:, 8 + n:9 + n],
                                                               in1=ea[:, 0, z0:z1], op0=ALU.mult, op1=ALU.add)
                                i.then_inc(df_weights_ready, 1)

            def layer_end(s, l):
                for st in s["steps"]:
                    if st["op"] == "df_f":
                        count["mh"] += 1
                        dve.wait_ge(second_hi_ready, count["mh"])
                        j = 4 + st["h"]
                        v.scalar_tensor_tensor(out=XL[:, j, :], in0=PP[:, 0, :], scalar=gain[:, G_SUB + l:G_SUB + l + 1],
                                               in1=XH[:, j, :].bitcast(F32), op0=ALU.mult, op1=ALU.subtract).then_inc(second_ready, 1)
                        dve.wait_ge(second_ready, count["mh"])
                        dve.sem_inc(p0_free, 1)
                combine(s, l)
                for st in s["steps"]:
                    if st["op"] == "t" and any(x["op"] == "sb_qk" for x in s["steps"]):
                        t_rest(st)

            dve.wait_ge(gain_done, 1)
            v.tensor_copy(gain[:, 0:GROWS], Z[:, 0:GROWS]).then_inc(gain_ready, 1)
            dve.wait_ge(gain_ready, 1)
            v.tensor_tensor(gain[:, G_MID:G_MID + KT], gain[:, G_FINAL:G_FINAL + KT], gain[:, G_ATTN:G_ATTN + KT], ALU.mult)
            for kt in range(KT):
                result(kt)
                v.tensor_copy(xT[:, kt, :], x_bank(kt)).then_inc(result_taken, 1)
                if kt:
                    prep_lo(G_NORM, kt - 1)
                if kt in (4, 7):
                    conv(kt // 7)
            dve.wait_ge(result_taken, KT)
            prep_lo(G_NORM, KT - 1)
            dve.wait_ge(par_landed, 16 * len(common))
            for l in range(DEPTH):
                for i in range(2):
                    c = slice(64 * l, 64 * l + 64)
                    v.tensor_tensor_reduce(lamw[:], lamv[:, 2 * i, c], lamv[:, 2 * i + 1, c], 1.0, 0.0, ALU.mult, ALU.add,
                                           lamd[:, 2 * l + i:2 * l + i + 1]).then_inc(lam_dot, 1)
                    dve.wait_ge(lam_dot, 2 * l + i + 1)
            dve.wait_ge(const_ready, 1)

            def add_x(ps, kt, last, r):
                i = v.tensor_tensor(xT[:, kt, :], xT[:, kt, :], ps, ALU.add)
                i.then_inc(result_taken, 1)
                if last:
                    dve.wait_ge(result_taken, r + 1)

            def gated(i):
                dve.wait_ge(sigmoid_ready, i + 1)
                dve.wait_ge(zo_ready, i + 1)
                v.tensor_tensor(oraw[:, i, :], sq[:, i % 2, :], oraw[:, i, :], ALU.mult).then_inc(product_ready, 1)

            def silu_scale(i):
                dve.wait_ge(sigmoid_ready, 8 + i + 1)
                after(v.scalar_tensor_tensor(out=sz[:, i, :], in0=tb[:, i % 2, :], scalar=gain[:, G_SCALE + i:G_SCALE + i + 1],
                                             in1=sq[:, i % 2, :], op0=ALU.mult, op1=ALU.mult))

            for s in plan["attn"]:
                t, j, kind, r = s["t"], s["j"], s["kind"], s["r"]
                def tiles_before():
                    if j:
                        gated(j - 1)
                    if j >= 2:
                        low(oraw[:, j - 2, :], j - 2)

                if kind == "z" and not s["steps"]:
                    tiles_before()
                swa_steps(s, 0)
                conv(t + 2)
                swa_steps(s, 1)
                if kind == "z" and s["steps"]:
                    tiles_before()
                ps = result(r)
                rb = rstd[:, 0:S]
                if kind == "k":
                    for g in range(2):
                        src = slice(64 * g, 64 * g + 64)
                        for half in range(2):
                            dst = slice(64 * half, 64 * half + 64)
                            if j:
                                i = v.tensor_tensor(kd[dst, 2 * j + g, :], U[src, r % 2, :], rstd[dst, 0:S], ALU.mult)
                            else:
                                i = v.tensor_copy(kd[dst, 2 * j + g, :], U[src, r % 2, :])
                    i.then_inc(result_taken, 1)
                    if j == 0:
                        for st in s["steps"]:
                            stat(st)
                        dve.wait_ge(result_taken, r + 1)
                        for g in range(2):
                            v.tensor_tensor(kd[:, g, :], kd[:, g, :], rb, ALU.mult)
                        dve.wait_ge(lam_exp, 1)
                        for l in range(DEPTH):
                            lam_init = 0.8 - 0.6 * math.exp(-0.3 * l)
                            v.scalar_tensor_tensor(out=neglam[:, l:l + 1], in0=lame[:, 2 * l + 1:2 * l + 2], scalar=-lam_init,
                                                   in1=lame[:, 2 * l:2 * l + 1], op0=ALU.add, op1=ALU.subtract)
                elif kind == "v":
                    for i in range(2):
                        ps = result(r + i)
                        n = 2 * j + i
                        v.tensor_scalar(v0[:, n, :], ps[:, 0:256], rstd[:, S + n:S + n + 1], None, ALU.mult).then_inc(result_taken, 1)
                elif kind == "q":
                    v.scalar_tensor_tensor(out=q0[:, j % 4, :], in0=ps, scalar=0.125, in1=rb, op0=ALU.mult, op1=ALU.mult).then_inc(result_taken, 1)
                elif kind == "z":
                    v.tensor_tensor(tb[:, j % 2, :], ps, rb, ALU.mult).then_inc(result_taken, 1)
                    if j == 7:
                        low(oraw[:, 6, :], 6)
                        gated(7)
                        dve.wait_ge(product_ready, 8)
                        low(oraw[:, 7, :], 7)
                elif kind == "out":
                    add_x(ps, j, True, r)
                    prep_lo(G_NORM + 8, j)
            def pooled(j):
                w = POOL_W[j // 2]
                u = pad[:, j % 2, PAD:]
                dve.wait_ge(pair_ready, j + 1)
                dve.wait_ge(product_ready, 8 + j)
                src, sh = 2 + j % 2, 2
                while sh < w:
                    dst = 5 if src == 4 else 4
                    after(v.tensor_tensor(pad[:, dst, PAD:], pad[:, src, PAD:], pad[:, src, PAD - sh:PAD + S - sh], ALU.add))
                    src, sh = dst, 2 * sh
                head = pad[:, src, PAD:PAD + w]
                after(v.scalar_tensor_tensor(out=head, in0=head, scalar=float(w), in1=inv_n[:, 0:w], op0=ALU.mult, op1=ALU.mult))
                if j >= 2:
                    dve.wait_ge(second_ready, 8 + j - 1)
                v.scalar_tensor_tensor(out=pf[:, j % 2, :], in0=pad[:, src, PAD:], scalar=1.0 / w, in1=u,
                                       op0=ALU.mult, op1=ALU.subtract).then_inc(product_ready, 1)

            after(v.memset(pad[:, :, 0:PAD], 0.0))
            for s in plan["pool"]:
                t, j, kind, r = s["t"], s["j"], s["kind"], s["r"]
                i = j + 8 * (kind == "pz")
                if kind in ("pu", "pz") and 2 <= i <= 9:
                    low(pf[:, i % 2, :], i - 2)
                if kind in ("pu", "pz") and 1 <= i <= 8:
                    pooled(i - 1)
                if kind == "pz" and j:
                    silu_scale(j - 1)
                if kind != "mix":
                    conv(t + 2)
                for st in s["steps"]:
                    stat(st)
                ps = result(r)
                rb = rstd[:, 0:S]
                if kind == "pu":
                    v.tensor_tensor(pad[:, j % 2, PAD:], ps, rb, ALU.mult).then_inc(result_taken, 1)
                elif kind == "pz":
                    v.tensor_tensor(tb[:, j % 2, :], ps, rb, ALU.mult).then_inc(result_taken, 1)
                elif kind == "mix":
                    for i in range(4):
                        if i:
                            ps = result(r + i)
                        c = 2 * i + j
                        dve.wait_ge(second_ready, count["mh"])
                        v.tensor_tensor(tb[:, i % 2, :], ps, sz[:, c, :], ALU.mult).then_inc(result_taken, 1)
                        if i == 0 and j == 0:
                            silu_scale(7)
                        if i:
                            low(tb[:, (i - 1) % 2, :], c - 2, XL, XH)
                        if i == 1:
                            conv(t + 2)
                    dve.wait_ge(result_taken, r + 4)
                    low(tb[:, 1, :], 6 + j, XL, XH)
                elif kind == "out":
                    add_x(ps, j, True, r)
                    prep_lo(G_MID, j, (MH, ML))
            ropes = 0
            for l in range(DEPTH):
                for s in plan["layer", l]:
                    t, j, kind, r = s["t"], s["j"], s["kind"], s["r"]
                    first = any(st["op"] == "sb_qk" for st in s["steps"])
                    if first:
                        conv(t + 2)
                    layer_begin(s, l)
                    if not first:
                        for st in s["steps"]:
                            if st["op"] == "t":
                                t_rest(st)
                        if not s.get("second"):
                            conv(t + 2)
                    if kind == "dfk" and j == 0:
                        dve.wait_ge(cs_landed, 16 * (l + 1))
                    layer_end(s, l)
                    ps = result(r)
                    rb = rstd[:, 0:S]
                    if kind in ("dfk", "dfq"):
                        ropes += 1
                        dve.wait_ge(rope_shifted, ropes)
                        scale = 0.125 if kind == "dfq" else 1.0
                        v.scalar_tensor_tensor(out=qk[kind][:, j, :], in0=ps, scalar=scale, in1=cs[:, 0, :], op0=ALU.mult, op1=ALU.mult)
                        after(v.scalar_tensor_tensor(out=tb[:, 0, :], in0=tb[:, 0, :], scalar=scale, in1=cs[:, 1, :], op0=ALU.mult, op1=ALU.mult))
                        v.tensor_tensor(qk[kind][:, j, :], tb[:, 0, :], qk[kind][:, j, :], ALU.add).then_inc(result_taken, 1)
                    elif kind == "sbk":
                        v.tensor_tensor(qk[kind][:, j, :], ps, rb, ALU.mult).then_inc(result_taken, 1)
                    elif kind == "sbq":
                        v.scalar_tensor_tensor(out=qk[kind][:, j, :], in0=ps, scalar=0.125, in1=rb, op0=ALU.mult, op1=ALU.mult).then_inc(result_taken, 1)
                    elif kind in ("dfv", "sbv"):
                        for i in range(2):
                            if i:
                                ps = result(r + i)
                            n = 2 * (j % 2) + i
                            c = 256 * (j // 2)
                            v.tensor_scalar(qk[kind][:, n, c:c + 256], ps[:, 0:256], rstd[:, S + n:S + n + 1], None, ALU.mult).then_inc(result_taken, 1)
                    elif kind == "wo":
                        if l == 0 and j == 0:
                            dve.wait_ge(xt_ready, KT)
                        for i in range(2):
                            if i:
                                ps = result(r + i)
                            kt = 2 * (j % 4) + i
                            add_x(ps, kt, s["second"], r + i)
                            if s["second"] and i == 0:
                                conv(t + 2)
                            if s["second"]:
                                prep_lo(G_MLP + 8 * l, kt, (MH, ML))
                    for st in s["steps"]:
                        if st["op"] == "stat":
                            stat(st)
                            if not st.get("res"):
                                v.tensor_tensor(keys[:, 0, :], keys[:, 0, :], rstd[:, 0:S], ALU.mult)
                                for i in range(2):
                                    after(v.tensor_tensor(cs[:, i, :], cs[:, i, :], rstd[:, 0:S], ALU.mult))
                t0, r0 = plan["ff", l]
                loop_r[0] = r0 - t0
                m0 = count["mh"]
                u0 = count["usq"]

                def ff_block(b, first=False, last=False):
                    for i in range(16):
                        if t0 + 16 * (BLOCKS - 1) + i + 2 < LAST_T or not last:
                            conv(t0 + i + 2, b)
                        if first and i == 0:
                            stat(plan["ff_stat", l])
                        ps = result(r0 + i, b)
                        if i < 8:
                            v.scalar_tensor_tensor(out=tb[:, i % 2, :], in0=ps, scalar=0.0, in1=rstd[:, 0:S], op0=ALU.max,
                                                   op1=ALU.mult).then_inc(result_taken, 1)
                            dve.wait_ge(relu_squared, b * 8 + (u0 + i + 1))
                            dve.wait_ge(second_hi_ready, b * 8 + (m0 + i + 1))
                            v.tensor_tensor(XL[:, i, :], sq[:, i % 2, :], XH[:, i, :].bitcast(F32), ALU.subtract).then_inc(second_ready, 1)
                        else:
                            kt = i - 8
                            add_x(ps, kt, last, r0 + 16 * b + i if last else None)
                            if last and l < DEPTH - 1:
                                prep_lo(G_ATTN + 8 * (l + 1), kt, (MH, ML))
                            elif last:
                                v.tensor_scalar(xf[:, kt, :], xT[:, kt, :], gain[:, G_LAST + kt:G_LAST + kt + 1], None, ALU.mult).then_inc(xt_ready, 1)

                ff_block(0, first=True)
                with dve.Fori(1, BLOCKS - 1) as b:
                    ff_block(b)
                ff_block(BLOCKS - 1, last=True)
                count["mh"] += 8 * BLOCKS
                count["usq"] += 8 * BLOCKS
            stat(plan["last_stat"], S)
            dve.wait_ge(rstd_done, 2)
            for m in range(0, 2 * NB, 2):
                n, c = m % NB, 512 * (m // NB)
                dve.wait_ge(y_done, m + 1)
                v.tensor_scalar(yrow[:, n, c:c + 512], y_bank(m), rstd[:, S + n:S + n + 1], None, ALU.mult).then_inc(y_dve, 1)

        @block.tensor
        def _(pe):
            mm = nc.tensor.matmul

            def begin(r, loop=None):
                if r < KT + 2:
                    need = {KT - 1: 2, KT: 1, KT + 1: KT}.get(r)
                    if need:
                        pe.wait_ge(result_taken, need)
                elif loop is None:
                    if r >= 2:
                        pe.wait_ge(result_taken, r - 1)
                else:
                    pe.wait_ge(result_taken, loop * 16 + (r - 1))
                return U[:, r % 2, :]

            def three(o, wh, wl, xh, xl, first, last, **kw):
                mm(o, wl, xh, start=first, stop=False, **kw)
                mm(o, wh, xl, start=False, stop=False, **kw)
                return mm(o, wh, xh, start=False, stop=last, **kw)

            def tile_parts(s, kts=None, ready=None):
                kind, t, r = s["kind"], s["t"], s["r"]
                a, al = operands[s["operand"]]

                def part(i):
                    if i == 0 and kind[-1] != "v":
                        pe.wait_ge(lo_done, t + 1)
                    if i == 0 and kind[-1] == "v":
                        pe.wait_ge(lo_done, t - t % 2 + 2)
                    if kind == "wo":
                        res, k0 = r + i // 2, 2 * (i % 2)
                        o = begin(res) if i % 2 == 0 else U[:, res % 2, :]
                        base = 0 if s["second"] else 4
                        for k in range(k0, k0 + 2):
                            if ready and i < 2:
                                pe.wait_ge(second_ready, ready[k])
                            c = slice(256 * k + P * (i // 2), 256 * k + P * (i // 2) + P)
                            last = three(o, WH[:, t % 4, c], WL[:, t % 4, c], a[:, base + k, :], al[:, base + k, :], k == 0, k == 3)
                        if i % 2:
                            last.then_inc(psum_done, 1)
                    elif kind == "mix":
                        g = i
                        o = begin(r + g)
                        for k in range(2):
                            c = slice(P * (2 * g + k), P * (2 * g + k) + P)
                            last = three(o, WH[:, t % 4, c], WL[:, t % 4, c], a[:, 2 * g + k, :], al[:, 2 * g + k, :], k == 0, k == 1)
                        last.then_inc(psum_done, 1)
                    elif kind[-1] == "v":
                        res = r + i // 2
                        n = 2 * (s["j"] % 2) + i // 2
                        o = begin(res) if i % 2 == 0 else U[:, res % 2, :]
                        t2 = t - t % 2
                        s2 = t2 % 4
                        q = slice(P * n, P * n + P)
                        for k in range(4 * (i % 2), 4 * (i % 2) + 4):
                            c = slice(P * k, P * k + P)
                            wh, wl = WH[:, s2:s2 + 2, c], WL[:, s2:s2 + 2, c]
                            o2 = o[:, 0:256]
                            mm(o2, a[:, k, q], wl, start=k == 0, stop=False)
                            mm(o2, al[:, k, q], wh, start=False, stop=False)
                            last = mm(o2, a[:, k, q], wh, start=False, stop=k == 7)
                        if i % 2:
                            last.then_inc(psum_done, 1)
                    else:
                        o = begin(r) if i == 0 else U[:, r % 2, :]
                        order = kts or list(range(8))
                        for k in order[2 * i:2 * i + 2]:
                            if ready:
                                pe.wait_ge(ready["sem"], ready[k])
                            c = slice(P * k, P * k + P)
                            last = three(o, WH[:, t % 4, c], WL[:, t % 4, c], a[:, k, :], al[:, k, :], k == order[0], k == order[7])
                        if i == 3:
                            last.then_inc(psum_done, 1)
                return [lambda i=i: part(i) for i in range(4)]

            def stat(st):
                if not st.get("res"):
                    pe.wait_ge(acc_done, sum(squares[:stats[0] + 1]))
                    stats[0] += 1
                if st["z"]:
                    pe.wait_ge(z_free, st["z"])
                terms = [(eps_w, acc), (mean_w, acc_mid)] if st.get("mid") else [(mean_w, acc)]
                for i, (w, x) in enumerate(terms):
                    mm(Z[:, 0:S], w[:], x[:], start=i == 0, stop=i == len(terms) - 1)
                for n in range(NB):
                    for i, (w, x) in enumerate(terms):
                        last = mm(Z[:, 512 + n:513 + n], x[:, P * n:P * n + P], w[:, 0:1], start=i == 0, stop=i == len(terms) - 1)
                last.then_inc(z_done, 1)

            stats = [0]
            pe.wait_ge(const_ready, 1)
            pe.wait_ge(gains_landed, 16 * len(gains))
            nc.tensor.transpose(Z[:, 0:GROWS], grow[:], ident[0:GROWS, 0:GROWS]).then_inc(gain_done, 1)
            for kt in range(KT):
                pe.wait_ge(in_landed, 16 * (1 + kt // (KT // 2)))
                begin(kt)
                o = x_bank(kt)
                for n in range(NB):
                    i = nc.tensor.transpose(o[:, P * n:P * n + P], xin[:, n, P * kt:P * kt + P], ident[:])
                i.then_inc(psum_done, 1)
            pe.wait_ge(gain_ready, 1)

            def swa_qk(st):
                h = st["h"]
                j, g, b = h // 2, h // 4, 64 * (h % 2)
                q = [s for s in plan["attn"] if s["kind"] == "q" and s["j"] == j][0]
                pe.wait_ge(result_taken, q["r"] + 1)
                pe.wait_ge(z_free, st["z"])
                rows_ = slice(b, b + 64)
                for n in range(NB):
                    k0 = max(n - 1, 0) * P
                    o0 = 256 * n + (P if n == 0 else 0)
                    i = mm(Z[:, o0:256 * n + 256], q0[rows_, j % 4, P * n:P * n + P], kd[rows_, g, k0:P * n + P], start=True, stop=True)
                i.then_inc(z_done, 1)

            def swa_t(st):
                h = st["h"]
                pe.wait_ge(probs_ready, h + 1)
                if st["p0"]:
                    pe.wait_ge(p0_free, st["p0"])
                for k in range(4):
                    i = nc.tensor.transpose(PP[:, 0, P * k:P * k + P], pr[:, h % 3, P * k:P * k + P], ident[:])
                i.then_inc(p0_done, 1)
                if st["p1"]:
                    pe.wait_ge(p1_free, st["p1"])
                for k in range(3):
                    i = nc.tensor.transpose(PP[:, 1, P * k:P * k + P], pr[:, h % 3, 512 + P * k:640 + P * k], ident[:])
                i.then_inc(p1_done, 1)

            def swa_pv(st):
                h = st["h"]
                g, b = h // 4, 64 * (h % 2)
                pe.wait_ge(p0_free, st["p0"] + 1)
                pe.wait_ge(p1_free, st["p1"] + 1)
                if h % 2 == 0 and st["o"]:
                    pe.wait_ge(o_free, st["o"])
                for n in range(NB):
                    w = 256 if n < NB - 1 else P
                    i = mm(O[b:b + 64, P * n:P * n + w], v0[:, n, 64 * g:64 * g + 64], pt0[:, 256 * n:256 * n + w],
                           start=n == 0, stop=n == NB - 1, skip_group_check=True)
                if h % 2:
                    i.then_inc(o_done, 1)

            for s in plan["attn"]:
                kind = s["kind"]
                ready = None
                if s["t"] == 0:
                    ready = {"sem": normed_ready, **{k: k + 1 for k in range(8)}}
                if kind == "out" and s["j"] == 0:
                    ready = {"sem": second_ready, **{k: k + 1 for k in range(8)}}
                parts = tile_parts(s, ready=ready)
                for half in range(2):
                    steps = [st for st in s["steps"] if st.get("half") == half]
                    for st in steps:
                        if st["op"] == "swa_qk":
                            swa_qk(st)
                    for st in steps:
                        if st["op"] == "swa_t":
                            swa_t(st)
                    parts[2 * half]()
                    parts[2 * half + 1]()
                    for st in steps:
                        if st["op"] == "swa_t":
                            swa_pv(st)
                for st in s["steps"]:
                    if st["op"] == "stat":
                        stat(st)
            for s in plan["pool"]:
                kind = s["kind"]
                ready, kts = None, None
                if kind == "pu" and s["j"] == 0:
                    ready = {"sem": normed_ready, **{k: 8 + k + 1 for k in range(8)}}
                if kind == "mix" and s["j"] == 0:
                    pe.wait_ge(second_ready, 16)
                if kind == "out" and s["j"] == 0:
                    kts = [0, 2, 4, 6, 1, 3, 5, 7]
                    ready = {"sem": second_ready, **{c: 16 + n + 1 for n, c in enumerate(kts)}}
                for part in tile_parts(s, kts=kts, ready=ready):
                    part()
                for st in s["steps"]:
                    stat(st)

            def pair_slot(l, kind, j):
                return [s for s in plan["layer", l] if s["kind"] == kind and s["j"] == j][0]

            def qk_step(st, l):
                df = st["op"] == "df_qk"
                name = "df" if df else "sb"
                j, b = (st["h"], 64 * st["m"]) if df else (st["h"] // 2, 64 * (st["h"] % 2))
                pe.wait_ge(result_taken, pair_slot(l, name + "q", j)["r"] + 1)
                after_sb = not df and st["h"] > 0
                if not after_sb:
                    pe.wait_ge(z_free, st["z"])
                rows_ = slice(b, b + 64)
                for c, (_, _, blocks) in enumerate(CHUNKS):
                    if after_sb:
                        pe.wait_ge(sb_logs_ready, 3 * (8 * l + st["h"] - 1) + c + 1)
                    for n in blocks:
                        z0, w = ZOFF[n], P * (n + 1)
                        i = mm(Z[:, z0:z0 + w], qk[name + "q"][rows_, j, P * n:P * n + P], qk[name + "k"][rows_, j, 0:w],
                               start=True, stop=True)
                        if not df:
                            i = mm(Z[:, z0 + w - P:z0 + w], identb[:], mask_sb[:], start=False, stop=True, skip_group_check=True)
                    if not df:
                        i.then_inc(z_done, 1)
                if df:
                    i.then_inc(z_done, 1)

            def t_src(st):
                return cc[:] if st["df"] else ea[:, 1 + st["h"] % 2, :]

            def t1(st, l):
                w = t_src(st)
                done, n = (df_weights_ready, 3 * (4 * l + st["h"])) if st["df"] else (sb_weights_ready, 3 * (8 * l + st["h"]))
                pe.wait_ge(done, n + 1)
                pe.wait_ge(p0_free, st["p0"])
                for k in range(4):
                    i = nc.tensor.transpose(PP[:, 0, P * k:P * k + P], w[:, P * k:P * k + P], ident[:])
                i.then_inc(p0_done, 1)
                pe.wait_ge(done, n + 2)
                pe.wait_ge(p1_free, st["p1"])
                for k in range(4):
                    i = nc.tensor.transpose(PP[:, 1, P * k:P * k + P], w[:, 512 + P * k:640 + P * k], ident[:])
                i.then_inc(p1_done, 1)

            def t2(st, l):
                w = t_src(st)
                done, n = (df_weights_ready, 3 * (4 * l + st["h"])) if st["df"] else (sb_weights_ready, 3 * (8 * l + st["h"]))
                pe.wait_ge(done, n + 3)
                pe.wait_ge(p0_free, st["p0"] + 1)
                for k in range(2):
                    i = nc.tensor.transpose(PP[:, 0, P * k:P * k + P], w[:, 1024 + P * k:1152 + P * k], ident[:])
                i.then_inc(p0_done, 1)

            def pv(st, l):
                h = st["h"]
                pe.wait_ge(p0_free, st["p0"] + 2)
                pe.wait_ge(p1_free, st["p1"] + 1)
                last_v = pair_slot(l, "dfv" if st["df"] else "sbv", 1 + 2 * (h // (2 if st["df"] else 4)))
                pe.wait_ge(result_taken, last_v["r"] + 2)
                if st["df"] or h % 2 == 0:
                    pe.wait_ge(o_free, st["o"])
                if st["df"]:
                    for n in range(NB):
                        for k in range(n + 1):
                            i = mm(O[:, P * n:P * n + P], pt[:, k, P * n:P * n + P], qk["dfv"][:, k, P * h:P * h + P],
                                   start=k == 0, stop=k == n)
                    i.then_inc(o_done, 1)
                else:
                    b = 64 * (h % 2)
                    for k in range(NB):
                        i = mm(O[b:b + 64, P * k:S], qk["sbv"][:, k, 64 * h:64 * h + 64], pt[:, k, P * k:S],
                               start=k == 0, stop=k == NB - 1, skip_group_check=True)
                    if h % 2:
                        i.then_inc(o_done, 1)

            def df_f(st, l):
                pe.wait_ge(df_out_ready, 4 * l + st["h"] + 1)
                pe.wait_ge(p0_free, st["p0"])
                for n in range(NB):
                    i = nc.tensor.transpose(PP[:, 0, P * n:P * n + P], tb[:, 1, P * n:P * n + P], ident[:])
                i.then_inc(p0_done, 1)

            m_seen = 24
            for l in range(DEPTH):
                for s in plan["layer", l]:
                    ready = None
                    if s["kind"] == "dfk" and s["j"] == 0:
                        ready = {"sem": normed_ready, **{k: 16 + 16 * l + k + 1 for k in range(8)}}
                    if s["kind"] == "wo" and s["j"] == 0:
                        ready = {k: m_seen + [1, 2, 3, 4][k] for k in range(4)}
                    if s["kind"] == "wo" and s["j"] == 4:
                        ready = {k: m_seen + 4 + k + 1 for k in range(4)}
                    parts = tile_parts(s, ready=ready)
                    ts = [st for st in s["steps"] if st["op"] == "t"]
                    for st in s["steps"]:
                        if st["op"] in ("sb_qk", "df_qk"):
                            qk_step(st, l)
                    parts[0]()
                    parts[1]()
                    for st in ts:
                        t1(st, l)
                    parts[2]()
                    for st in s["steps"]:
                        if st["op"] == "df_f":
                            df_f(st, l)
                    for st in ts:
                        t2(st, l)
                    parts[3]()
                    for st in ts:
                        pv(st, l)
                    for st in s["steps"]:
                        if st["op"] == "stat":
                            stat(st)
                m_seen += 8
                t0, r0 = plan["ff", l]

                def ff_block(b, first=False):
                    for i in range(16):
                        t, r = t0 + i, r0 + i
                        pe.wait_ge(lo_done, b * 16 + (t + 1))
                        o = begin(r, b)
                        for k in range(KT):
                            if first and i == 0:
                                pe.wait_ge(normed_ready, 24 + 16 * l + k + 1)
                            if i == 8:
                                pe.wait_ge(second_ready, b * 8 + (m_seen + k + 1))
                            h_, l_ = (MH, ML) if i < 8 else (XH, XL)
                            c = slice(P * k, P * k + P)
                            last = three(o, WH[:, t % 4, c], WL[:, t % 4, c], h_[:, k, :], l_[:, k, :], k == 0, k == KT - 1)
                        last.then_inc(psum_done, 1)
                        if first and i == 0:
                            stat(plan["ff_stat", l])

                ff_block(0, first=True)
                with pe.Fori(1, BLOCKS) as b:
                    ff_block(b)
                m_seen += 8 * BLOCKS
            def y_turn(m):
                half, n = m // NB, m % NB
                for k in range(4):
                    pe.wait_ge(xt_ready, KT + 4 * half + k + 1)
                    i = nc.tensor.transpose(y_bank(m)[:, P * k:P * k + P], xf[:, 4 * half + k, P * n:P * n + P], ident[:])
                i.then_inc(y_done, 1)

            st = plan["last_stat"]
            pe.wait_ge(z_free, st["z"])
            pe.wait_ge(o_free, plan["o"])
            for m in range(NB):
                y_turn(m)
            pe.wait_ge(acc_done, sum(sums))
            pe.wait_ge(sq_ready, sum(squares))
            for n in range(NB):
                q = slice(P * n, P * n + P)
                mm(Z[:, 512 + n:513 + n], acc[:, q], mean_w[:, 0:1], start=True, stop=False)
                i = mm(Z[:, 512 + n:513 + n], sq[:, (KT - 1) % 2, q], mean_w[:, 0:1], start=False, stop=True)
            i.then_inc(z_done, 1)
            for m in range(NB, 2 * NB):
                if m > NB:
                    pe.wait_ge(result_taken, r0 + 16 * BLOCKS)
                if m == 2 * NB - 1:
                    pe.wait_ge(y_dve, 1)
                y_turn(m)


INPUTS = ["x", "norm_g", "attn_w_in", "attn_sinks", "attn_w_out", "pool_w_in", "pool_w_mix", "pool_scale",
          "pool_w_out", "final_g", "w_in_2", "w_o_2", "attn_norm_2", "subln_norm_2", "lam_q1_2", "lam_k1_2",
          "lam_q2_2", "lam_k2_2", "mlp_norm_2", "w_ff1_2", "w_ff2_2", "final_norm_2"]


def kernel(**inputs):
    import numpy as np
    import concourse.bacc as bacc
    from concourse.bass_utils import run_bass_kernel_spmd as run

    nc = bacc.Bacc("TRN2", target_bir_lowering=False, num_devices=1)
    arrays, args = {}, []
    for name in INPUTS:
        a = np.ascontiguousarray(inputs[name])
        arrays["in_" + name] = a
        args.append(nc.dram_tensor("in_" + name, a.shape, mybir.dt.from_np(a.dtype), kind="ExternalInput").ap())
    freq = (1.0 / (np.float32(10000.0) ** (np.arange(0, 64, 2, dtype=np.float32) / np.float32(64)))).astype(np.float32)
    angle = (freq[:, None] * np.arange(512, dtype=np.float32)[None, :]).astype(np.float32)
    cos, sin = np.cos(angle), np.sin(angle)
    table = np.stack([np.concatenate([cos] * 4), np.concatenate([-sin, sin] * 2)], axis=1).astype(np.float32)
    table = np.ascontiguousarray(table)
    arrays["in_rope_table"] = table
    args.append(nc.dram_tensor("in_rope_table", table.shape, mybir.dt.float32, kind="ExternalInput").ap())
    args.append(nc.dram_tensor("out_x", inputs["x"].shape, mybir.dt.float32, kind="ExternalOutput").ap())
    build(nc, *args)
    return run(nc, [arrays], core_ids=[0]).results[0]["out_x"]
```
